# Optimizing a Trainium2 kernel written in Bass

```python
import jax, jax.numpy as jnp
from jax import lax
import numpy as np

D_MODEL = 1024
BATCH = 1
SEQ = 256
DEPTH = 2

HEAD_DIM = 64
GROUP_HEADS = 4
GROUP_WIDTH = GROUP_HEADS * HEAD_DIM
N_GROUPS = 4
MIX_WIDTH = N_GROUPS * GROUP_WIDTH
ROPE_THETA = 10000.0
EPS = 1e-6
Q_BLOCK = 128
NEG = -1e30

MLA_Q_RANK = 192
MLA_KV_RANK = 128
MLA_NOPE = 64
MLA_ROPE = 32
MLA_V = 64
MLA_QK = MLA_NOPE + MLA_ROPE
SWA_KV_HEADS = 2
WINDOW = 128
MOBA_BLOCK = 256
MOBA_TOPK = 3
D_FF = 2816
CONV_WIDTH = 3
PLE_DIM = 256

SB_COLS = 3 * GROUP_WIDTH
MLA_COLS = MLA_Q_RANK + MLA_KV_RANK + MLA_ROPE
SWA_COLS = GROUP_WIDTH + 2 * SWA_KV_HEADS * HEAD_DIM
MOBA_COLS = 3 * GROUP_WIDTH
OFF_SB = 0
OFF_MLA = OFF_SB + SB_COLS
OFF_SWA = OFF_MLA + MLA_COLS
OFF_MOBA = OFF_SWA + SWA_COLS
N_IN = OFF_MOBA + MOBA_COLS

kernel_name = 'hybrid_parallel_head_groups_block'

def rms_norm(x, g):
    xf = x.astype(jnp.float32)
    y = xf * lax.rsqrt(jnp.mean(xf * xf, axis=-1, keepdims=True) + EPS)
    return (y * g.astype(jnp.float32)).astype(x.dtype)

def rope(x, pos):
    half = x.shape[-1] // 2
    inv = ROPE_THETA ** (-jnp.arange(half, dtype=jnp.float32) / half)
    ang = pos.astype(jnp.float32)[..., None] * inv
    cos = jnp.cos(ang)[:, :, None, :]
    sin = jnp.sin(ang)[:, :, None, :]
    xf = x.astype(jnp.float32)
    x1, x2 = xf[..., :half], xf[..., half:]
    return jnp.concatenate([x1 * cos - x2 * sin, x2 * cos + x1 * sin], axis=-1).astype(x.dtype)

def map_query_blocks(fn, q):
    B, S, H, d = q.shape
    nq = S // Q_BLOCK
    qb = q.reshape(B, nq, Q_BLOCK, H, d).transpose(1, 0, 2, 3, 4)
    out = lax.map(fn, (qb, jnp.arange(nq)))
    return out.transpose(1, 0, 2, 3, 4).reshape(B, S, H, out.shape[-1])

def stick_breaking_attn(q, k, v):
    S = q.shape[1]
    scale = q.shape[-1] ** -0.5
    kpos = jnp.arange(S)

    def block(args):
        qb, i = args
        qpos = i * Q_BLOCK + jnp.arange(Q_BLOCK)
        z = jnp.einsum('bqhd,bshd->bhqs', qb, k, preferred_element_type=jnp.float32) * scale
        mask = kpos[None, :] < qpos[:, None]
        log_beta = jax.nn.log_sigmoid(z)
        log_keep = jnp.where(mask, jax.nn.log_sigmoid(-z), 0.0)
        shifted = jnp.concatenate([log_keep[..., 1:], jnp.zeros_like(log_keep[..., :1])], axis=-1)
        tail = lax.cumsum(shifted, axis=3, reverse=True)
        w = jnp.where(mask, jnp.exp(log_beta + tail), 0.0).astype(v.dtype)
        return jnp.einsum('bhqs,bshd->bqhd', w, v)

    return map_query_blocks(block, q)

def causal_softmax_attn(q, k, v):
    S = q.shape[1]
    scale = q.shape[-1] ** -0.5
    kpos = jnp.arange(S)

    def block(args):
        qb, i = args
        qpos = i * Q_BLOCK + jnp.arange(Q_BLOCK)
        s = jnp.einsum('bqhd,bshd->bhqs', qb, k, preferred_element_type=jnp.float32) * scale
        s = jnp.where(kpos[None, :] <= qpos[:, None], s, NEG)
        pr = jax.nn.softmax(s, axis=-1).astype(v.dtype)
        return jnp.einsum('bhqs,bshd->bqhd', pr, v)

    return map_query_blocks(block, q)

def sliding_window_sink_attn(q, k, v, sinks):
    B, S, Hq, d = q.shape
    Hkv = k.shape[2]
    G = Hq // Hkv
    nb = S // WINDOW
    scale = d ** -0.5
    qb = q.reshape(B, nb, WINDOW, Hkv, G, d)
    kb = k.reshape(B, nb, WINDOW, Hkv, d)
    vb = v.reshape(B, nb, WINDOW, Hkv, d)
    pad = ((0, 0), (1, 0), (0, 0), (0, 0), (0, 0))
    kcat = jnp.concatenate([jnp.pad(kb, pad)[:, :-1], kb], axis=2)
    vcat = jnp.concatenate([jnp.pad(vb, pad)[:, :-1], vb], axis=2)
    s = jnp.einsum('bnqkgd,bnskd->bnkgqs', qb, kcat, preferred_element_type=jnp.float32) * scale
    qi = jnp.arange(WINDOW)[:, None] + WINDOW
    si = jnp.arange(2 * WINDOW)[None, :]
    band = (si <= qi) & (qi - si < WINDOW)
    has_prev = (jnp.arange(nb)[:, None, None] > 0) | (si[None] >= WINDOW)
    mask = band[None] & has_prev
    s = jnp.where(mask[None, :, None, None], s, NEG)
    sink = sinks.astype(jnp.float32).reshape(Hkv, G)[None, None, :, :, None, None]
    sink = jnp.broadcast_to(sink, s.shape[:-1] + (1,))
    pr = jax.nn.softmax(jnp.concatenate([s, sink], axis=-1), axis=-1)[..., :-1].astype(v.dtype)
    o = jnp.einsum('bnkgqs,bnskd->bnqkgd', pr, vcat)
    return o.reshape(B, S, Hq, d)

def moba_attn(q, k, v):
    B, S, H, d = q.shape
    nblk = -(-S // MOBA_BLOCK)
    s_pad = nblk * MOBA_BLOCK
    padw = ((0, 0), (0, s_pad - S), (0, 0), (0, 0))
    kblk = jnp.pad(k, padw).reshape(B, nblk, MOBA_BLOCK, H, d).transpose(0, 3, 1, 2, 4)
    vblk = jnp.pad(v, padw).reshape(B, nblk, MOBA_BLOCK, H, d).transpose(0, 3, 1, 2, 4)
    kmean = jnp.mean(kblk.astype(jnp.float32), axis=3)
    top = min(MOBA_TOPK, nblk)
    scale = d ** -0.5
    b_idx = jnp.arange(B)[:, None, None, None]
    h_idx = jnp.arange(H)[None, :, None, None]
    blk_ids = jnp.arange(nblk)

    def block(args):
        qb, i = args
        qh = qb.transpose(0, 2, 1, 3)
        own = (i * Q_BLOCK) // MOBA_BLOCK
        qpos = i * Q_BLOCK + jnp.arange(Q_BLOCK)
        gate = jnp.einsum('bhqd,bhnd->bhqn', qh.astype(jnp.float32), kmean)
        gate = jnp.where(blk_ids < own, gate, NEG)
        _, top_idx = lax.top_k(gate, top)
        valid = jnp.arange(top) < own
        ksel = kblk[b_idx, h_idx, top_idx]
        vsel = vblk[b_idx, h_idx, top_idx]
        s_sel = jnp.einsum('bhqd,bhqjsd->bhqjs', qh, ksel, preferred_element_type=jnp.float32) * scale
        s_sel = jnp.where(valid[:, None], s_sel, NEG)
        k_own = lax.dynamic_index_in_dim(kblk, own, axis=2, keepdims=False)
        v_own = lax.dynamic_index_in_dim(vblk, own, axis=2, keepdims=False)
        s_own = jnp.einsum('bhqd,bhsd->bhqs', qh, k_own, preferred_element_type=jnp.float32) * scale
        own_pos = own * MOBA_BLOCK + jnp.arange(MOBA_BLOCK)
        s_own = jnp.where(own_pos[None, :] <= qpos[:, None], s_own, NEG)
        n_sel = top * MOBA_BLOCK
        logits = jnp.concatenate([s_sel.reshape(B, H, Q_BLOCK, n_sel), s_own], axis=-1)
        pr = jax.nn.softmax(logits, axis=-1).astype(v.dtype)
        p_sel = pr[..., :n_sel].reshape(B, H, Q_BLOCK, top, MOBA_BLOCK)
        o = (jnp.einsum('bhqjs,bhqjsd->bhqd', p_sel, vsel)
             + jnp.einsum('bhqs,bhsd->bhqd', pr[..., n_sel:], v_own))
        return o.transpose(0, 2, 1, 3)

    return map_query_blocks(block, q)

def causal_depthwise_conv(u, w, b):
    C = u.shape[-1]
    y = lax.conv_general_dilated(u, w[:, None, :].astype(u.dtype), window_strides=(1,),
                                 padding=[(CONV_WIDTH - 1, 0)],
                                 dimension_numbers=('NWC', 'WIO', 'NWC'),
                                 feature_group_count=C)
    return y + b.astype(u.dtype)

def setup_inputs(seed: int = 0) -> dict:
    key = jax.random.key(seed)
    ks = jax.random.split(key, 32)
    f32 = jnp.float32

    def nrm(k, shape, fan_in):
        return jax.random.normal(k, shape, f32) * (fan_in ** -0.5)

    def gain(k, shape):
        return 1.0 + 0.05 * jax.random.normal(k, shape, f32)

    L = DEPTH
    return {
        'x': jax.random.normal(ks[0], (BATCH, SEQ, D_MODEL), f32),
        'p': jax.random.normal(ks[1], (DEPTH, BATCH, SEQ, PLE_DIM), f32),
        'positions': jnp.tile(jnp.arange(SEQ, dtype=jnp.int32)[None, :], (BATCH, 1)),
        'attn_norm': gain(ks[2], (L, D_MODEL)),
        'w_in': nrm(ks[3], (L, D_MODEL, N_IN), D_MODEL),
        'mla_q_norm': gain(ks[4], (L, MLA_Q_RANK)),
        'mla_w_uq': nrm(ks[5], (L, MLA_Q_RANK, GROUP_HEADS * MLA_QK), MLA_Q_RANK),
        'mla_kv_norm': gain(ks[6], (L, MLA_KV_RANK)),
        'mla_w_ukv': nrm(ks[7], (L, MLA_KV_RANK, GROUP_HEADS * (MLA_NOPE + MLA_V)), MLA_KV_RANK),
        'mla_q_gain': gain(ks[8], (L, MLA_QK)),
        'mla_k_gain': gain(ks[9], (L, MLA_QK)),
        'swa_q_gain': gain(ks[10], (L, HEAD_DIM)),
        'swa_k_gain': gain(ks[11], (L, HEAD_DIM)),
        'swa_sinks': 0.5 * jax.random.normal(ks[12], (L, GROUP_HEADS), f32),
        'moba_q_gain': gain(ks[13], (L, HEAD_DIM)),
        'moba_k_gain': gain(ks[14], (L, HEAD_DIM)),
        'group_norm': gain(ks[15], (L, MIX_WIDTH)),
        'w_o': nrm(ks[16], (L, MIX_WIDTH, D_MODEL), MIX_WIDTH * 2 * DEPTH),
        'ffn_norm': gain(ks[17], (L, D_MODEL)),
        'w_up': nrm(ks[18], (L, D_MODEL, 2 * D_FF), D_MODEL),
        'conv_w': nrm(ks[19], (L, CONV_WIDTH, 2 * D_FF), CONV_WIDTH),
        'conv_b': 0.01 * jax.random.normal(ks[20], (L, 2 * D_FF), f32),
        'w_down': nrm(ks[21], (L, D_FF, D_MODEL), D_FF * 2 * DEPTH),
        'ple_proj': nrm(ks[22], (L, PLE_DIM, D_MODEL), PLE_DIM * 2 * DEPTH),
        'ple_gate': nrm(ks[23], (L, D_MODEL, D_MODEL), D_MODEL),
    }

def reference(x, p, positions, attn_norm, w_in, mla_q_norm, mla_w_uq, mla_kv_norm, mla_w_ukv,
              mla_q_gain, mla_k_gain, swa_q_gain, swa_k_gain, swa_sinks, moba_q_gain, moba_k_gain,
              group_norm, w_o, ffn_norm, w_up, conv_w, conv_b, w_down, ple_proj, ple_gate):
    B, S, _ = x.shape
    H = GROUP_HEADS
    for i in range(DEPTH):
        h = rms_norm(x, attn_norm[i])
        proj = h @ w_in[i]

        sb = proj[..., OFF_SB:OFF_SB + SB_COLS].reshape(B, S, 3, H, HEAD_DIM)
        o_a = stick_breaking_attn(sb[:, :, 0], sb[:, :, 1], sb[:, :, 2])

        mla = proj[..., OFF_MLA:OFF_MLA + MLA_COLS]
        c_q = rms_norm(mla[..., :MLA_Q_RANK], mla_q_norm[i])
        c_kv = rms_norm(mla[..., MLA_Q_RANK:MLA_Q_RANK + MLA_KV_RANK], mla_kv_norm[i])
        k_pe = mla[..., MLA_Q_RANK + MLA_KV_RANK:]
        q_m = (c_q @ mla_w_uq[i]).reshape(B, S, H, MLA_QK)
        kv_m = (c_kv @ mla_w_ukv[i]).reshape(B, S, H, MLA_NOPE + MLA_V)
        k_m = jnp.concatenate([kv_m[..., :MLA_NOPE],
                               jnp.broadcast_to(k_pe[:, :, None, :], (B, S, H, MLA_ROPE))], axis=-1)
        v_m = kv_m[..., MLA_NOPE:]
        q_m = rms_norm(q_m, mla_q_gain[i])
        k_m = rms_norm(k_m, mla_k_gain[i])
        q_m = jnp.concatenate([q_m[..., :MLA_NOPE], rope(q_m[..., MLA_NOPE:], positions)], axis=-1)
        k_m = jnp.concatenate([k_m[..., :MLA_NOPE], rope(k_m[..., MLA_NOPE:], positions)], axis=-1)
        o_b = causal_softmax_attn(q_m, k_m, v_m)

        swa = proj[..., OFF_SWA:OFF_SWA + SWA_COLS]
        kvw = SWA_KV_HEADS * HEAD_DIM
        q_c = swa[..., :GROUP_WIDTH].reshape(B, S, H, HEAD_DIM)
        k_c = swa[..., GROUP_WIDTH:GROUP_WIDTH + kvw].reshape(B, S, SWA_KV_HEADS, HEAD_DIM)
        v_c = swa[..., GROUP_WIDTH + kvw:].reshape(B, S, SWA_KV_HEADS, HEAD_DIM)
        q_c = rope(rms_norm(q_c, swa_q_gain[i]), positions)
        k_c = rope(rms_norm(k_c, swa_k_gain[i]), positions)
        o_c = sliding_window_sink_attn(q_c, k_c, v_c, swa_sinks[i])

        mb = proj[..., OFF_MOBA:OFF_MOBA + MOBA_COLS].reshape(B, S, 3, H, HEAD_DIM)
        q_d = rope(rms_norm(mb[:, :, 0], moba_q_gain[i]), positions)
        k_d = rope(rms_norm(mb[:, :, 1], moba_k_gain[i]), positions)
        o_d = moba_attn(q_d, k_d, mb[:, :, 2])

        groups = jnp.stack([o_a.reshape(B, S, GROUP_WIDTH), o_b.reshape(B, S, GROUP_WIDTH),
                            o_c.reshape(B, S, GROUP_WIDTH), o_d.reshape(B, S, GROUP_WIDTH)], axis=2)
        groups = rms_norm(groups, group_norm[i].reshape(N_GROUPS, GROUP_WIDTH))
        x = x + groups.reshape(B, S, MIX_WIDTH) @ w_o[i]

        h = rms_norm(x, ffn_norm[i])
        u = causal_depthwise_conv(h @ w_up[i], conv_w[i], conv_b[i])
        x = x + (jax.nn.silu(u[..., :D_FF]) * u[..., D_FF:]) @ w_down[i]

        x = x + (p[i] @ ple_proj[i]) * jax.nn.sigmoid(x @ ple_gate[i])
    return x


_drawn_inputs = setup_inputs


def setup_inputs(seed=0):
    import zlib

    import numpy as np

    out = dict(_drawn_inputs(seed))
    spreads = {}
    factors = {'mla_q_norm': 4.667,
     'mla_q_gain': 4.278,
     'mla_k_gain': 4.526,
     'swa_q_gain': 4.066,
     'swa_k_gain': 4.485,
     'swa_sinks': 64.0,
     'moba_q_gain': 4.8,
     'moba_k_gain': 4.567,
     'conv_b': 8.0}
    for name, (base, spread) in spreads.items():
        noise = np.random.default_rng([zlib.crc32(name.encode()), seed]).standard_normal(out[name].shape)
        drawn = base * np.exp(spread * noise) if base else spread * noise
        out[name] = __import__('jax').numpy.asarray(drawn.astype(out[name].dtype))
    for name, factor in factors.items():
        out[name] = (out[name] * factor).astype(out[name].dtype)
    return out
```

```python
from contextlib import ExitStack

import numpy as np

import concourse.bass as bass
from concourse import mybir

F32 = mybir.dt.float32
F32R = mybir.dt.float32r
BF16 = mybir.dt.bfloat16
I32 = mybir.dt.int32
ALU = mybir.AluOpType
ACT = mybir.ActivationFunctionType
AX = mybir.AxisListType

P = 128
D = 1024
SEQ = 256
DEPTH = 2
TT = SEQ // P
KT = D // P
H = 4
HD = 64
GW = H * HD
ROPE_THETA = 10000.0
EPS = 1e-6
NEG = -1e30
QR, KVR = 192, 128
NOPE, PE_DIM = 64, 32
QK = NOPE + PE_DIM
DFF = 2816
FT = DFF // P
PLE = 256

OFF_SB, OFF_MLA = 0, 3 * GW
OFF_SWA = OFF_MLA + QR + KVR + PE_DIM
OFF_MOBA = OFF_SWA + GW + 2 * 2 * HD
MLA_COLS = QR + KVR + PE_DIM

SB, MLA, SWA, MOBA = range(4)

G_ATTN, G_FFN, G_GROUP = 0, D, 2 * D
S_SWAQ, S_SWAK, S_MOBAQ, S_MOBAK = 0, 64, 128, 192
S_MLAQ, S_MLAK = 256, 256 + QK
S_QN = S_MLAK + QK
S_KVN = S_QN + QR
S_SINK = S_KVN + KVR
S_ALL = S_SINK + H

RING = 3
(M_MLA_A, M_MLA_B, M_MOBA_Q, M_MOBA_K, M_MOBA_V, M_SWA_Q, M_SWA_KV, M_SB_V, M_SB_Q, M_SB_K
 ) = range(10)
WIN_COLS = [(OFF_MLA, MLA_COLS // 2), (OFF_MLA + MLA_COLS // 2, MLA_COLS // 2),
            (OFF_MOBA, 256), (OFF_MOBA + 256, 256), (OFF_MOBA + 512, 256),
            (OFF_SWA, 256), (OFF_SWA + 256, 256),
            (OFF_SB + 512, 256), (OFF_SB, 256), (OFF_SB + 256, 256)]
WO_ROWS = [(0, 2), (2, 2), (4, 2), (6, 1), (7, 1)]
GATE_ROWS = [(0, 2), (2, 2), (4, 2), (6, 1), (7, 1)]
U_WO = len(WIN_COLS)
U_FFN = U_WO + len(WO_ROWS)
STEPS = FT // 2
LOOP_FROM = 3
LOOPS = (STEPS - LOOP_FROM) // 2
U_LOOP = U_FFN + 2 + 3 * (LOOP_FROM - 1)
U_AFTER = U_LOOP + 6 * LOOPS
U_PROJ = U_AFTER + 1
U_GATE = U_PROJ + 1
UNITS = U_GATE + len(GATE_ROWS)
assert UNITS % RING == 0 and LOOPS * 2 + LOOP_FROM == STEPS
MAGIC = 1.5 * 2.0 ** 23
TWO_PI = [6.28125, 0.0019353071693331003, 1.0253691153482577e-11]


SLOT = 2048
COLS = ([KT * w for _, w in WIN_COLS] + [n * D for _, n in WO_ROWS]
        + [SLOT] * (U_GATE - U_FFN) + [n * D for _, n in GATE_ROWS])
assert len(COLS) == UNITS and max(COLS) == SLOT


def unit_gate(s):
    return U_FFN + 3 * s - (1 if s else 0)


_at = [0]


def _cols(n):
    _at[0] += n
    return _at[0] - n


ST_X = _cols(6)
ST_L = _cols(12)
ST_PE = _cols(2)
ST_M = _cols(48)
ST_B = _cols(48)
ST_S = _cols(36)
RS_MLA, RS_MOBA, RS_SWA = _cols(8), _cols(8), _cols(8)
MX = _cols(8)
NB = _cols(8)
SNK = _cols(8)
DENS = [_cols(8) for _ in range(3)]
RDEN = _cols(8)
ST_G = _cols(24)
ST_ALL = _at[0]

GROUP_ORDER = [MLA, MOBA, SB, SWA]

FLOW = """x_squared stat_in stat_root hn_ready xT_ready xT_high xT_low
pr_ready squared lat_stat lat_root lat_done lat_T cT_ready mla_up mla_up_ready
v_ready mla_stat mla_root mla_qk mla_T mT_ready conv_T conv_ready
moba_stat moba_root moba_qk moba_T mobaT_ready swa_stat swa_root swa_qk swa_T swaT_ready
sbT_ready scores_ready half_scores half_z softmax_bias sink_arg sink_exp probs_ready probs_T pt_ready
pv_ready group_out group_sq group_stat group_root group_done
sb_z sb_abs sb_exp sb_log sb_soft sb_minus sb_probs groups_T mT_high mT_low
wo_done x_mid tap2 tap1 conv_done silu prod g_high g_low
p_T pT_high pT_low down_done x_low gate_ready sigmoid ple_term
act_step dve_step arrived""".split()


PAIRED = (0, 2, 1, 3)
GROUPED = (0, 1, 2, 3)


def build(nc, x_in, p_in, positions, w_in, w_uq, w_ukv, norm_gains, small_gains, w_o, w_up,
          conv_rows, w_down, ple_proj, ple_gate, out):
    with ExitStack() as ctx:
        def sb(name, shape, dt=F32):
            return ctx.enter_context(nc.sbuf_tensor(name, shape, dt))

        def sem(name):
            return ctx.enter_context(nc.semaphore(name))

        raw = sb("raw", [P, RING, SLOT])
        wh = sb("wh", [P, RING, SLOT], F32R)
        wl = sb("wl", [P, RING, SLOT], F32R)
        x = sb("x", [P, TT, D])
        hn = sb("hn", [P, TT, D])
        hT_h = sb("hT_h", [P, KT, SEQ], F32R)
        hT_l = sb("hT_l", [P, KT, SEQ], F32R)
        gT_h = sb("gT_h", [P, 2, 2, SEQ], F32R)
        gT_l = sb("gT_l", [P, 2, 2, SEQ], F32R)
        ng = sb("ng", [P, 3 * D])
        sg = sb("sg", [P, S_ALL])
        uq = sb("uq", [P, 2, H * QK])
        ukv = sb("ukv", [P, H * 2 * HD])
        p_sb = sb("p_sb", [P, TT, PLE])
        conv = sb("conv", [P, 4, 2 * FT])
        ident = sb("ident", [P, P])
        ident_b = sb("ident_b", [P, P], BF16)
        causal = sb("causal", [P, P], BF16)
        above = sb("above", [P, P], BF16)
        neg_tri = sb("neg_tri", [P, P])
        neg_ones = sb("neg_ones", [P, P])
        inv_freq = sb("inv_freq", [P, HD // 2])
        pos_i = sb("pos_i", [P, TT], I32)
        pos_f = sb("pos_f", [P, TT])
        rope_c = sb("rope_c", [P, TT, HD])
        rope_s = sb("rope_s", [P, TT, HD])
        rope_c32 = sb("rope_c32", [P, TT, PE_DIM])
        rope_s32 = sb("rope_s32", [P, TT, PE_DIM])
        gc = sb("gc", [P, 4, TT, HD])
        gs = sb("gs", [P, 4, TT, HD])
        pr = sb("pr", [P, 2, TT, 512])
        rot = sb("rot", [P, TT, 512])
        lat = sb("lat", [P, 1536])
        mk = sb("mk", [P, TT, H, QK])
        kpe = sb("kpe", [P, TT, PE_DIM])
        tmp = sb("tmp", [P, 1024])
        mT = sb("mT", [P, 2, H, SEQ])
        qkT_moba = sb("qkT_moba", [P, 4, SEQ])
        qkT_swa = sb("qkT_swa", [P, 3, SEQ])
        qkT_sb = sb("qkT_sb", [P, 4, SEQ])
        v_moba = sb("v_moba", [P, TT, GW])
        v_swa = sb("v_swa", [P, TT, 2 * HD])
        v_sb = sb("v_sb", [P, TT, GW])
        pb = sb("pb", [P, 1536])
        pt = sb("pt", [P, 1536])
        st = sb("st", [P, ST_ALL])

        ps = ctx.enter_context(nc.psum_tensor("ps", [P, 8, 512], F32))

        mq = lat[:, 0:768].rearrange("p (t h n) -> p t h n", t=TT, h=H)
        cT = lat[:, 768:1536].rearrange("p (k n) -> p k n", k=3)
        mkv = pr[:, 0].rearrange("p t (h n) -> p t h n", h=H)
        sb_e = mT[:].rearrange("p a h n -> p (a h n)")[:, 0:1536]
        sb_sp = lat
        cv = [pb[:, 0:1024].rearrange("p (a n) -> p a n", a=4),
              pt[:, 0:1024].rearrange("p (a n) -> p a n", a=4)]
        conv_raw = tmp[0:2 * FT, 0:512].rearrange("p (a n) -> p a n", a=4)
        pT_h, pT_l = gT_h[:, 1], gT_l[:, 1]

        raw_landed = [sem(f"raw_landed{n}") for n in range(RING)]
        h_made = sem("h_made")
        l_made = sem("l_made")
        w_used = sem("w_used")
        x_landed, pos_landed = sem("x_landed"), sem("pos_landed")
        ng_landed, sg_landed = sem("ng_landed"), sem("sg_landed")
        uq_landed, uq2_landed, ukv_landed = sem("uq_landed"), sem("uq2_landed"), sem("ukv_landed")
        p_landed, conv_landed = sem("p_landed"), sem("conv_landed")
        out_landed = sem("out_landed")
        column_0 = sem("column_0")
        consts_made = sem("consts_made")
        rope_step, rope_arg, rope_sin = sem("rope_step"), sem("rope_arg"), sem("rope_sin")
        released = sem("released")

        F = {name: sem(name) for name in FLOW}
        first = F[FLOW[0]].num
        assert [F[n].num for n in FLOW] == list(range(first, first + len(FLOW)))
        flow_range = range(first, first + len(FLOW))

        block = ctx.enter_context(nc.Block())

        def ge(eng, name, value):
            if not (isinstance(value, int) and value <= 0):
                eng.wait_ge(F[name], value)

        def stat(a, n=1):
            return st[:, a:a + n]

        def per_head(ap, width):
            return ap.unsqueeze(2).broadcast_to([P, ap.shape[1], width])

        def unit_done(eng, layer, u, turn=0):
            eng.wait_ge(w_used, layer * UNITS + turn * 6 + (u + 1 + RING))

        @block.sync
        def _(sp):
            for t in range(TT):
                sp.dma_start(x[:, t, :], x_in[0, t * P:(t + 1) * P, :]).then_inc(x_landed, 16)
            with sp.Fori(0, DEPTH) as layer:
                def load(src, u, turn=0):
                    slot, k = u % RING, src.shape[1]
                    sp.wait_ge(l_made, layer * UNITS + turn * 6 + (u + 1))
                    if u == M_SB_Q:
                        sp.sem_inc(column_0, 1)
                    sp.dma_start(raw[:, slot, 0:COLS[u]].rearrange("p (k n) -> p k n", k=k),
                                 src).then_inc(raw_landed[slot], 16)

                def rows(w, k, n):
                    return w[layer][k * P:(k + n) * P, :].rearrange("(k p) n -> p k n", p=P)

                def load_up(s, half, u, turn=0):
                    w = w_up[layer].rearrange("(k p) n -> p k n", p=P)
                    load(w[:, :, bass.ds(s * 256 + half * DFF, 256)], u, turn)

                def load_down(s, u, turn=0):
                    load(w_down[layer][bass.ds(s * 256, 256), :].rearrange(
                        "(k p) n -> p k n", p=P), u, turn)

                for u, (c, w) in enumerate(WIN_COLS):
                    load(w_in[layer].rearrange("(k p) n -> p k n", p=P)[:, :, c:c + w], u)
                for n, (k, m) in enumerate(WO_ROWS):
                    load(rows(w_o, k, m), U_WO + n)
                for s in range(LOOP_FROM):
                    for half in range(2):
                        load_up(s, half, unit_gate(s) + half)
                    if s:
                        load_down(s - 1, unit_gate(s) + 2)
                with sp.Fori(0, LOOPS) as turn:
                    for j in range(2):
                        u = unit_gate(LOOP_FROM + j)
                        for half in range(2):
                            load_up(turn * 2 + (LOOP_FROM + j), half, u + half, turn)
                        load_down(turn * 2 + (LOOP_FROM + j - 1), u + 2, turn)
                load_down(STEPS - 1, U_AFTER)
                load(rows(ple_proj, 0, 2), U_PROJ)
                for n, (k, m) in enumerate(GATE_ROWS):
                    load(rows(ple_gate, k, m), U_GATE + n)
            sp.wait_ge(released, DEPTH + 1)
            for t in range(TT):
                sp.dma_start(out[0, t * P:(t + 1) * P, :], x[:, t, :]).then_inc(out_landed, 16)
            sp.wait_ge(out_landed, 16 * TT)

        @block.gpsimd
        def _(pool):
            pool.sem_inc(l_made, RING)
            for t, v in ((ident, 0.0), (causal, 0.0), (above, 0.0), (neg_tri, -1.0),
                         (neg_ones, -1.0)):
                pool.memset(t[:], v).then_inc(consts_made, 1)
            for j in range(HD // 2):
                last = pool.memset(inv_freq[:, j:j + 1], float(np.float32(ROPE_THETA ** (-2.0 * j / HD))))
            last.then_inc(consts_made, 1)
            pool.wait_ge(consts_made, 6)
            for t, op, fill, sign in ((ident, ALU.not_equal, 1.0, 1), (causal, ALU.is_ge, NEG, 1),
                                      (above, ALU.is_gt, NEG, -1), (neg_tri, ALU.is_ge, 0.0, 1)):
                pool.affine_select(out=t[:], in_=t[:], compare_op=op, fill=fill, base=0,
                                   pattern=[[-sign, P]], channel_multiplier=sign
                                   ).then_inc(consts_made, 1)
            pool.wait_ge(consts_made, 7)
            pool.tensor_copy(ident_b[:], ident[:]).then_inc(consts_made, 1)
            with pool.Fori(0, DEPTH) as layer:
                def low(u, turn=0):
                    slot, n = u % RING, COLS[u]
                    pool.wait_ge(h_made, layer * UNITS + turn * 6 + (u + 1 + RING))
                    pool.wait_ge(w_used, layer * UNITS + turn * 6 + (u + 1))
                    pool.tensor_tensor(wl[:, slot, 0:n], raw[:, slot, 0:n],
                                       wh[:, slot, 0:n].bitcast(F32), ALU.subtract
                                       ).then_inc(l_made, 1)

                for u in range(U_LOOP):
                    low(u)
                with pool.Fori(0, LOOPS) as turn:
                    for u in range(U_LOOP, U_LOOP + 6):
                        low(u, turn)
                for u in range(U_AFTER, UNITS):
                    low(u)

        @block.scalar
        def _(act):
            act.sem_inc(h_made, RING)
            act.sem_inc(released, 1)
            act.dma_start(pos_i[:], positions.rearrange("a (t p) -> p (a t)", p=P),
                          allow_slow_non_contiguous=True).then_inc(pos_landed, 16)
            act.wait_ge(rope_arg, 1)
            for table, a in ((rope_s[:, :, 32:64], 0), (rope_c[:, :, 0:32], 64)):
                act.activation(table, tmp[:, a:a + 64].rearrange("p (t n) -> p t n", t=TT),
                               ACT.Sin).then_inc(rope_sin, 1)

            with act.Fori(0, DEPTH) as layer:
                steps = [0]

                def chained(ins):
                    steps[0] += 1
                    ins.then_inc(F["act_step"], 1)
                    act.wait_ge(F["act_step"], steps[0])

                def high(u, turn=0):
                    slot, n = u % RING, COLS[u]
                    act.wait_ge(raw_landed[slot],
                                (layer * (UNITS // RING) + turn * (6 // RING) + (u // RING + 1)) * 16)
                    act.wait_ge(w_used, layer * UNITS + turn * 6 + (u + 1))
                    act.activation(wh[:, slot, 0:n], raw[:, slot, 0:n], ACT.Copy
                                   ).then_inc(h_made, 1)

                def x_squares():
                    for t in range(TT):
                        act.activation(hn[:, t, :], x[:, t, :], ACT.Square,
                                       accum_out=stat(ST_X + t)).then_inc(F["x_squared"], 1)

                def root(a, n, ready, k, done):
                    act.wait_ge(F[ready], k)
                    chained(act.activation(stat(a + n, n), stat(a, n), ACT.Ln))
                    act.activation(stat(a + n, n), stat(a + n, n), ACT.Exp, scale=-0.5
                                   ).then_inc(F[done], 1)

                def x_high(n, bank):
                    for k in range(4):
                        t, half = divmod(k, 2)
                        act.wait_ge(F["xT_ready"], n + k + 1)
                        act.activation(hT_h[:, 4 * half:4 * half + 4, t * P:(t + 1) * P],
                                       ps[:, bank + k, :].rearrange("p (k n) -> p k n", k=4),
                                       ACT.Copy).then_inc(F["xT_high"], 1)

                def copied(dst, src, ready, n, done, **kw):
                    if ready == "unit":
                        unit_done(act, layer, n)
                    else:
                        act.wait_ge(F[ready], n)
                    act.activation(dst, src, ACT.Copy, **kw).then_inc(F[done], 1)

                def exps(g, rs, den, order=PAIRED):
                    act.wait_ge(F["softmax_bias"], g + 1)
                    ge(act, "probs_T", 3 * g)
                    for h in range(H):
                        act.activation(pb[:, h * P:(h + 1) * P], ps[:, 4, h * P:(h + 1) * P],
                                       ACT.Exp, bias=stat(NB + h), scale=stat(rs + h),
                                       accum_out=stat(den + h)).then_inc(F["probs_ready"], 1)
                    for i, h in enumerate(order):
                        act.activation(pb[:, 512 + i * 256:768 + i * 256],
                                       ps[:, 5 + i // 2, (i % 2) * 256:(i % 2) * 256 + 256],
                                       ACT.Exp, bias=stat(NB + H + h), scale=stat(rs + H + h),
                                       accum_out=stat(den + H + h)).then_inc(F["probs_ready"], 1)

                def group_squares(n):
                    c = GROUP_ORDER[n] * GW
                    act.wait_ge(F["group_out"], n + 1)
                    for t in range(TT):
                        act.activation(junk(t), hn[:, t, c:c + GW], ACT.Square,
                                       accum_out=stat(ST_G + 6 * n + t)
                                       ).then_inc(F["group_sq"], 1)

                def group_root(n):
                    root(ST_G + 6 * n, 2, "group_stat", n + 1, "group_root")

                def junk(t):
                    return qkT_moba[:, 2 * t, :]

                act.dma_start(ng[:], norm_gains[layer].partition_broadcast(P)
                              ).then_inc(ng_landed, 16)
                act.wait_ge(x_landed, 16 * TT)
                x_squares()
                act.dma_start(sg[:], small_gains[layer].partition_broadcast(P)
                              ).then_inc(sg_landed, 16)
                root(ST_X, 2, "stat_in", 1, "stat_root")
                high(0)
                act.dma_start(uq[:, 0, :], w_uq[layer][0:P, :]).then_inc(uq_landed, 16)
                act.dma_start(uq[0:QR - P, 1, :], w_uq[layer][P:QR, :]).then_inc(uq2_landed, 16)
                act.dma_start(ukv[:], w_ukv[layer]).then_inc(ukv_landed, 16)
                act.wait_ge(rope_sin, 2)
                act.dma_start(conv_raw, conv_rows[layer]).then_inc(conv_landed, 16)
                act.dma_start(p_sb[:], p_in[layer, 0].rearrange("(t p) n -> p t n", p=P)
                              ).then_inc(p_landed, 16)
                x_high(0, 4)
                high(1)
                high(2)

                for t in range(TT):
                    copied(pr[:, 0, t, 0:MLA_COLS], ps[:, t, 0:MLA_COLS], "unit", M_MLA_B,
                           "pr_ready")
                for t in range(TT):
                    act.wait_ge(F["pr_ready"], t + 1)
                    act.activation(rot[:, t, 0:MLA_COLS], pr[:, 0, t, 0:MLA_COLS], ACT.Square
                                   ).then_inc(F["squared"], 1)
                high(3)
                root(ST_L, 4, "lat_stat", 1, "lat_root")
                high(4)
                high(5)
                for t in range(TT):
                    copied(cT[:, :, t * P:(t + 1) * P],
                           ps[:, 4 + t, 0:384].rearrange("p (k n) -> p k n", k=3),
                           "lat_T", 1 + t, "cT_ready")
                for t in range(TT):
                    copied(pr[:, 1, t, :], ps[:, 2 + t, :], "unit", M_MOBA_K, "pr_ready")
                high(6)
                for t in range(TT):
                    copied(mq[:, t].rearrange("p h n -> p (h n)"), ps[:, 4 + 2 * t, 0:H * QK],
                           "mla_up", 1 + t, "mla_up_ready")
                    copied(pr[:, 0, t, :], ps[:, 5 + 2 * t, :], "lat_T", 2, "mla_up_ready")
                act.wait_ge(F["mla_up_ready"], 4)
                act.wait_ge(F["lat_stat"], 1)
                act.activation(rot[:, :, 0:H * QK], mq.rearrange("p t h n -> p t (h n)"),
                               ACT.Square).then_inc(F["squared"], 1)
                act.wait_ge(F["conv_T"], 1)
                act.wait_ge(F["lat_done"], 2)
                for t in range(TT):
                    act.activation(
                        tmp[:, t * 256:(t + 1) * 256].rearrange("p (h n) -> p h n", h=H),
                        mkv[:, t, :, 0:NOPE], ACT.Square).then_inc(F["squared"], 1)
                for t in range(TT):
                    copied(v_moba[:, t, :], ps[:, t, 0:256], "unit", M_MOBA_V, "v_ready")
                high(7)
                root(ST_M, 16, "mla_stat", 1, "mla_root")
                act.wait_ge(F["pr_ready"], 4)
                act.activation(rot[:], pr[:, 1], ACT.Square).then_inc(F["squared"], 1)
                high(8)
                for t in range(TT):
                    for a in range(2):
                        copied(mT[0:QK, a, :, t * P:(t + 1) * P],
                               ps[0:QK, 4 + 2 * t + a, :].rearrange("p (k n) -> p k n", k=H),
                               "mla_T", 1 + t, "mT_ready")
                root(ST_B, 16, "moba_stat", 1, "moba_root")
                high(9)
                act.wait_ge(F["moba_qk"], 1)
                for t in range(TT):
                    copied(pr[:, 1, t, 0:384], ps[:, 2 + t, 0:384], "unit", M_SWA_KV,
                           "pr_ready")
                    act.activation(v_swa[:, t, :], ps[:, 2 + t, 384:512], ACT.Copy
                                   ).then_inc(F["v_ready"], 1)
                exps(0, RS_MLA, DENS[0])
                for t in range(TT):
                    copied(qkT_moba[:, :, t * P:(t + 1) * P],
                           ps[:, t, :].rearrange("p (k n) -> p k n", k=4),
                           "moba_T", 1 + t, "mobaT_ready")
                act.wait_ge(F["pr_ready"], 6)
                act.activation(rot[:, :, 0:384], pr[:, 1, :, 0:384], ACT.Square
                               ).then_inc(F["squared"], 1)
                high(10)
                for t in range(TT):
                    copied(v_sb[:, t, :], ps[:, 2 + t, 0:256], "unit", M_SB_V, "v_ready")
                root(ST_S, 12, "swa_stat", 1, "swa_root")
                high(11)
                copied(qkT_sb[:, 0:2, :], ps[:, 0, :].rearrange("p (k n) -> p k n", k=2),
                       "unit", M_SB_Q, "sbT_ready", scale=HD ** -0.5)
                exps(1, RS_MOBA, DENS[1])
                for t in range(TT):
                    copied(qkT_swa[:, :, t * P:(t + 1) * P],
                           ps[:, 2 + t, 0:384].rearrange("p (k n) -> p k n", k=3),
                           "swa_T", 1 + t, "swaT_ready")
                copied(qkT_sb[:, 2:4, :], ps[:, 1, :].rearrange("p (k n) -> p k n", k=2),
                       "unit", M_SB_K, "sbT_ready")
                act.wait_ge(F["scores_ready"], 2)
                group_squares(0)
                high(12)
                group_root(0)
                for b in range(3):
                    c = slice(b * 512, (b + 1) * 512)
                    act.wait_ge(F["sb_z"], b + 1)
                    act.activation(sb_e[:, c], ps[:, b, :], ACT.Abs).then_inc(F["sb_abs"], 1)
                for b in range(3):
                    c = slice(b * 512, (b + 1) * 512)
                    act.wait_ge(F["sb_abs"], b + 1)
                    act.activation(sb_e[:, c], sb_e[:, c], ACT.Exp, scale=-1.0
                                   ).then_inc(F["sb_exp"], 1)
                for b in range(3):
                    c = slice(b * 512, (b + 1) * 512)
                    act.wait_ge(F["sb_exp"], b + 1)
                    act.activation(sb_e[:, c], sb_e[:, c], ACT.Ln, bias=1.0
                                   ).then_inc(F["sb_log"], 1)
                act.wait_ge(F["sink_arg"], 1)
                act.activation(stat(SNK, 8), stat(SNK, 8), ACT.Exp).then_inc(F["sink_exp"], 1)
                exps(2, RS_SWA, DENS[2], GROUPED)
                for b in range(3):
                    c = slice(b * 512, (b + 1) * 512)
                    act.wait_ge(F["sb_minus"], b + 1)
                    act.activation(sb_e[:, c], ps[:, b, :], ACT.Exp).then_inc(F["sb_probs"], 1)
                group_squares(1)
                group_root(1)
                for n in (2, 3):
                    group_squares(n)
                    group_root(n)
                for n, g in enumerate(GROUP_ORDER):
                    copied(hT_h[:, 2 * g:2 * g + 2, :],
                           ps[:, 4 + n, :].rearrange("p (k n) -> p k n", k=2),
                           "groups_T", n + 1, "mT_high")
                high(13)
                high(14)
                high(15)

                act.wait_ge(F["x_mid"], TT)
                act.wait_ge(F["groups_T"], 4)
                x_squares()
                root(ST_X, 2, "stat_in", 2, "stat_root")
                high(16)
                x_high(4, 4)

                def mlp(s, par, this, u, turn=0):
                    bank = 4 + 2 * par
                    high(u, turn)
                    high(u + 1, turn)
                    ge(act, "g_low", s - 1)
                    for half in range(2):
                        unit_done(act, layer, this + half, turn)
                        for j in range(2):
                            f = bass.ds(s * 2 + (half * FT + j), 1)
                            act.activation(cv[par][:, 2 * half + j, :],
                                           ps[:, bank + half, j * 256:(j + 1) * 256],
                                           ACT.Identity, bias=conv[:, 3, f],
                                           scale=conv[:, 2, f]).then_inc(F["tap2"], 1)
                    act.wait_ge(F["conv_done"], s * 4 + 2)
                    act.activation(cv[par][:, 0:2, :], cv[par][:, 0:2, :], ACT.Silu
                                   ).then_inc(F["silu"], 1)
                    act.wait_ge(F["prod"], s + 1)
                    if not (isinstance(s, int) and s < 2):
                        unit_done(act, layer, this - 1, turn)
                    act.activation(gT_h[:, par], cv[par][:, 0:2, :], ACT.Copy
                                   ).then_inc(F["g_high"], 1)
                    high(u + 2, turn)

                act.wait_ge(F["conv_ready"], 1)
                for s in range(LOOP_FROM):
                    mlp(s, s % 2, unit_gate(s), unit_gate(s + 1))
                with act.Fori(0, LOOPS) as turn:
                    for j in range(2):
                        s = LOOP_FROM + j
                        mlp(turn * 2 + s, s % 2, unit_gate(s), unit_gate(s + 1), turn)

                act.wait_ge(F["p_T"], 1)
                unit_done(act, layer, U_AFTER - 1)
                act.activation(pT_h, ps[:, 6, :].rearrange("p (k n) -> p k n", k=2), ACT.Copy
                               ).then_inc(F["pT_high"], 1)
                high(U_GATE + 1)
                x_high(8, 0)
                for n in range(2, len(GATE_ROWS)):
                    high(U_GATE + n)
                for b in range(4):
                    t, half = divmod(b, 2)
                    if b < 3:
                        act.wait_ge(F["gate_ready"], b + 1)
                    else:
                        unit_done(act, layer, UNITS - 1)
                    act.activation(hn[:, t, half * 512:(half + 1) * 512], ps[:, b, :],
                                   ACT.Sigmoid).then_inc(F["sigmoid"], 1)
                act.drain()
                act.wait_ge(F["arrived"], 2)
                act.sem_clear(flow_range)
                act.sem_inc(released, 1)

        @block.tensor
        def _(pe):
            pe.sem_inc(w_used, RING)
            pe.wait_ge(consts_made, 11)
            with pe.Fori(0, DEPTH) as layer:
                def unit(u, turn=0):
                    pe.wait_ge(l_made, layer * UNITS + turn * 6 + (u + 1 + RING))
                    return u % RING

                def split_product(dst, a_h, a_l, b_h, b_l, start, stop, last=False):
                    pe.matmul(dst, a_h, b_h, start=start, stop=False, skip_group_check=True)
                    pe.matmul(dst, a_h, b_l, start=False, stop=False, skip_group_check=True)
                    return pe.matmul(dst, a_l, b_h, start=False, stop=stop,
                                     skip_group_check=True)

                def project(u, banks, col):
                    slot, w = unit(u), WIN_COLS[u][1]
                    for t in range(TT):
                        tok = slice(t * P, (t + 1) * P)
                        for k in range(KT):
                            c = slice(k * w, (k + 1) * w)
                            mm = split_product(ps[:, banks[t], col:col + w],
                                               hT_h[:, k, tok], hT_l[:, k, tok],
                                               wh[:, slot, c], wl[:, slot, c],
                                               k == 0, k == KT - 1)
                    mm.then_inc(w_used, 1)

                def project_T(u, bank):
                    slot = unit(u)
                    for j in range(2):
                        for k in range(KT):
                            c = slice(k * 256 + j * P, k * 256 + (j + 1) * P)
                            mm = split_product(ps[:, bank, j * 256:(j + 1) * 256],
                                               wh[:, slot, c], wl[:, slot, c],
                                               hT_h[:, k, :], hT_l[:, k, :],
                                               k == 0, k == KT - 1)
                    mm.then_inc(w_used, 1)

                def x_T(src, bank, ready):
                    for k in range(4):
                        t, half = divmod(k, 2)
                        if half == 0:
                            pe.wait_ge(F[ready[0]], ready[1] + t)
                        for j in range(4):
                            c = (4 * half + j) * P
                            mm = pe.transpose(ps[:, bank + k, j * P:(j + 1) * P],
                                              src[:, t, c:c + P], ident[:])
                        mm.then_inc(F["xT_ready"], 1)

                def wide(u, n, k0, act_h, act_l, first, last, banks=0, name=None, turn=0):
                    slot = unit(u, turn)
                    for b in range(4):
                        t, half = divmod(b, 2)
                        tok = slice(t * P, (t + 1) * P)
                        for k in range(n):
                            c = slice(k * D + half * 512, k * D + half * 512 + 512)
                            mm = split_product(ps[:, banks + b, :],
                                               act_h[:, k0 + k, tok], act_l[:, k0 + k, tok],
                                               wh[:, slot, c], wl[:, slot, c],
                                               first and k == 0, last and k == n - 1)
                        if b < 3 and name:
                            mm.then_inc(F[name], 1)
                    mm.then_inc(w_used, 1)

                def scores(g, q, k, prev_mask, order=PAIRED):
                    def tile_0(heads):
                        for h in heads:
                            o = ps[:, 4, h * P:(h + 1) * P]
                            pe.matmul(o, q(h)[:, 0:P], k(h)[:, 0:P], start=(h == 0), stop=False,
                                      skip_group_check=True)
                            mm = pe.matmul(o, ident_b[:], causal[:], start=False, stop=True,
                                           skip_group_check=True)
                        return mm

                    tile_0(order[0:2]).then_inc(F["half_scores"], 1)
                    for i, h in enumerate(order):
                        c = (i % 2) * 256
                        o = ps[:, 5 + i // 2, c:c + 256]
                        pe.matmul(o, q(h)[:, P:SEQ], k(h)[:, 0:SEQ], start=(i % 2 == 0),
                                  stop=False, skip_group_check=True)
                        if prev_mask is not None:
                            pe.matmul(o[:, 0:P], ident_b[:], prev_mask[:], start=False,
                                      stop=True, skip_group_check=True)
                        pe.matmul(o[:, P:256], ident_b[:], causal[:], start=False,
                                  stop=True, skip_group_check=True)
                    pe.wait_ge(F["half_scores"], g + 1)
                    tile_0(order[2:4]).then_inc(F["scores_ready"], 1)

                def probs_T(g):
                    for h in range(H):
                        if h == 0:
                            pe.wait_ge(F["probs_ready"], 8 * g + 4)
                        mm = pe.transpose(ps[:, 4, h * P:(h + 1) * P], pb[:, h * P:(h + 1) * P],
                                          ident[:])
                    mm.then_inc(F["probs_T"], 1)
                    for b in range(2):
                        pe.wait_ge(F["probs_ready"], 8 * g + 6 + 2 * b)
                        for j in range(4):
                            c = 512 + b * 512 + j * P
                            mm = pe.transpose(ps[:, 5 + b, j * P:(j + 1) * P], pb[:, c:c + P],
                                              ident[:])
                        mm.then_inc(F["probs_T"], 1)

                def pv(g, v, bank, order=PAIRED):
                    pe.wait_ge(F["pt_ready"], 3 * g + 3)
                    for h in range(H):
                        pe.matmul(ps[:, bank, h * HD:(h + 1) * HD], pt[:, h * P:(h + 1) * P],
                                  v(h, 0), start=True, stop=True, skip_group_check=True)
                    for h in range(H):
                        for k in range(TT):
                            c = 512 + order.index(h) * 256 + k * P
                            mm = pe.matmul(ps[:, bank, 256 + h * HD:256 + (h + 1) * HD],
                                           pt[:, c:c + P], v(h, k), start=(k == 0),
                                           stop=(k == TT - 1), skip_group_check=True)
                    mm.then_inc(F["pv_ready"], 1)

                def head(qkT, pair, h):
                    return qkT[(h % 2) * HD:(h % 2) * HD + HD, pair + h // 2, :]

                x_T(hn, 4, ("hn_ready", 1))
                pe.wait_ge(F["xT_low"], 4)
                project(M_MLA_A, (0, 1), 0)
                pe.wait_ge(conv_landed, layer * 16 + 16)
                project(M_MLA_B, (0, 1), MLA_COLS // 2)
                for a in range(4):
                    mm = pe.transpose(ps[:, 7, a * 44:a * 44 + 44], conv_raw[:, a, :],
                                      ident[0:2 * FT, 0:2 * FT])
                mm.then_inc(F["conv_T"], 1)
                project(M_MOBA_Q, (2, 3), 0)
                for t in range(TT):
                    pe.wait_ge(F["lat_done"], t + 1)
                    for n, (c, w) in enumerate(((0, P), (P, QR - P), (QR, KVR))):
                        mm = pe.transpose(ps[0:w, 4 + t, n * P:(n + 1) * P], pr[:, 0, t, c:c + w],
                                          ident[:])
                    mm.then_inc(F["lat_T"], 1)
                project(M_MOBA_K, (2, 3), 256)
                pe.wait_ge(uq_landed, layer * 16 + 16)
                pe.wait_ge(uq2_landed, layer * 16 + 16)
                pe.wait_ge(ukv_landed, layer * 16 + 16)
                pe.wait_ge(F["cT_ready"], 2)
                pe.wait_ge(F["conv_ready"], 1)
                for t in range(TT):
                    tok = slice(t * P, (t + 1) * P)
                    o = ps[:, 4 + 2 * t, 0:H * QK]
                    pe.matmul(o, cT[:, 0, tok], uq[:, 0, :], start=True, stop=False)
                    pe.matmul(o, cT[0:QR - P, 1, tok], uq[0:QR - P, 1, :], start=False, stop=True)
                    pe.matmul(ps[:, 5 + 2 * t, :], cT[:, 2, tok], ukv[:], start=True, stop=True
                              ).then_inc(F["mla_up"], 1)
                pe.wait_ge(F["pr_ready"], 2)
                project(M_MOBA_V, (0, 1), 0)
                pe.wait_ge(F["pr_ready"], 4)
                project(M_SWA_Q, (2, 3), 0)
                pe.wait_ge(F["mla_up_ready"], 4)
                pe.wait_ge(F["mla_qk"], 2)
                for t in range(TT):
                    for a, src in ((0, mq), (1, mk)):
                        for h in range(H):
                            mm = pe.transpose(ps[0:QK, 4 + 2 * t + a, h * P:(h + 1) * P],
                                              src[:, t, h, :], ident[:])
                    mm.then_inc(F["mla_T"], 1)
                project(M_SWA_KV, (2, 3), 256)
                pe.wait_ge(F["mT_ready"], 4)
                scores(0, lambda h: mT[0:QK, 0, h, :], lambda h: mT[0:QK, 1, h, :], None)
                pe.wait_ge(F["v_ready"], 2)
                pe.wait_ge(F["moba_qk"], 1)
                for t in range(TT):
                    for j in range(4):
                        mm = pe.transpose(ps[:, t, j * P:(j + 1) * P], rot[:, t, j * P:(j + 1) * P],
                                          ident[:])
                    mm.then_inc(F["moba_T"], 1)
                pe.wait_ge(F["pr_ready"], 6)
                pe.wait_ge(F["v_ready"], 4)
                project(M_SB_V, (2, 3), 0)
                probs_T(0)
                pe.wait_ge(F["mobaT_ready"], 2)
                project_T(M_SB_Q, 0)
                pv(0, lambda h, k: mkv[:, k, h, NOPE:], 7)
                scores(1, lambda h: head(qkT_moba, 0, h), lambda h: head(qkT_moba, 2, h), None)
                pe.wait_ge(F["v_ready"], 6)
                pe.wait_ge(F["swa_qk"], 1)
                for t in range(TT):
                    for j in range(3):
                        mm = pe.transpose(ps[:, 2 + t, j * P:(j + 1) * P],
                                          pr[:, 1, t, j * P:(j + 1) * P], ident[:])
                    mm.then_inc(F["swa_T"], 1)
                project_T(M_SB_K, 1)
                probs_T(1)
                pe.wait_ge(F["sbT_ready"], 2)
                pe.wait_ge(F["swaT_ready"], 2)
                for b in range(2):
                    for j in range(2):
                        h = PAIRED[2 * b + j]
                        o = ps[:, b, j * 256:(j + 1) * 256]
                        pe.matmul(o, head(qkT_sb, 2, h)[:, 0:P], head(qkT_sb, 0, h),
                                  start=(j == 0), stop=False, skip_group_check=True)
                        mm = pe.matmul(o[:, 0:P], ident_b[:], above[:], start=False, stop=True,
                                       skip_group_check=True)
                    mm.then_inc(F["sb_z"], 1)
                for i, h in enumerate(PAIRED):
                    o = ps[:, 2, h * P:(h + 1) * P]
                    if i == 2:
                        pe.wait_ge(F["half_z"], 1)
                    pe.matmul(o, head(qkT_sb, 2, h)[:, P:SEQ], head(qkT_sb, 0, h)[:, P:SEQ],
                              start=(i == 0), stop=False, skip_group_check=True)
                    mm = pe.matmul(o, ident_b[:], above[:], start=False, stop=True,
                                   skip_group_check=True)
                    if i == 1:
                        mm.then_inc(F["half_z"], 1)
                mm.then_inc(F["sb_z"], 1)
                pe.wait_ge(F["group_out"], 1)
                pv(1, lambda h, k: v_moba[:, k, h * HD:(h + 1) * HD], 7)

                scores(2, lambda h: qkT_swa[(h // 2) * HD:(h // 2) * HD + HD, h % 2, :],
                       lambda h: qkT_swa[(h // 2) * HD:(h // 2) * HD + HD, 2, :], above,
                       GROUPED)
                pe.wait_ge(F["sb_soft"], 3)
                for b in range(2):
                    for j in range(2):
                        i = 2 * b + j
                        h = PAIRED[i]
                        o = ps[:, b, j * 256:(j + 1) * 256]
                        pe.matmul(o, neg_tri[:], sb_sp[:, i * 256:(i + 1) * 256], start=False,
                                  stop=False, skip_group_check=True)
                        mm = pe.matmul(o[:, P:256], neg_ones[:],
                                       sb_sp[:, 1024 + h * P:1024 + (h + 1) * P], start=False,
                                       stop=True, skip_group_check=True)
                    mm.then_inc(F["sb_minus"], 1)
                pe.matmul(ps[:, 2, :], neg_tri[:], sb_sp[:, 1024:1536], start=False, stop=True,
                          skip_group_check=True).then_inc(F["sb_minus"], 1)
                probs_T(2)
                pe.wait_ge(F["group_out"], 2)
                pe.wait_ge(F["sb_probs"], 3)
                for t in range(TT):
                    for h in range(H):
                        o = ps[:, 7, t * 256 + h * HD:t * 256 + (h + 1) * HD]
                        c = PAIRED.index(h) * 256 + t * P
                        mm = pe.matmul(o, sb_e[:, c:c + P], v_sb[:, 0, h * HD:(h + 1) * HD],
                                       start=True, stop=(t == 0), skip_group_check=True)
                        if t == 1:
                            mm = pe.matmul(o, sb_e[:, 1024 + h * P:1024 + (h + 1) * P],
                                           v_sb[:, 1, h * HD:(h + 1) * HD], start=False,
                                           stop=True, skip_group_check=True)
                mm.then_inc(F["pv_ready"], 1)
                pv(2, lambda h, k: v_swa[:, k, (h // 2) * HD:(h // 2 + 1) * HD], 3,
                   GROUPED)
                for n, g in enumerate(GROUP_ORDER):
                    pe.wait_ge(F["group_done"], n + 1)
                    for k in range(2):
                        for t in range(TT):
                            mm = pe.transpose(
                                ps[:, 4 + n, k * 256 + t * P:k * 256 + (t + 1) * P],
                                hn[:, t, g * GW + k * P:g * GW + (k + 1) * P], ident[:])
                    mm.then_inc(F["groups_T"], 1)
                pe.wait_ge(F["mT_low"], 4)
                pe.wait_ge(F["group_out"], 4)
                for n, (k, m) in enumerate(WO_ROWS):
                    last = n == len(WO_ROWS) - 1
                    wide(U_WO + n, m, k, hT_h, hT_l, n == 0, last,
                         name="wo_done" if last else None)

                x_T(hn, 4, ("hn_ready", 3))
                pe.wait_ge(F["xT_low"], 8)

                def up(s, par, u, turn=0):
                    for half in range(2):
                        slot = unit(u + half, turn)
                        if half == 0:
                            ge(pe, "conv_done", (s - 1) * 4)
                        for j in range(2):
                            for k in range(KT):
                                c = slice(k * 256 + j * P, k * 256 + (j + 1) * P)
                                mm = split_product(
                                    ps[:, 4 + 2 * par + half, j * 256:(j + 1) * 256],
                                    wh[:, slot, c], wl[:, slot, c], hT_h[:, k, :], hT_l[:, k, :],
                                    k == 0, k == KT - 1)
                        mm.then_inc(w_used, 1)

                def down(s, par, u, first=False, last=False, turn=0):
                    pe.wait_ge(F["g_low"], s + 1)
                    if first:
                        pe.wait_ge(F["x_mid"], TT)
                    wide(u, 2, 0, gT_h[:, par], gT_l[:, par], first, last,
                         name="down_done" if last else None, turn=turn)

                up(0, 0, unit_gate(0))
                for s in range(1, LOOP_FROM):
                    up(s, s % 2, unit_gate(s))
                    down(s - 1, (s - 1) % 2, unit_gate(s) + 2, first=(s == 1))
                with pe.Fori(0, LOOPS) as turn:
                    for j in range(2):
                        s = LOOP_FROM + j
                        up(turn * 2 + s, s % 2, unit_gate(s), turn)
                        down(turn * 2 + (s - 1), (s - 1) % 2, unit_gate(s) + 2, turn=turn)
                pe.wait_ge(F["conv_done"], 4 * (STEPS - 1))
                pe.wait_ge(p_landed, layer * 16 + 16)
                for k in range(2):
                    for t in range(TT):
                        mm = pe.transpose(ps[:, 6, k * 256 + t * P:k * 256 + (t + 1) * P],
                                          p_sb[:, t, k * P:(k + 1) * P], ident[:])
                mm.then_inc(F["p_T"], 1)
                down(STEPS - 1, 0, U_AFTER, last=True)

                pe.wait_ge(F["conv_done"], 4 * STEPS)
                pe.wait_ge(F["pT_low"], 1)
                wide(U_PROJ, 2, 0, pT_h, pT_l, True, True, banks=4)
                x_T(x, 0, ("x_low", 1))
                pe.wait_ge(F["xT_low"], 12)
                for n, (k, m) in enumerate(GATE_ROWS):
                    last = n == len(GATE_ROWS) - 1
                    wide(U_GATE + n, m, k, hT_h, hT_l, n == 0, last,
                         name="gate_ready" if last else None)
                pe.drain().then_inc(F["arrived"], 1)
                pe.wait_ge(released, layer + 2)

        @block.vector
        def _(dve):
            tt, stt, ts = dve.tensor_tensor, dve.scalar_tensor_tensor, dve.tensor_scalar

            rope_steps = [0]

            def rope_chained(ins):
                rope_steps[0] += 1
                ins.then_inc(rope_step, 1)
                dve.wait_ge(rope_step, rope_steps[0])

            dve.wait_ge(pos_landed, 16)
            rope_chained(dve.tensor_copy(pos_f[:], pos_i[:]))
            dve.wait_ge(consts_made, 6)
            angle, turns = tmp[:, 128:192], tmp[:, 192:256]
            for t in range(TT):
                rope_chained(ts(angle[:, t * 32:(t + 1) * 32], inv_freq[:], pos_f[:, t:t + 1],
                                None, ALU.mult))
            rope_chained(ts(turns, angle, float(1.0 / (2.0 * np.pi)), MAGIC, ALU.mult, ALU.add))
            rope_chained(ts(turns, turns, -MAGIC, None, ALU.add))
            for part in TWO_PI:
                rope_chained(stt(angle, turns, -part, angle, ALU.mult, ALU.add))
            pi = 3.1415925
            rope_chained(ts(tmp[:, 0:64], angle, pi, -pi, ALU.min, ALU.max))
            rope_chained(ts(tmp[:, 64:128], tmp[:, 0:64], -1.0, None, ALU.mult))
            rope_chained(tt(tmp[:, 64:128], tmp[:, 64:128], tmp[:, 0:64], ALU.min))
            rope_chained(ts(tmp[:, 64:128], tmp[:, 64:128], float(np.pi / 2), None, ALU.add))
            dve.sem_inc(rope_arg, 1)
            dve.wait_ge(rope_sin, 2)
            rope_chained(dve.tensor_copy(rope_c[:, :, 32:64], rope_c[:, :, 0:32]))
            rope_chained(ts(rope_s[:, :, 0:32], rope_s[:, :, 32:64], -1.0, None, ALU.mult))
            for a in range(2):
                rope_chained(dve.tensor_copy(rope_c32[:, :, a * 16:(a + 1) * 16],
                                             rope_c[:, :, 0:32:2]))
                rope_chained(dve.tensor_copy(rope_s32[:, :, a * 16:(a + 1) * 16],
                                             rope_s[:, :, a * 32:(a + 1) * 32:2]))

            with dve.Fori(0, DEPTH) as layer:
                steps = [0]

                def chained(ins):
                    steps[0] += 1
                    ins.then_inc(F["dve_step"], 1)
                    dve.wait_ge(F["dve_step"], steps[0])

                def mean(a, n, width, name=None):
                    ins = ts(stat(a, n), stat(a, n), 1.0 / width, EPS, ALU.mult, ALU.add)
                    if name:
                        ins.then_inc(F[name], 1)
                    else:
                        chained(ins)

                def newton(a, n, name, k):
                    dve.wait_ge(F[name], k)
                    y, r = stat(a + n, n), stat(a + 2 * n, n)
                    chained(tt(r, y, y, ALU.mult))
                    chained(stt(r, r, -0.5, stat(a, n), ALU.mult, ALU.mult))
                    chained(stt(r, r, 1.5, y, ALU.add, ALU.mult))

                def norm(n):
                    dve.wait_ge(F["x_squared"], TT * (n + 1))
                    mean(ST_X, TT, D, "stat_in")
                    newton(ST_X, TT, "stat_root", n + 1)
                    g = ng[:, n * D:(n + 1) * D]
                    for t in range(TT):
                        stt(hn[:, t, :], x[:, t, :], stat(ST_X + 4 + t), g, ALU.mult, ALU.mult
                            ).then_inc(F["hn_ready"], 1)

                def x_low(n, bank):
                    for k in range(4):
                        t, half = divmod(k, 2)
                        o = (slice(None), slice(4 * half, 4 * half + 4), slice(t * P, (t + 1) * P))
                        dve.wait_ge(F["xT_high"], n + k + 1)
                        tt(hT_l[o], ps[:, bank + k, :].rearrange("p (k n) -> p k n", k=4),
                           hT_h[o].bitcast(F32), ALU.subtract).then_inc(F["xT_low"], 1)

                def rotate(i_q, i_k, kh, name):
                    w = HD // 2
                    view = lambda ap, c, n: ap[:, :, c:c + n * HD].rearrange(
                        "p t (h n) -> p t h n", h=n)
                    tmp2 = tmp[:].rearrange("p (t n) -> p t n", t=TT)
                    for i, c, n in ((i_q, 0, H), (i_k, GW, kh)):
                        src, r, o = view(pr[:, 1], c, n), view(rot, c, n), view(tmp2, c, n)
                        shape = [P, TT, n, HD]
                        last = tt(r, src, gc[:, i].unsqueeze(2).broadcast_to(shape), ALU.mult)
                        half = [P, TT, n, w]
                        for a in range(2):
                            last = tt(o[:, :, :, a * w:(a + 1) * w],
                                      src[:, :, :, (1 - a) * w:(2 - a) * w],
                                      gs[:, i, :, a * w:(a + 1) * w].unsqueeze(2)
                                      .broadcast_to(half), ALU.mult)
                    chained(last)
                    if kh == H:
                        tt(rot[:], rot[:], tmp2, ALU.add).then_inc(F[name], 1)
                        return
                    for t in range(TT):
                        order = [ap[:, t, 0:GW].rearrange("p (a b n) -> p b a n", a=2, b=2)
                                 for ap in (rot, tmp2)]
                        tt(pr[:, 1, t, 0:GW].rearrange("p (b a n) -> p b a n", a=2, b=2),
                           *order, ALU.add)
                    n = slice(GW, GW + kh * HD)
                    tt(pr[:, 1, :, n], rot[:, :, n], tmp2[:, :, n], ALU.add
                       ).then_inc(F[name], 1)

                def heads_norm(a, kh, stat_name, root_name, rs):
                    n = TT * (H + kh)
                    chained(dve.tensor_reduce(
                        stat(a, n), rot[:, :, 0:(H + kh) * HD].rearrange("p t (h n) -> p t h n", n=HD),
                        AX.X, ALU.add))
                    mean(a, n, HD, stat_name)
                    newton(a, n, root_name, 1)
                    r = stat(a + 2 * n, n).rearrange("p (t h) -> p t h", t=TT)
                    ts(stat(rs, 8).rearrange("p (t h) -> p t h", t=TT), r[:, :, 0:H], HD ** -0.5,
                       None, ALU.mult)
                    k = pr[:, 1, :, GW:GW + kh * HD].rearrange("p t (h n) -> p t h n", h=kh)
                    chained(tt(k, k, r[:, :, H:H + kh].unsqueeze(3).broadcast_to([P, TT, kh, HD]),
                               ALU.mult))

                def row_max(g, rs, signal=True):
                    dve.wait_ge(F["scores_ready"], g + 1)
                    ge(dve, "probs_ready", 8 * g)
                    dve.tensor_reduce(stat(MX, H), ps[:, 4, :].rearrange("p (h n) -> p h n", h=H),
                                      AX.X, ALU.max)
                    heads = ("p (h b) -> p b h" if g < 2 else "p (b h) -> p b h")
                    chained(dve.tensor_reduce(
                        stat(MX + H, H).rearrange(heads, b=2),
                        ps[:, 5:7, :].rearrange("p b (h n) -> p b h n", h=2), AX.X, ALU.max))
                    if signal:
                        stt(stat(NB, 8), stat(MX, 8), -1.0, stat(rs, 8), ALU.mult, ALU.mult
                            ).then_inc(F["softmax_bias"], 1)

                def probs_out(g):
                    ge(dve, "pv_ready", g)
                    for b in range(3):
                        dve.wait_ge(F["probs_T"], 3 * g + b + 1)
                        dve.tensor_copy(pt[:, b * 512:(b + 1) * 512], ps[:, 4 + b, :]
                                        ).then_inc(F["pt_ready"], 1)

                def group_cols(ap, n):
                    c = GROUP_ORDER[n] * GW
                    return ap[:, :, c:c + GW]

                def out_heads(n):
                    return group_cols(hn, n).rearrange("p t (h n) -> p t h n", h=H)

                def divided(n, bank, den, pv_n):
                    dve.wait_ge(F["pv_ready"], pv_n)
                    chained(dve.reciprocal(stat(RDEN, 8), stat(den, 8)))
                    tt(out_heads(n), ps[:, bank, :].rearrange("p (t h n) -> p t h n", t=TT, h=H),
                       stat(RDEN, 8).rearrange("p (t h) -> p t h", t=TT).unsqueeze(3)
                       .broadcast_to([P, TT, H, HD]), ALU.mult).then_inc(F["group_out"], 1)

                def group_mean(n):
                    dve.wait_ge(F["group_sq"], TT * (n + 1))
                    mean(ST_G + 6 * n, TT, GW, "group_stat")

                def group_norm(n):
                    newton(ST_G + 6 * n, TT, "group_root", n + 1)
                    c = GROUP_ORDER[n] * GW
                    for t in range(TT):
                        last = stt(hn[:, t, c:c + GW], hn[:, t, c:c + GW],
                                   stat(ST_G + 6 * n + 4 + t),
                                   ng[:, G_GROUP + c:G_GROUP + c + GW], ALU.mult, ALU.mult)
                    last.then_inc(F["group_done"], 1)

                dve.wait_ge(ng_landed, layer * 16 + 16)
                norm(0)
                x_low(0, 4)
                dve.wait_ge(sg_landed, layer * 16 + 16)
                for i, c in enumerate((S_SWAQ, S_SWAK, S_MOBAQ, S_MOBAK)):
                    def gain(a, n):
                        return sg[:, a:a + n].unsqueeze(1).broadcast_to([P, TT, n])
                    tt(gc[:, i], rope_c[:], gain(c, HD), ALU.mult)
                    tt(gs[:, i, :, 0:32], rope_s[:, :, 0:32], gain(c + 32, 32), ALU.mult)
                    last = tt(gs[:, i, :, 32:64], rope_s[:, :, 32:64], gain(c, 32), ALU.mult)
                chained(last)
                dve.wait_ge(F["conv_T"], 1)
                dve.tensor_copy(conv[:], ps[:, 7, 0:176].rearrange("p (a n) -> p a n", a=4)
                                ).then_inc(F["conv_ready"], 1)

                dve.wait_ge(F["squared"], 2)
                for a, c, w in ((ST_L, 0, QR), (ST_L + 2, QR, KVR), (ST_PE, QR + KVR, PE_DIM)):
                    last = dve.tensor_reduce(stat(a, 2), rot[:, :, c:c + w], AX.X, ALU.add)
                chained(last)
                chained(ts(stat(ST_L, 2), stat(ST_L, 2), 1.0 / QR, EPS, ALU.mult, ALU.add))
                mean(ST_L + 2, 2, KVR, "lat_stat")
                def rope32(o, src, scratch, shape):
                    full, half = [*shape, PE_DIM], [*shape, 16]

                    def table(a, c, w):
                        a = a[:, :, c:c + w]
                        return a if len(shape) == 2 else a.unsqueeze(2).broadcast_to([*shape, w])
                    one, two = scratch
                    tt(one, src, table(rope_c32, 0, PE_DIM), ALU.mult)
                    at = [slice(None)] * (len(shape))
                    for a in range(2):
                        last = tt(two[(*at, slice(a * 16, a * 16 + 16))],
                                  src[(*at, slice(16 - a * 16, 32 - a * 16))],
                                  table(rope_s32, a * 16, 16), ALU.mult)
                    chained(last)
                    return tt(o, one, two, ALU.add)

                kp = tmp[:, 512:576].rearrange("p (t n) -> p t n", t=TT)
                chained(tt(kp, pr[:, 0, :, QR + KVR:MLA_COLS],
                           sg[:, S_MLAK + NOPE:S_MLAK + QK].unsqueeze(1)
                           .broadcast_to([P, TT, PE_DIM]), ALU.mult))
                chained(rope32(kpe[:], kp, [tmp[:, 576 + 64 * a:640 + 64 * a].rearrange(
                    "p (t n) -> p t n", t=TT) for a in range(2)], [P, TT]))
                newton(ST_L, 4, "lat_root", 1)
                for t in range(TT):
                    for j, (c, w, g) in enumerate(((0, QR, S_QN), (QR, KVR, S_KVN))):
                        v = pr[:, 0, t, c:c + w]
                        last = stt(v, v, stat(ST_L + 8 + 2 * j + t), sg[:, g:g + w], ALU.mult,
                                   ALU.mult)
                    last.then_inc(F["lat_done"], 1)

                dve.wait_ge(F["squared"], 5)
                dve.tensor_reduce(stat(ST_M, 8),
                                  rot[:, :, 0:H * QK].rearrange("p t (h n) -> p t h n", n=QK),
                                  AX.X, ALU.add)
                chained(dve.tensor_reduce(
                    stat(ST_M + 8, 8), tmp[:, 0:512].rearrange("p (h n) -> p h n", n=NOPE),
                    AX.X, ALU.add))
                ssk = stat(ST_M + 8, 8).rearrange("p (t h) -> p t h", t=TT)
                chained(tt(ssk, ssk, stat(ST_PE, 2).unsqueeze(2).broadcast_to([P, TT, H]),
                           ALU.add))
                mean(ST_M, 16, QK, "mla_stat")
                q8 = mq.rearrange("p t h n -> p (t h) n")
                chained(tt(q8, q8, sg[:, S_MLAQ:S_MLAQ + QK].unsqueeze(1)
                           .broadcast_to([P, 8, QK]), ALU.mult))
                qpe = mq[:, :, :, NOPE:QK]
                rope32(qpe, qpe, [tmp[:, 512 + 256 * a:768 + 256 * a].rearrange(
                    "p (t h n) -> p t h n", t=TT, h=H) for a in range(2)], [P, TT, H]
                    ).then_inc(F["mla_qk"], 1)
                newton(ST_M, 16, "mla_root", 1)
                ts(stat(RS_MLA, 8), stat(ST_M + 32, 8), QK ** -0.5, None, ALU.mult)
                rk = stat(ST_M + 40, 8).rearrange("p (t h) -> p t h", t=TT)
                chained(tt(mk[:, :, :, 0:NOPE], mkv[:, :, :, 0:NOPE],
                           rk.unsqueeze(3).broadcast_to([P, TT, H, NOPE]), ALU.mult))
                k8 = mk[:].rearrange("p t h n -> p (t h) n")[:, :, 0:NOPE]
                tt(k8, k8, sg[:, S_MLAK:S_MLAK + NOPE].unsqueeze(1).broadcast_to([P, 8, NOPE]),
                   ALU.mult)
                tt(mk[:, :, :, NOPE:QK], kpe[:].unsqueeze(2).broadcast_to([P, TT, H, PE_DIM]),
                   rk.unsqueeze(3).broadcast_to([P, TT, H, PE_DIM]), ALU.mult
                   ).then_inc(F["mla_qk"], 1)

                dve.wait_ge(F["squared"], 6)
                heads_norm(ST_B, H, "moba_stat", "moba_root", RS_MOBA)
                rotate(2, 3, H, "moba_qk")

                row_max(0, RS_MLA)
                probs_out(0)
                dve.wait_ge(F["squared"], 7)
                dve.wait_ge(F["moba_T"], 2)
                heads_norm(ST_S, 2, "swa_stat", "swa_root", RS_SWA)
                rotate(0, 1, 2, "swa_qk")
                divided(0, 7, DENS[0], 1)
                row_max(1, RS_MOBA)
                group_mean(0)
                group_norm(0)
                probs_out(1)
                for b in range(3):
                    c = slice(b * 512, (b + 1) * 512)
                    dve.wait_ge(F["sb_log"], b + 1)
                    stt(sb_sp[:, c], ps[:, b, :], 0.0, sb_e[:, c], ALU.max, ALU.add
                        ).then_inc(F["sb_soft"], 1)
                divided(1, 7, DENS[1], 2)
                row_max(2, RS_SWA, signal=False)
                sinks = sg[:, S_SINK:S_SINK + H].unsqueeze(1).broadcast_to([P, TT, H])
                chained(tt(stat(MX, 8), stat(MX, 8), stat(RS_SWA, 8), ALU.mult))
                mx = stat(MX, 8).rearrange("p (t h) -> p t h", t=TT)
                chained(tt(mx, mx, sinks, ALU.max))
                tt(stat(SNK, 8).rearrange("p (t h) -> p t h", t=TT), sinks, mx, ALU.subtract
                   ).then_inc(F["sink_arg"], 1)
                ts(stat(NB, 8), stat(MX, 8), -1.0, None, ALU.mult).then_inc(F["softmax_bias"], 1)
                group_mean(1)
                group_norm(1)
                probs_out(2)
                dve.wait_ge(F["pv_ready"], 3)
                dve.tensor_copy(group_cols(hn, 2),
                                ps[:, 7, :].rearrange("p (t n) -> p t n", t=TT)
                                ).then_inc(F["group_out"], 1)
                dve.wait_ge(F["probs_ready"], 24)
                dve.wait_ge(F["sink_exp"], 1)
                chained(tt(stat(DENS[2], 8), stat(DENS[2], 8), stat(SNK, 8), ALU.add))
                divided(3, 3, DENS[2], 4)
                for n in (2, 3):
                    group_mean(n)
                    group_norm(n)
                for n, g in enumerate(GROUP_ORDER):
                    dve.wait_ge(F["mT_high"], n + 1)
                    o = hT_l[:, 2 * g:2 * g + 2, :]
                    tt(o, ps[:, 4 + n, :].rearrange("p (k n) -> p k n", k=2),
                       hT_h[:, 2 * g:2 * g + 2, :].bitcast(F32), ALU.subtract
                       ).then_inc(F["mT_low"], 1)

                def add_to_x(name, unit, done):
                    for t in range(TT):
                        if t == 0:
                            dve.wait_ge(F[name], 2)
                        else:
                            unit_done(dve, layer, unit)
                        xs = x[:, t, :].rearrange("p (b n) -> p b n", b=2)
                        tt(xs, xs, ps[:, 2 * t:2 * t + 2, :], ALU.add).then_inc(F[done], 1)

                add_to_x("wo_done", U_FFN - 1, "x_mid")
                norm(1)
                x_low(4, 4)

                def mlp(s, par):
                    bank = 4 + 2 * par
                    for tap, name, before in ((1, "tap1", "tap2"), (0, "conv_done", "tap1")):
                        d = 2 - tap
                        for i in range(4):
                            half, j = divmod(i, 2)
                            f = bass.ds(s * 2 + (half * FT + j), 1)
                            o = cv[par][:, i, d:SEQ]
                            dve.wait_ge(F[before], s * 4 + (2 * half + 2 if tap else i + 1))
                            stt(o, ps[:, bank + half, j * 256:j * 256 + SEQ - d],
                                conv[:, tap, f], o, ALU.mult, ALU.add).then_inc(F[name], 1)
                    dve.wait_ge(F["silu"], s + 1)
                    dve.wait_ge(F["conv_done"], s * 4 + 4)
                    g = cv[par][:, 0:2, :]
                    tt(g, g, cv[par][:, 2:4, :], ALU.mult).then_inc(F["prod"], 1)
                    dve.wait_ge(F["g_high"], s + 1)
                    tt(gT_l[:, par], g, gT_h[:, par].bitcast(F32), ALU.subtract
                       ).then_inc(F["g_low"], 1)

                for s in range(LOOP_FROM):
                    mlp(s, s % 2)
                with dve.Fori(0, LOOPS) as turn:
                    for j in range(2):
                        mlp(turn * 2 + (LOOP_FROM + j), (LOOP_FROM + j) % 2)

                dve.wait_ge(F["pT_high"], 1)
                tt(pT_l, ps[:, 6, :].rearrange("p (k n) -> p k n", k=2), pT_h.bitcast(F32),
                   ALU.subtract).then_inc(F["pT_low"], 1)
                add_to_x("down_done", U_AFTER, "x_low")
                x_low(8, 0)
                for b in range(4):
                    t, half = divmod(b, 2)
                    c = slice(half * 512, (half + 1) * 512)
                    dve.wait_ge(F["sigmoid"], b + 1)
                    unit_done(dve, layer, U_PROJ)
                    tt(hn[:, t, c], ps[:, 4 + b, :], hn[:, t, c], ALU.mult
                       ).then_inc(F["ple_term"], 1)
                    dve.wait_ge(F["ple_term"], b + 1)
                    tt(x[:, t, c], x[:, t, c], hn[:, t, c], ALU.add)
                dve.drain().then_inc(F["arrived"], 1)
                dve.wait_ge(released, layer + 2)


def kernel(x, p, positions, attn_norm, w_in, mla_q_norm, mla_w_uq, mla_kv_norm, mla_w_ukv,
           mla_q_gain, mla_k_gain, swa_q_gain, swa_k_gain, swa_sinks, moba_q_gain, moba_k_gain,
           group_norm, w_o, ffn_norm, w_up, conv_w, conv_b, w_down, ple_proj, ple_gate):
    import concourse.bacc as bacc
    from concourse.bass_utils import run_bass_kernel_spmd

    a = {k: np.asarray(v) for k, v in locals().items() if k not in ("bacc", "run_bass_kernel_spmd")}
    norm_gains = np.concatenate([a["attn_norm"], a["ffn_norm"], a["group_norm"]], axis=1)
    small = np.concatenate([a[n] for n in (
        "swa_q_gain", "swa_k_gain", "moba_q_gain", "moba_k_gain", "mla_q_gain", "mla_k_gain",
        "mla_q_norm", "mla_kv_norm", "swa_sinks")], axis=1)
    taps = a["conv_w"].reshape(DEPTH, 3, 2 * FT, P).transpose(0, 2, 1, 3)
    bias = a["conv_b"].reshape(DEPTH, 2 * FT, 1, P)
    conv_rows = np.concatenate([taps, bias], axis=2)
    arrays = {"x_in": a["x"], "p_in": a["p"], "positions": a["positions"], "w_in": a["w_in"],
              "w_uq": a["mla_w_uq"], "w_ukv": a["mla_w_ukv"], "norm_gains": norm_gains,
              "small_gains": small, "w_o": a["w_o"], "w_up": a["w_up"], "conv_rows": conv_rows,
              "w_down": a["w_down"], "ple_proj": a["ple_proj"], "ple_gate": a["ple_gate"]}
    arrays = {k: np.ascontiguousarray(v) for k, v in arrays.items()}
    nc = bacc.Bacc("TRN2", target_bir_lowering=False, num_devices=1)
    args = [nc.dram_tensor(k, v.shape, mybir.dt.from_np(v.dtype), kind="ExternalInput").ap()
            for k, v in arrays.items()]
    out = nc.dram_tensor("out", (1, SEQ, D), F32, kind="ExternalOutput").ap()
    build(nc, *args, out)
    r = run_bass_kernel_spmd(nc, [arrays], core_ids=[0])
    return r.results[0]["out"]
```

```python
from contextlib import ExitStack

import numpy as np

import concourse.bass as bass
from concourse import mybir

F32 = mybir.dt.float32
F32R = mybir.dt.float32r
BF16 = mybir.dt.bfloat16
I32 = mybir.dt.int32
ALU = mybir.AluOpType
ACT = mybir.ActivationFunctionType
AX = mybir.AxisListType

P = 128
D = 1024
SEQ = 256
DEPTH = 2
TT = SEQ // P
KT = D // P
H = 4
HD = 64
GW = H * HD
ROPE_THETA = 10000.0
EPS = 1e-6
NEG = -1e30
QR, KVR = 192, 128
NOPE, PE_DIM = 64, 32
QK = NOPE + PE_DIM
DFF = 2816
FT = DFF // P
PLE = 256

OFF_SB, OFF_MLA = 0, 3 * GW
OFF_SWA = OFF_MLA + QR + KVR + PE_DIM
OFF_MOBA = OFF_SWA + GW + 2 * 2 * HD
MLA_COLS = QR + KVR + PE_DIM

SB, MLA, SWA, MOBA = range(4)

G_ATTN, G_FFN, G_GROUP = 0, D, 2 * D
S_SWAQ, S_SWAK, S_MOBAQ, S_MOBAK = 0, 64, 128, 192
S_MLAQ, S_MLAK = 256, 256 + QK
S_QN = S_MLAK + QK
S_KVN = S_QN + QR
S_SINK = S_KVN + KVR
S_ALL = S_SINK + H

RING = 3
(M_MLA_A, M_MLA_B, M_SB_Q, M_SB_K, M_SB_V, M_MOBA_Q, M_MOBA_K, M_SWA_Q, M_SWA_KV, M_MOBA_V
 ) = range(10)
WIN_PARTS = [(OFF_MLA, MLA_COLS, 0, KT // 2), (OFF_MLA, MLA_COLS, KT // 2, KT // 2),
             (OFF_SB, 256, 0, KT), (OFF_SB + 256, 256, 0, KT), (OFF_SB + 512, 256, 0, KT),
             (OFF_MOBA, 256, 0, KT), (OFF_MOBA + 256, 256, 0, KT),
             (OFF_SWA, 256, 0, KT), (OFF_SWA + 256, 256, 0, KT), (OFF_MOBA + 512, 256, 0, KT)]
WO_ROWS = [(0, 2), (2, 2), (6, 1), (7, 1), (4, 2)]
GATE_ROWS = [(0, 1), (1, 2), (3, 1), (4, 2), (6, 2)]
U_WO = len(WIN_PARTS)
U_FFN = U_WO + len(WO_ROWS)
STEPS = FT // 2
LOOP_FROM = 3
LOOPS = (STEPS - LOOP_FROM) // 2
U_LOOP = U_FFN + 2 + 3 * (LOOP_FROM - 1)
U_AFTER = U_LOOP + 6 * LOOPS
U_PROJ = U_AFTER
U_DOWN = U_PROJ + 1
U_GATE = U_DOWN + 1
UNITS = U_GATE + len(GATE_ROWS)
assert UNITS % RING == 0 and LOOPS * 2 + LOOP_FROM == STEPS
MAGIC = 1.5 * 2.0 ** 23
TWO_PI = [6.28125, 0.0019353071693331003, 1.0253691153482577e-11]
ROOT_GUESS = float(0x5F3759DF - 0x00400000)
SLOT = 2048
COLS = ([n * w for _, w, _, n in WIN_PARTS] + [n * D for _, n in WO_ROWS]
        + [SLOT] * (U_GATE - U_FFN) + [n * D for _, n in GATE_ROWS])
assert len(COLS) == UNITS and max(COLS) == SLOT


def unit_gate(s):
    return U_FFN + 3 * s - (1 if s else 0)


_at = [0]


def _cols(n):
    _at[0] += n
    return _at[0] - n


ST_X = _cols(10)
ST_L = _cols(12)
ST_PE = _cols(2)
ST_M = _cols(48)
ST_B = _cols(48)
ST_S = _cols(36)
RS_MLA, RS_MOBA, RS_SWA = _cols(8), _cols(8), _cols(8)
MX = _cols(8)
NB = _cols(8)
SNK = _cols(8)
DENS = [_cols(8) for _ in range(3)]
RDEN = _cols(8)
ST_G = _cols(24)
ST_ALL = _at[0]

GROUP_ORDER = [SB, MLA, MOBA, SWA]

FLOW = """x_squared hn_ready xT_ready xT_high xT_low
pr_ready squared squares_read lat_done lat_T cT_ready mla_up mla_up_ready
v_ready mla_qk mla_T mT_ready conv_T conv_ready
moba_qk moba_T mobaT_ready swa_qk swa_T swaT_ready
sbT_ready scores_ready half_scores half_z softmax_bias sink_arg sink_exp probs_ready probs_T
pt_ready pv_ready group_out group_sq group_done
sb_z sb_abs sb_exp sb_log sb_soft sb_minus sb_probs groups_T mT_high mT_low
wo_done x_mid tap2 tap1 conv_done silu prod g_high g_low
p_T pT_high pT_low down_done x_low gate_ready sigmoid ple_term
dve_step arrived""".split()


PAIRED = (0, 2, 1, 3)
GROUPED = (0, 1, 2, 3)


def build(nc, x_in, p_in, positions, w_in, w_uq, w_ukv, norm_gains, small_gains, w_o, w_up,
          conv_rows, w_down, ple_proj, ple_gate, out):
    with ExitStack() as ctx:
        def sb(name, shape, dt=F32):
            return ctx.enter_context(nc.sbuf_tensor(name, shape, dt))

        def sem(name):
            return ctx.enter_context(nc.semaphore(name))

        raw = sb("raw", [P, RING, SLOT])
        wh = sb("wh", [P, RING, SLOT], F32R)
        wl = sb("wl", [P, RING, SLOT], F32R)
        x = sb("x", [P, TT, D])
        hn = sb("hn", [P, TT, D])
        hT_h = sb("hT_h", [P, KT, SEQ], F32R)
        hT_l = sb("hT_l", [P, KT, SEQ], F32R)
        gT_h = sb("gT_h", [P, 2, 2, SEQ], F32R)
        gT_l = sb("gT_l", [P, 2, 2, SEQ], F32R)
        pT_h = sb("pT_h", [P, 2, SEQ], F32R)
        pT_l = sb("pT_l", [P, 2, SEQ], F32R)
        ng = sb("ng", [P, 3 * D])
        sg = sb("sg", [P, S_ALL])
        uq = sb("uq", [P, 2, H * QK])
        ukv = sb("ukv", [P, H * 2 * HD])
        p_sb = sb("p_sb", [P, TT, PLE])
        conv = sb("conv", [P, 4, 2 * FT])
        ident = sb("ident", [P, P])
        ident_b = sb("ident_b", [P, P], BF16)
        causal = sb("causal", [P, P], BF16)
        above = sb("above", [P, P], BF16)
        neg_tri = sb("neg_tri", [P, P])
        neg_ones = sb("neg_ones", [P, P])
        inv_freq = sb("inv_freq", [P, HD // 2])
        pos_i = sb("pos_i", [P, TT], I32)
        pos_f = sb("pos_f", [P, TT])
        rope_c = sb("rope_c", [P, TT, HD])
        rope_s = sb("rope_s", [P, TT, HD])
        rope_c32 = sb("rope_c32", [P, TT, PE_DIM])
        rope_s32 = sb("rope_s32", [P, TT, PE_DIM])
        gc = sb("gc", [P, 4, TT, HD])
        gs = sb("gs", [P, 4, TT, HD])
        pr = sb("pr", [P, 2, TT, 512])
        rot = sb("rot", [P, TT, 512])
        lat = sb("lat", [P, 1536])
        kpe = sb("kpe", [P, TT, PE_DIM])
        tmp = sb("tmp", [P, 1024])
        mT = sb("mT", [P, 2, H, SEQ])
        qkT_moba = sb("qkT_moba", [P, 4, SEQ])
        qkT_swa = sb("qkT_swa", [P, 3, SEQ])
        qkT_sb = sb("qkT_sb", [P, 4, SEQ])
        v_moba = sb("v_moba", [P, TT, GW])
        v_swa = sb("v_swa", [P, TT, 2 * HD])
        v_sb = sb("v_sb", [P, TT, GW])
        pb = sb("pb", [P, 1536])
        pt = sb("pt", [P, 1536])
        st = sb("st", [P, ST_ALL])

        ps = ctx.enter_context(nc.psum_tensor("ps", [P, 8, 512], F32))

        mk = qkT_moba[:].rearrange("p k n -> p (k n)")[:, 0:TT * H * QK].rearrange(
            "p (t h n) -> p t h n", t=TT, h=H)
        mq = lat[:, 0:768].rearrange("p (t h n) -> p t h n", t=TT, h=H)
        cT = lat[:, 768:1536].rearrange("p (k n) -> p k n", k=3)
        mkv = pr[:, 0].rearrange("p t (h n) -> p t h n", h=H)
        sb_e, sb_sp = pb, pt
        cv = [pb[:, 0:1024].rearrange("p (a n) -> p a n", a=4),
              pt[:, 0:1024].rearrange("p (a n) -> p a n", a=4)]
        conv_raw = tmp[0:2 * FT, 0:512].rearrange("p (a n) -> p a n", a=4)
        tmp2 = tmp[:].rearrange("p (t n) -> p t n", t=TT)

        raw_landed = [sem(f"raw_landed{n}") for n in range(RING)]
        h_made = sem("h_made")
        l_made = sem("l_made")
        w_used = sem("w_used")
        x_landed = [sem(f"x_landed{t}") for t in range(TT)]
        pos_landed = sem("pos_landed")
        first_squares = sem("first_squares")
        gain_landed = sem("gain_landed")
        x_done = sem("x_done")
        ng_landed, sg_landed = sem("ng_landed"), sem("sg_landed")
        uq_landed, uq2_landed, ukv_landed = sem("uq_landed"), sem("uq2_landed"), sem("ukv_landed")
        p_landed, conv_landed = sem("p_landed"), sem("conv_landed")
        out_landed = sem("out_landed")
        column_0 = sem("column_0")
        consts_made = sem("consts_made")
        rope_step, rope_arg, rope_sin = sem("rope_step"), sem("rope_arg"), sem("rope_sin")
        released = sem("released")

        F = {name: sem(name) for name in FLOW}
        first = F[FLOW[0]].num
        assert [F[n].num for n in FLOW] == list(range(first, first + len(FLOW)))
        flow_range = range(first, first + len(FLOW))

        block = ctx.enter_context(nc.Block())

        def ge(eng, name, value):
            if not (isinstance(value, int) and value <= 0):
                eng.wait_ge(F[name], value)

        def quarter(i):
            half, t = divmod(i, 2)
            return t, slice(half * 512, (half + 1) * 512)

        def stat(a, n=1):
            return st[:, a:a + n]

        def per_head(ap, width):
            return ap.unsqueeze(2).broadcast_to([P, ap.shape[1], width])

        def unit_done(eng, layer, u, turn=0):
            eng.wait_ge(w_used, layer * UNITS + turn * 6 + (u + 1 + RING))

        @block.sync
        def _(sp):
            for t in range(TT):
                sp.dma_start(x[:, t, :], x_in[0, t * P:(t + 1) * P, :]).then_inc(x_landed[t], 16)
            with sp.Fori(0, DEPTH) as layer:
                def load(src, u, turn=0):
                    slot, k = u % RING, src.shape[1]
                    sp.wait_ge(l_made, layer * UNITS + turn * 6 + (u + 1))
                    if u == M_SB_Q:
                        sp.sem_inc(column_0, 1)
                    sp.dma_start(raw[:, slot, 0:COLS[u]].rearrange("p (k n) -> p k n", k=k),
                                 src).then_inc(raw_landed[slot], 16)

                def rows(w, k, n):
                    return w[layer][k * P:(k + n) * P, :].rearrange("(k p) n -> p k n", p=P)

                def load_up(s, half, u, turn=0):
                    w = w_up[layer].rearrange("(k p) n -> p k n", p=P)
                    load(w[:, :, bass.ds(s * 256 + half * DFF, 256)], u, turn)

                def load_down(s, u, turn=0):
                    load(w_down[layer][bass.ds(s * 256, 256), :].rearrange(
                        "(k p) n -> p k n", p=P), u, turn)

                for u, (c, w, k, n) in enumerate(WIN_PARTS):
                    load(rows(w_in, k, n)[:, :, c:c + w], u)
                for n, (k, m) in enumerate(WO_ROWS):
                    load(rows(w_o, k, m), U_WO + n)
                for s in range(LOOP_FROM):
                    for half in range(2):
                        load_up(s, half, unit_gate(s) + half)
                    if s:
                        load_down(s - 1, unit_gate(s) + 2)
                with sp.Fori(0, LOOPS) as turn:
                    for j in range(2):
                        u = unit_gate(LOOP_FROM + j)
                        for half in range(2):
                            load_up(turn * 2 + (LOOP_FROM + j), half, u + half, turn)
                        load_down(turn * 2 + (LOOP_FROM + j - 1), u + 2, turn)
                load(rows(ple_proj, 0, 2), U_PROJ)
                load_down(STEPS - 1, U_DOWN)
                for n, (k, m) in enumerate(GATE_ROWS):
                    load(rows(ple_gate, k, m), U_GATE + n)
            for i in range(4):
                t, c = quarter(i)
                sp.wait_ge(x_done, (DEPTH - 1) * 4 + i + 1)
                sp.dma_start(out[0, t * P:(t + 1) * P, c], x[:, t, c]).then_inc(out_landed, 16)
            sp.wait_ge(out_landed, 16 * 4)
            sp.wait_ge(gain_landed, 16 * (DEPTH + 1))

        @block.gpsimd
        def _(pool):
            pool.sem_inc(l_made, RING)
            for t, v in ((ident, 0.0), (causal, 0.0), (above, 0.0), (neg_tri, -1.0),
                         (neg_ones, -1.0)):
                pool.memset(t[:], v).then_inc(consts_made, 1)
            for j in range(HD // 2):
                last = pool.memset(inv_freq[:, j:j + 1], float(np.float32(ROPE_THETA ** (-2.0 * j / HD))))
            last.then_inc(consts_made, 1)
            pool.wait_ge(consts_made, 6)
            for t, op, fill, sign in ((ident, ALU.not_equal, 1.0, 1), (causal, ALU.is_ge, NEG, 1),
                                      (above, ALU.is_gt, NEG, -1), (neg_tri, ALU.is_ge, 0.0, 1)):
                pool.affine_select(out=t[:], in_=t[:], compare_op=op, fill=fill, base=0,
                                   pattern=[[-sign, P]], channel_multiplier=sign
                                   ).then_inc(consts_made, 1)
            pool.wait_ge(consts_made, 7)
            pool.tensor_copy(ident_b[:], ident[:]).then_inc(consts_made, 1)
            with pool.Fori(0, DEPTH) as layer:
                def low(u, turn=0):
                    slot, n = u % RING, COLS[u]
                    pool.wait_ge(h_made, layer * UNITS + turn * 6 + (u + 1 + RING))
                    pool.wait_ge(w_used, layer * UNITS + turn * 6 + (u + 1))
                    pool.tensor_tensor(wl[:, slot, 0:n], raw[:, slot, 0:n],
                                       wh[:, slot, 0:n].bitcast(F32), ALU.subtract
                                       ).then_inc(l_made, 1)

                for u in range(U_LOOP):
                    low(u)
                with pool.Fori(0, LOOPS) as turn:
                    for u in range(U_LOOP, U_LOOP + 6):
                        low(u, turn)
                for u in range(U_AFTER, UNITS):
                    low(u)

        @block.scalar
        def _(act):
            act.sem_inc(h_made, RING)
            act.dma_start(pos_i[:], positions.rearrange("a (t p) -> p (a t)", p=P),
                          allow_slow_non_contiguous=True).then_inc(pos_landed, 16)
            act.dma_start(ng[:, 0:D], norm_gains[DEPTH - 1, 0:D].partition_broadcast(P)
                          ).then_inc(gain_landed, 16)

            def x_square(i):
                t, c = quarter(i)
                return act.activation(hn[:, t, c], x[:, t, c], ACT.Square,
                                      accum_out=stat(ST_X + i))

            for i in (0, 2):
                act.wait_ge(x_landed[0], 16)
                x_square(i).then_inc(first_squares, 1)
            act.wait_ge(rope_arg, 1)
            for table, a in ((rope_s[:, :, 32:64], 0), (rope_c[:, :, 0:32], 64)):
                act.activation(table, tmp[:, a:a + 64].rearrange("p (t n) -> p t n", t=TT),
                               ACT.Sin).then_inc(rope_sin, 1)
            for i in (1, 3):
                act.wait_ge(x_landed[1], 16)
                x_square(i).then_inc(first_squares, 1)
            act.wait_ge(first_squares, 4)
            act.sem_inc(released, 1)

            with act.Fori(0, DEPTH) as layer:
                def high(u, turn=0):
                    slot, n = u % RING, COLS[u]
                    act.wait_ge(raw_landed[slot],
                                (layer * (UNITS // RING) + turn * (6 // RING) + (u // RING + 1)) * 16)
                    act.wait_ge(w_used, layer * UNITS + turn * 6 + (u + 1))
                    act.activation(wh[:, slot, 0:n], raw[:, slot, 0:n], ACT.Copy
                                   ).then_inc(h_made, 1)

                def x_high(n, bank):
                    for k in range(4):
                        half, t = divmod(k, 2)
                        act.wait_ge(F["xT_ready"], n + k + 1)
                        act.activation(hT_h[:, 4 * half:4 * half + 4, t * P:(t + 1) * P],
                                       ps[:, bank + k, :].rearrange("p (k n) -> p k n", k=4),
                                       ACT.Copy).then_inc(F["xT_high"], 1)

                def copied(dst, src, ready, n, done, **kw):
                    if ready == "unit":
                        unit_done(act, layer, n)
                    else:
                        act.wait_ge(F[ready], n)
                    act.activation(dst, src, ACT.Copy, **kw).then_inc(F[done], 1)

                def exps(g, rs, den, order=PAIRED):
                    act.wait_ge(F["softmax_bias"], g + 1)
                    if g:
                        act.wait_ge(F["probs_T"], 3 * g)
                    else:
                        act.wait_ge(F["pv_ready"], 1)
                    for h in range(H):
                        act.activation(pb[:, h * P:(h + 1) * P], ps[:, 4, h * P:(h + 1) * P],
                                       ACT.Exp, bias=stat(NB + h), scale=stat(rs + h),
                                       accum_out=stat(den + h)).then_inc(F["probs_ready"], 1)
                    for i, h in enumerate(order):
                        act.activation(pb[:, 512 + i * 256:768 + i * 256],
                                       ps[:, 5 + i // 2, (i % 2) * 256:(i % 2) * 256 + 256],
                                       ACT.Exp, bias=stat(NB + H + h), scale=stat(rs + H + h),
                                       accum_out=stat(den + H + h)).then_inc(F["probs_ready"], 1)

                def group_squares(n):
                    c = GROUP_ORDER[n] * GW
                    act.wait_ge(F["group_out"], n + 1)
                    for t in range(TT):
                        act.activation(junk(t), hn[:, t, c:c + GW], ACT.Square,
                                       accum_out=stat(ST_G + 6 * n + t)
                                       ).then_inc(F["group_sq"], 1)

                def junk(t):
                    return lat[:, 768 + t * GW:768 + (t + 1) * GW]

                def group_high(n):
                    g = GROUP_ORDER[n]
                    copied(hT_h[:, 2 * g:2 * g + 2, :],
                           ps[:, 7, :].rearrange("p (k n) -> p k n", k=2),
                           "groups_T", n + 1, "mT_high")

                high(0)
                act.dma_start(sg[:], small_gains[layer].partition_broadcast(P)
                              ).then_inc(sg_landed, 16)
                act.dma_start(uq[:, 0, :], w_uq[layer][0:P, :]).then_inc(uq_landed, 16)
                act.dma_start(uq[0:QR - P, 1, :], w_uq[layer][P:QR, :]).then_inc(uq2_landed, 16)
                act.dma_start(ukv[:], w_ukv[layer]).then_inc(ukv_landed, 16)
                act.wait_ge(rope_sin, 2)
                act.dma_start(conv_raw, conv_rows[layer]).then_inc(conv_landed, 16)
                act.dma_start(p_sb[:], p_in[layer, 0].rearrange("(t p) n -> p t n", p=P)
                              ).then_inc(p_landed, 16)
                x_high(0, 4)
                high(1)
                high(2)
                act.dma_start(ng[:, D:3 * D], norm_gains[layer, D:3 * D].partition_broadcast(P)
                              ).then_inc(ng_landed, 16)
                act.wait_ge(F["hn_ready"], 4)
                act.dma_start(ng[:, 0:D], norm_gains[layer, 0:D].partition_broadcast(P)
                              ).then_inc(gain_landed, 16)

                high(3)
                for t in range(TT):
                    copied(pr[:, 0, t, 0:MLA_COLS], ps[:, t, 0:MLA_COLS], "unit", M_MLA_B,
                           "pr_ready")
                for t in range(TT):
                    act.wait_ge(F["pr_ready"], t + 1)
                    act.activation(rot[:, t, 0:MLA_COLS], pr[:, 0, t, 0:MLA_COLS], ACT.Square
                                   ).then_inc(F["squared"], 1)
                high(4)
                copied(qkT_sb[:, 0:2, :], ps[:, 2, :].rearrange("p (k n) -> p k n", k=2),
                       "unit", M_SB_Q, "sbT_ready", scale=HD ** -0.5)
                high(5)
                for t in range(TT):
                    copied(cT[:, :, t * P:(t + 1) * P],
                           ps[:, 4 + t, 0:384].rearrange("p (k n) -> p k n", k=3),
                           "lat_T", 1 + t, "cT_ready")
                copied(qkT_sb[:, 2:4, :], ps[:, 3, :].rearrange("p (k n) -> p k n", k=2),
                       "unit", M_SB_K, "sbT_ready")
                high(6)
                for t in range(TT):
                    copied(mq[:, t].rearrange("p h n -> p (h n)"), ps[:, 4 + 2 * t, 0:H * QK],
                           "mla_up", 1 + t, "mla_up_ready")
                    copied(pr[:, 0, t, :], ps[:, 5 + 2 * t, :], "lat_T", 2, "mla_up_ready")
                act.wait_ge(F["mla_up_ready"], 4)
                act.wait_ge(F["squares_read"], 1)
                act.activation(rot[:, :, 0:H * QK], mq.rearrange("p t h n -> p t (h n)"),
                               ACT.Square).then_inc(F["squared"], 1)
                act.wait_ge(F["conv_T"], 1)
                act.wait_ge(F["lat_done"], 2)
                for t in range(TT):
                    act.activation(
                        tmp[:, t * 256:(t + 1) * 256].rearrange("p (h n) -> p h n", h=H),
                        mkv[:, t, :, 0:NOPE], ACT.Square).then_inc(F["squared"], 1)
                for t in range(TT):
                    copied(v_sb[:, t, :], ps[:, t, 0:256], "unit", M_SB_V, "v_ready")
                high(7)
                high(8)
                for b in range(3):
                    c = slice(b * 512, (b + 1) * 512)
                    act.wait_ge(F["sb_z"], b + 1)
                    act.activation(sb_e[:, c], ps[:, 4 + b, :], ACT.Abs).then_inc(F["sb_abs"], 1)
                for b in range(3):
                    c = slice(b * 512, (b + 1) * 512)
                    act.wait_ge(F["sb_abs"], b + 1)
                    act.activation(sb_e[:, c], sb_e[:, c], ACT.Exp, scale=-1.0
                                   ).then_inc(F["sb_exp"], 1)
                for b in range(3):
                    c = slice(b * 512, (b + 1) * 512)
                    act.wait_ge(F["sb_exp"], b + 1)
                    act.activation(sb_e[:, c], sb_e[:, c], ACT.Ln, bias=1.0
                                   ).then_inc(F["sb_log"], 1)
                for t in range(TT):
                    copied(pr[:, 1, t, :], ps[:, 2 + t, :], "unit", M_MOBA_K, "pr_ready")
                act.wait_ge(F["pr_ready"], 4)
                act.wait_ge(F["squares_read"], 2)
                act.activation(rot[:], pr[:, 1], ACT.Square).then_inc(F["squared"], 1)
                high(9)
                for t in range(TT):
                    if t == 1:
                        high(10)
                    for a in range(2):
                        copied(mT[0:QK, a, :, t * P:(t + 1) * P],
                               ps[0:QK, a, :].rearrange("p (k n) -> p k n", k=H),
                               "mla_T", 1 + t, "mT_ready")
                for b in range(3):
                    c = slice(b * 512, (b + 1) * 512)
                    act.wait_ge(F["sb_minus"], b + 1)
                    act.activation(sb_e[:, c], ps[:, 4 + b, :], ACT.Exp
                                   ).then_inc(F["sb_probs"], 1)
                act.wait_ge(F["moba_qk"], 1)
                for t in range(TT):
                    copied(pr[:, 1, t, 0:384], ps[:, 2 + t, 0:384], "unit", M_SWA_KV,
                           "pr_ready")
                    act.activation(v_swa[:, t, :], ps[:, 2 + t, 384:512], ACT.Copy
                                   ).then_inc(F["v_ready"], 1)
                act.wait_ge(F["pr_ready"], 6)
                act.activation(tmp2[:, :, 0:384], pr[:, 1, :, 0:384], ACT.Square
                               ).then_inc(F["squared"], 1)
                high(11)
                group_squares(0)
                for t in range(TT):
                    copied(qkT_moba[:, :, t * P:(t + 1) * P],
                           ps[:, t, :].rearrange("p (k n) -> p k n", k=4),
                           "moba_T", 1 + t, "mobaT_ready")
                exps(0, RS_MLA, DENS[0])
                for t in range(TT):
                    copied(v_moba[:, t, :], ps[:, 2 + t, 0:256], "unit", M_MOBA_V, "v_ready")
                high(12)
                group_high(0)
                for t in range(TT):
                    copied(qkT_swa[:, :, t * P:(t + 1) * P],
                           ps[:, 2 + t, 0:384].rearrange("p (k n) -> p k n", k=3),
                           "swa_T", 1 + t, "swaT_ready")
                group_squares(1)
                exps(1, RS_MOBA, DENS[1])
                group_high(1)
                high(13)
                group_squares(2)
                act.wait_ge(F["sink_arg"], 1)
                act.activation(stat(SNK, 8), stat(SNK, 8), ACT.Exp).then_inc(F["sink_exp"], 1)
                exps(2, RS_SWA, DENS[2], GROUPED)
                group_high(2)
                high(14)
                high(15)
                group_squares(3)
                high(16)
                group_high(3)
                act.wait_ge(F["p_T"], 1)
                act.activation(pT_h[:], ps[:, 4, :].rearrange("p (k n) -> p k n", k=2), ACT.Copy
                               ).then_inc(F["pT_high"], 1)

                act.wait_ge(F["groups_T"], 4)
                for i in range(4):
                    act.wait_ge(F["x_mid"], i + 1)
                    x_square(i).then_inc(F["x_squared"], 1)
                x_high(4, 4)

                def mlp(s, par, this, u, turn=0):
                    bank = 4 + 2 * par
                    high(u, turn)
                    high(u + 1, turn)
                    ge(act, "g_low", s - 1)
                    for half in range(2):
                        unit_done(act, layer, this + half, turn)
                        for j in range(2):
                            f = bass.ds(s * 2 + (half * FT + j), 1)
                            act.activation(cv[par][:, 2 * half + j, :],
                                           ps[:, bank + half, j * 256:(j + 1) * 256],
                                           ACT.Identity, bias=conv[:, 3, f],
                                           scale=conv[:, 2, f]).then_inc(F["tap2"], 1)
                    act.wait_ge(F["conv_done"], s * 4 + 2)
                    act.activation(cv[par][:, 0:2, :], cv[par][:, 0:2, :], ACT.Silu
                                   ).then_inc(F["silu"], 1)
                    act.wait_ge(F["prod"], s + 1)
                    if not (isinstance(s, int) and s < 2):
                        unit_done(act, layer, this - 1, turn)
                    act.activation(gT_h[:, par], cv[par][:, 0:2, :], ACT.Copy
                                   ).then_inc(F["g_high"], 1)
                    high(u + 2, turn)

                act.wait_ge(F["conv_ready"], 1)
                for s in range(LOOP_FROM):
                    mlp(s, s % 2, unit_gate(s), unit_gate(s + 1))
                with act.Fori(0, LOOPS) as turn:
                    for j in range(2):
                        s = LOOP_FROM + j
                        mlp(turn * 2 + s, s % 2, unit_gate(s), unit_gate(s + 1), turn)

                high(U_GATE + 1)
                x_high(8, 0)
                for n in range(2, len(GATE_ROWS)):
                    high(U_GATE + n)
                for b in range(4):
                    t, c = quarter(b)
                    if b < 3:
                        act.wait_ge(F["gate_ready"], b + 1)
                    else:
                        unit_done(act, layer, UNITS - 1)
                    act.activation(hn[:, t, c], ps[:, b, :], ACT.Sigmoid
                                   ).then_inc(F["sigmoid"], 1)
                for i in range(4):
                    act.wait_ge(x_done, layer * 4 + (i + 1))
                    x_square(i).then_inc(F["x_squared"], 1)
                act.wait_ge(F["x_squared"], 8)
                act.drain()
                act.wait_ge(F["arrived"], 2)
                act.sem_clear(flow_range)
                act.sem_inc(released, 1)

        @block.tensor
        def _(pe):
            pe.sem_inc(w_used, RING)
            pe.wait_ge(consts_made, 11)
            with pe.Fori(0, DEPTH) as layer:
                def unit(u, turn=0):
                    pe.wait_ge(l_made, layer * UNITS + turn * 6 + (u + 1 + RING))
                    return u % RING

                def split_product(dst, a_h, a_l, b_h, b_l, start, stop, last=False):
                    pe.matmul(dst, a_h, b_h, start=start, stop=False, skip_group_check=True)
                    pe.matmul(dst, a_h, b_l, start=False, stop=False, skip_group_check=True)
                    return pe.matmul(dst, a_l, b_h, start=False, stop=stop,
                                     skip_group_check=True)

                def project(u, banks, col, quarters=None):
                    slot, (_, w, k0, n) = unit(u), WIN_PARTS[u]
                    for t in range(TT):
                        tok = slice(t * P, (t + 1) * P)
                        if quarters is not None:
                            pe.wait_ge(F["xT_low"], quarters + t + 1)
                        for i in range(n):
                            k, c = k0 + i, slice(i * w, (i + 1) * w)
                            mm = split_product(ps[:, banks[t], col:col + w],
                                               hT_h[:, k, tok], hT_l[:, k, tok],
                                               wh[:, slot, c], wl[:, slot, c],
                                               k == 0, k == KT - 1)
                    mm.then_inc(w_used, 1)

                def project_T(u, bank):
                    slot = unit(u)
                    for j in range(2):
                        for k in range(KT):
                            c = slice(k * 256 + j * P, k * 256 + (j + 1) * P)
                            mm = split_product(ps[:, bank, j * 256:(j + 1) * 256],
                                               wh[:, slot, c], wl[:, slot, c],
                                               hT_h[:, k, :], hT_l[:, k, :],
                                               k == 0, k == KT - 1)
                    mm.then_inc(w_used, 1)

                def x_T(src, bank, ready):
                    for k in range(4):
                        half, t = divmod(k, 2)
                        pe.wait_ge(F[ready[0]], ready[1] + k + 1)
                        for j in range(4):
                            c = (4 * half + j) * P
                            mm = pe.transpose(ps[:, bank + k, j * P:(j + 1) * P],
                                              src[:, t, c:c + P], ident[:])
                        mm.then_inc(F["xT_ready"], 1)

                def wide(u, n, k0, act_h, act_l, first, last, banks=0, name=None, turn=0,
                         split=None):
                    slot = unit(u, turn)
                    for b in range(4):
                        half, t = divmod(b, 2)
                        tok = slice(t * P, (t + 1) * P)
                        if split is not None:
                            pe.wait_ge(F["xT_low"], split + max(b + 1, 2))
                        for k in range(n):
                            c = slice(k * D + half * 512, k * D + half * 512 + 512)
                            mm = split_product(ps[:, banks + b, :],
                                               act_h[:, k0 + k, tok], act_l[:, k0 + k, tok],
                                               wh[:, slot, c], wl[:, slot, c],
                                               first and k == 0, last and k == n - 1)
                        if b < 3 and name:
                            mm.then_inc(F[name], 1)
                    mm.then_inc(w_used, 1)

                def scores(g, q, k, prev_mask, order=PAIRED):
                    def tile_0(heads):
                        for h in heads:
                            o = ps[:, 4, h * P:(h + 1) * P]
                            pe.matmul(o, q(h)[:, 0:P], k(h)[:, 0:P], start=(h == 0), stop=False,
                                      skip_group_check=True)
                            mm = pe.matmul(o, ident_b[:], causal[:], start=False, stop=True,
                                           skip_group_check=True)
                        return mm

                    tile_0(order[0:2]).then_inc(F["half_scores"], 1)
                    for i, h in enumerate(order):
                        c = (i % 2) * 256
                        o = ps[:, 5 + i // 2, c:c + 256]
                        pe.matmul(o, q(h)[:, P:SEQ], k(h)[:, 0:SEQ], start=(i % 2 == 0),
                                  stop=False, skip_group_check=True)
                        if prev_mask is not None:
                            pe.matmul(o[:, 0:P], ident_b[:], prev_mask[:], start=False,
                                      stop=True, skip_group_check=True)
                        pe.matmul(o[:, P:256], ident_b[:], causal[:], start=False,
                                  stop=True, skip_group_check=True)
                    pe.wait_ge(F["half_scores"], g + 1)
                    tile_0(order[2:4]).then_inc(F["scores_ready"], 1)

                def probs_T(g):
                    for h in range(H):
                        if h == 0:
                            pe.wait_ge(F["probs_ready"], 8 * g + 4)
                        mm = pe.transpose(ps[:, 4, h * P:(h + 1) * P], pb[:, h * P:(h + 1) * P],
                                          ident[:])
                    mm.then_inc(F["probs_T"], 1)
                    for b in range(2):
                        pe.wait_ge(F["probs_ready"], 8 * g + 6 + 2 * b)
                        for j in range(4):
                            c = 512 + b * 512 + j * P
                            mm = pe.transpose(ps[:, 5 + b, j * P:(j + 1) * P], pb[:, c:c + P],
                                              ident[:])
                        mm.then_inc(F["probs_T"], 1)

                def pv(g, v, bank, order=PAIRED):
                    pe.wait_ge(F["pt_ready"], 3 * g + 3)
                    for h in range(H):
                        pe.matmul(ps[:, bank, h * HD:(h + 1) * HD], pt[:, h * P:(h + 1) * P],
                                  v(h, 0), start=True, stop=True, skip_group_check=True)
                    for h in range(H):
                        for k in range(TT):
                            c = 512 + order.index(h) * 256 + k * P
                            mm = pe.matmul(ps[:, bank, 256 + h * HD:256 + (h + 1) * HD],
                                           pt[:, c:c + P], v(h, k), start=(k == 0),
                                           stop=(k == TT - 1), skip_group_check=True)
                    mm.then_inc(F["pv_ready"], 1)

                def head(qkT, pair, h):
                    return qkT[(h % 2) * HD:(h % 2) * HD + HD, pair + h // 2, :]

                x_T(hn, 4, ("hn_ready", 0))
                project(M_MLA_A, (0, 1), 0, quarters=0)
                pe.wait_ge(conv_landed, layer * 16 + 16)
                project(M_MLA_B, (0, 1), 0, quarters=2)
                for a in range(4):
                    mm = pe.transpose(ps[:, 7, a * 44:a * 44 + 44], conv_raw[:, a, :],
                                      ident[0:2 * FT, 0:2 * FT])
                mm.then_inc(F["conv_T"], 1)
                project_T(M_SB_Q, 2)
                for t in range(TT):
                    pe.wait_ge(F["lat_done"], t + 1)
                    for n, (c, w) in enumerate(((0, P), (P, QR - P), (QR, KVR))):
                        mm = pe.transpose(ps[0:w, 4 + t, n * P:(n + 1) * P], pr[:, 0, t, c:c + w],
                                          ident[:])
                    mm.then_inc(F["lat_T"], 1)
                project_T(M_SB_K, 3)
                pe.wait_ge(uq_landed, layer * 16 + 16)
                pe.wait_ge(uq2_landed, layer * 16 + 16)
                pe.wait_ge(ukv_landed, layer * 16 + 16)
                pe.wait_ge(F["cT_ready"], 2)
                pe.wait_ge(F["conv_ready"], 1)
                for t in range(TT):
                    tok = slice(t * P, (t + 1) * P)
                    o = ps[:, 4 + 2 * t, 0:H * QK]
                    pe.matmul(o, cT[:, 0, tok], uq[:, 0, :], start=True, stop=False)
                    pe.matmul(o, cT[0:QR - P, 1, tok], uq[0:QR - P, 1, :], start=False, stop=True)
                    pe.matmul(ps[:, 5 + 2 * t, :], cT[:, 2, tok], ukv[:], start=True, stop=True
                              ).then_inc(F["mla_up"], 1)
                pe.wait_ge(F["pr_ready"], 2)
                project(M_SB_V, (0, 1), 0)
                pe.wait_ge(F["sbT_ready"], 2)
                project(M_MOBA_Q, (2, 3), 0)
                pe.wait_ge(F["mla_up_ready"], 4)
                for b in range(2):
                    for j in range(2):
                        h = PAIRED[2 * b + j]
                        o = ps[:, 4 + b, j * 256:(j + 1) * 256]
                        pe.matmul(o, head(qkT_sb, 2, h)[:, 0:P], head(qkT_sb, 0, h),
                                  start=(j == 0), stop=False, skip_group_check=True)
                        mm = pe.matmul(o[:, 0:P], ident_b[:], above[:], start=False, stop=True,
                                       skip_group_check=True)
                    mm.then_inc(F["sb_z"], 1)
                for i, h in enumerate(PAIRED):
                    o = ps[:, 6, h * P:(h + 1) * P]
                    if i == 2:
                        pe.wait_ge(F["half_z"], 1)
                    pe.matmul(o, head(qkT_sb, 2, h)[:, P:SEQ], head(qkT_sb, 0, h)[:, P:SEQ],
                              start=(i == 0), stop=False, skip_group_check=True)
                    mm = pe.matmul(o, ident_b[:], above[:], start=False, stop=True,
                                   skip_group_check=True)
                    if i == 1:
                        mm.then_inc(F["half_z"], 1)
                mm.then_inc(F["sb_z"], 1)
                project(M_MOBA_K, (2, 3), 256)

                def mla_T(t):
                    for a, src in ((0, mq), (1, mk)):
                        for h in range(H):
                            mm = pe.transpose(ps[0:QK, a, h * P:(h + 1) * P], src[:, t, h, :],
                                              ident[:])
                    mm.then_inc(F["mla_T"], 1)

                pe.wait_ge(F["v_ready"], 2)
                pe.wait_ge(F["mla_qk"], 2)
                mla_T(0)
                pe.wait_ge(F["pr_ready"], 4)
                project(M_SWA_Q, (2, 3), 0)
                pe.wait_ge(F["mT_ready"], 2)
                mla_T(1)
                pe.wait_ge(F["sb_soft"], 3)
                for b in range(2):
                    for j in range(2):
                        i = 2 * b + j
                        h = PAIRED[i]
                        o = ps[:, 4 + b, j * 256:(j + 1) * 256]
                        pe.matmul(o, neg_tri[:], sb_sp[:, i * 256:(i + 1) * 256], start=False,
                                  stop=False, skip_group_check=True)
                        mm = pe.matmul(o[:, P:256], neg_ones[:],
                                       sb_sp[:, 1024 + h * P:1024 + (h + 1) * P], start=False,
                                       stop=True, skip_group_check=True)
                    mm.then_inc(F["sb_minus"], 1)
                pe.matmul(ps[:, 6, :], neg_tri[:], sb_sp[:, 1024:1536], start=False, stop=True,
                          skip_group_check=True).then_inc(F["sb_minus"], 1)
                project(M_SWA_KV, (2, 3), 256)
                pe.wait_ge(F["sb_probs"], 3)
                for t in range(TT):
                    for h in range(H):
                        o = ps[:, 7, t * 256 + h * HD:t * 256 + (h + 1) * HD]
                        c = PAIRED.index(h) * 256 + t * P
                        mm = pe.matmul(o, sb_e[:, c:c + P], v_sb[:, 0, h * HD:(h + 1) * HD],
                                       start=True, stop=(t == 0), skip_group_check=True)
                        if t == 1:
                            mm = pe.matmul(o, sb_e[:, 1024 + h * P:1024 + (h + 1) * P],
                                           v_sb[:, 1, h * HD:(h + 1) * HD], start=False,
                                           stop=True, skip_group_check=True)
                mm.then_inc(F["pv_ready"], 1)

                def group_T(n):
                    g = GROUP_ORDER[n]
                    pe.wait_ge(F["group_done"], n + 1)
                    for k in range(2):
                        for t in range(TT):
                            mm = pe.transpose(
                                ps[:, 7, k * 256 + t * P:k * 256 + (t + 1) * P],
                                hn[:, t, g * GW + k * P:g * GW + (k + 1) * P], ident[:])
                    mm.then_inc(F["groups_T"], 1)

                def project_out(n):
                    k, m = WO_ROWS[n]
                    last = n == len(WO_ROWS) - 1
                    wide(U_WO + n, m, k, hT_h, hT_l, n == 0, last,
                         name="wo_done" if last else None)

                pe.wait_ge(F["mT_ready"], 4)
                scores(0, lambda h: mT[0:QK, 0, h, :], lambda h: mT[0:QK, 1, h, :], None)
                pe.wait_ge(F["moba_qk"], 1)
                for t in range(TT):
                    for j in range(4):
                        mm = pe.transpose(ps[:, t, j * P:(j + 1) * P], rot[:, t, j * P:(j + 1) * P],
                                          ident[:])
                    mm.then_inc(F["moba_T"], 1)
                pe.wait_ge(F["pr_ready"], 6)
                pe.wait_ge(F["v_ready"], 4)
                project(M_MOBA_V, (2, 3), 0)
                group_T(0)
                probs_T(0)
                pe.wait_ge(F["v_ready"], 6)
                pe.wait_ge(F["swa_qk"], 1)
                for t in range(TT):
                    for j in range(3):
                        mm = pe.transpose(ps[:, 2 + t, j * P:(j + 1) * P],
                                          pr[:, 1, t, j * P:(j + 1) * P], ident[:])
                    mm.then_inc(F["swa_T"], 1)
                pe.wait_ge(F["mT_low"], 1)
                pv(0, lambda h, k: mkv[:, k, h, NOPE:], 7)
                pe.wait_ge(F["mobaT_ready"], 2)
                scores(1, lambda h: head(qkT_moba, 0, h), lambda h: head(qkT_moba, 2, h), None)
                pe.wait_ge(F["swaT_ready"], 2)
                project_out(0)
                group_T(1)
                probs_T(1)
                pe.wait_ge(F["mT_low"], 2)
                pv(1, lambda h, k: v_moba[:, k, h * HD:(h + 1) * HD], 7)
                scores(2, lambda h: qkT_swa[(h // 2) * HD:(h // 2) * HD + HD, h % 2, :],
                       lambda h: qkT_swa[(h // 2) * HD:(h // 2) * HD + HD, 2, :], above,
                       GROUPED)
                project_out(1)
                group_T(2)
                probs_T(2)
                pe.wait_ge(F["mT_low"], 3)
                project_out(2)
                pv(2, lambda h, k: v_swa[:, k, (h // 2) * HD:(h // 2 + 1) * HD], 7,
                   GROUPED)
                project_out(3)
                pe.wait_ge(p_landed, layer * 16 + 16)
                for k in range(2):
                    for t in range(TT):
                        mm = pe.transpose(ps[:, 4, k * 256 + t * P:k * 256 + (t + 1) * P],
                                          p_sb[:, t, k * P:(k + 1) * P], ident[:])
                mm.then_inc(F["p_T"], 1)
                group_T(3)
                pe.wait_ge(F["mT_low"], 4)
                project_out(4)

                pe.wait_ge(F["pT_low"], 1)
                x_T(hn, 4, ("hn_ready", 4))

                def up(s, par, u, turn=0, first=False):
                    for half in range(2):
                        slot = unit(u + half, turn)
                        if half == 0:
                            ge(pe, "conv_done", (s - 1) * 4)
                        for j in range(2):
                            for k in range(KT):
                                c = slice(k * 256 + j * P, k * 256 + (j + 1) * P)
                                if first and half == 0 and j == 0 and k % 4 == 0:
                                    pe.wait_ge(F["xT_low"], 6 + k // 2)
                                mm = split_product(
                                    ps[:, 4 + 2 * par + half, j * 256:(j + 1) * 256],
                                    wh[:, slot, c], wl[:, slot, c], hT_h[:, k, :], hT_l[:, k, :],
                                    k == 0, k == KT - 1)
                        mm.then_inc(w_used, 1)

                def down(s, par, u, first=False, last=False, turn=0):
                    pe.wait_ge(F["g_low"], s + 1)
                    if first:
                        pe.wait_ge(F["x_mid"], 4)
                    wide(u, 2, 0, gT_h[:, par], gT_l[:, par], first, last,
                         name="down_done" if last else None, turn=turn)

                up(0, 0, unit_gate(0), first=True)
                for s in range(1, LOOP_FROM):
                    up(s, s % 2, unit_gate(s))
                    down(s - 1, (s - 1) % 2, unit_gate(s) + 2, first=(s == 1))
                with pe.Fori(0, LOOPS) as turn:
                    for j in range(2):
                        s = LOOP_FROM + j
                        up(turn * 2 + s, s % 2, unit_gate(s), turn)
                        down(turn * 2 + (s - 1), (s - 1) % 2, unit_gate(s) + 2, turn=turn)
                pe.wait_ge(F["conv_done"], 4 * STEPS)
                wide(U_PROJ, 2, 0, pT_h, pT_l, True, True, banks=4)
                down(STEPS - 1, 0, U_DOWN, last=True)
                x_T(x, 0, ("x_low", 0))
                for n, (k, m) in enumerate(GATE_ROWS):
                    last = n == len(GATE_ROWS) - 1
                    wide(U_GATE + n, m, k, hT_h, hT_l, n == 0, last,
                         name="gate_ready" if last else None, split=8 if n == 0 else None)
                pe.drain().then_inc(F["arrived"], 1)
                pe.wait_ge(released, layer + 2)

        @block.vector
        def _(dve):
            tt, stt, ts = dve.tensor_tensor, dve.scalar_tensor_tensor, dve.tensor_scalar

            rope_steps = [0]

            def rope_chained(ins):
                rope_steps[0] += 1
                ins.then_inc(rope_step, 1)
                dve.wait_ge(rope_step, rope_steps[0])

            dve.wait_ge(pos_landed, 16)
            rope_chained(dve.tensor_copy(pos_f[:], pos_i[:]))
            dve.wait_ge(consts_made, 6)
            angle, turns = tmp[:, 128:192], tmp[:, 192:256]
            for t in range(TT):
                rope_chained(ts(angle[:, t * 32:(t + 1) * 32], inv_freq[:], pos_f[:, t:t + 1],
                                None, ALU.mult))
            rope_chained(ts(turns, angle, float(1.0 / (2.0 * np.pi)), MAGIC, ALU.mult, ALU.add))
            rope_chained(ts(turns, turns, -MAGIC, None, ALU.add))
            for part in TWO_PI:
                rope_chained(stt(angle, turns, -part, angle, ALU.mult, ALU.add))
            pi = 3.1415925
            rope_chained(ts(tmp[:, 0:64], angle, pi, -pi, ALU.min, ALU.max))
            rope_chained(ts(tmp[:, 64:128], tmp[:, 0:64], -1.0, None, ALU.mult))
            rope_chained(tt(tmp[:, 64:128], tmp[:, 64:128], tmp[:, 0:64], ALU.min))
            rope_chained(ts(tmp[:, 64:128], tmp[:, 64:128], float(np.pi / 2), None, ALU.add))
            dve.sem_inc(rope_arg, 1)
            dve.wait_ge(rope_sin, 2)
            rope_chained(dve.tensor_copy(rope_c[:, :, 32:64], rope_c[:, :, 0:32]))
            rope_chained(ts(rope_s[:, :, 0:32], rope_s[:, :, 32:64], -1.0, None, ALU.mult))
            for a in range(2):
                rope_chained(dve.tensor_copy(rope_c32[:, :, a * 16:(a + 1) * 16],
                                             rope_c[:, :, 0:32:2]))
                rope_chained(dve.tensor_copy(rope_s32[:, :, a * 16:(a + 1) * 16],
                                             rope_s[:, :, a * 32:(a + 1) * 32:2]))

            dve.wait_ge(released, 1)
            with dve.Fori(0, DEPTH) as layer:
                steps = [0]

                def chained(ins):
                    steps[0] += 1
                    ins.then_inc(F["dve_step"], 1)
                    dve.wait_ge(F["dve_step"], steps[0])

                def half_mean(a, n, width):
                    return ts(stat(a, n), stat(a, n), 0.5 / width, 0.5 * EPS, ALU.mult, ALU.add)

                def inverse_root(a, n):
                    y, r, half = stat(a + 2 * n, n), stat(a + n, n), stat(a, n)
                    chained(ts(y.bitcast(I32), half.bitcast(I32), 1, None,
                               ALU.logical_shift_right))
                    chained(ts(y.bitcast(I32), y.bitcast(I32), -1.0, ROOT_GUESS, ALU.mult,
                               ALU.add))
                    for _ in range(3):
                        chained(tt(r, half, y, ALU.mult))
                        chained(stt(r, r, -1.0, y, ALU.mult, ALU.mult))
                        chained(stt(y, r, 1.5, y, ALU.add, ALU.mult))

                def norm(n):
                    chained(tt(stat(ST_X + 4, TT), stat(ST_X, TT), stat(ST_X + 2, TT), ALU.add))
                    chained(half_mean(ST_X + 4, TT, D))
                    inverse_root(ST_X + 4, TT)
                    for i in range(4):
                        t, c = quarter(i)
                        g = ng[:, n * D + c.start:n * D + c.stop]
                        stt(hn[:, t, c], x[:, t, c], stat(ST_X + 8 + t), g, ALU.mult, ALU.mult
                            ).then_inc(F["hn_ready"], 1)

                def x_low(n, bank):
                    for k in range(4):
                        half, t = divmod(k, 2)
                        o = (slice(None), slice(4 * half, 4 * half + 4), slice(t * P, (t + 1) * P))
                        dve.wait_ge(F["xT_high"], n + k + 1)
                        tt(hT_l[o], ps[:, bank + k, :].rearrange("p (k n) -> p k n", k=4),
                           hT_h[o].bitcast(F32), ALU.subtract).then_inc(F["xT_low"], 1)

                def rotate(i_q, i_k, kh, name):
                    w = HD // 2
                    view = lambda ap, c, n: ap[:, :, c:c + n * HD].rearrange(
                        "p t (h n) -> p t h n", h=n)
                    for i, c, n in ((i_q, 0, H), (i_k, GW, kh)):
                        src, r, o = view(pr[:, 1], c, n), view(rot, c, n), view(tmp2, c, n)
                        shape = [P, TT, n, HD]
                        last = tt(r, src, gc[:, i].unsqueeze(2).broadcast_to(shape), ALU.mult)
                        half = [P, TT, n, w]
                        for a in range(2):
                            last = tt(o[:, :, :, a * w:(a + 1) * w],
                                      src[:, :, :, (1 - a) * w:(2 - a) * w],
                                      gs[:, i, :, a * w:(a + 1) * w].unsqueeze(2)
                                      .broadcast_to(half), ALU.mult)
                    chained(last)
                    if kh == H:
                        tt(rot[:], rot[:], tmp2, ALU.add).then_inc(F[name], 1)
                        return
                    for t in range(TT):
                        order = [ap[:, t, 0:GW].rearrange("p (a b n) -> p b a n", a=2, b=2)
                                 for ap in (rot, tmp2)]
                        tt(pr[:, 1, t, 0:GW].rearrange("p (b a n) -> p b a n", a=2, b=2),
                           *order, ALU.add)
                    n = slice(GW, GW + kh * HD)
                    tt(pr[:, 1, :, n], rot[:, :, n], tmp2[:, :, n], ALU.add
                       ).then_inc(F[name], 1)

                def squares_read(ins, k):
                    ins.then_inc(F["squares_read"], 1)
                    dve.wait_ge(F["squares_read"], k)

                def heads_norm(a, kh, squares, k, rs):
                    n = TT * (H + kh)
                    chained(dve.tensor_reduce(
                        stat(a, n),
                        squares[:, :, 0:(H + kh) * HD].rearrange("p t (h n) -> p t h n", n=HD),
                        AX.X, ALU.add))
                    squares_read(half_mean(a, n, HD), k)
                    inverse_root(a, n)
                    r = stat(a + 2 * n, n).rearrange("p (t h) -> p t h", t=TT)
                    ts(stat(rs, 8).rearrange("p (t h) -> p t h", t=TT), r[:, :, 0:H], HD ** -0.5,
                       None, ALU.mult)
                    k = pr[:, 1, :, GW:GW + kh * HD].rearrange("p t (h n) -> p t h n", h=kh)
                    chained(tt(k, k, r[:, :, H:H + kh].unsqueeze(3).broadcast_to([P, TT, kh, HD]),
                               ALU.mult))

                def row_max(g, rs, signal=True):
                    dve.wait_ge(F["scores_ready"], g + 1)
                    ge(dve, "probs_ready", 8 * g)
                    dve.tensor_reduce(stat(MX, H), ps[:, 4, :].rearrange("p (h n) -> p h n", h=H),
                                      AX.X, ALU.max)
                    heads = ("p (h b) -> p b h" if g < 2 else "p (b h) -> p b h")
                    chained(dve.tensor_reduce(
                        stat(MX + H, H).rearrange(heads, b=2),
                        ps[:, 5:7, :].rearrange("p b (h n) -> p b h n", h=2), AX.X, ALU.max))
                    if signal:
                        stt(stat(NB, 8), stat(MX, 8), -1.0, stat(rs, 8), ALU.mult, ALU.mult
                            ).then_inc(F["softmax_bias"], 1)

                def probs_out(g):
                    dve.wait_ge(F["pv_ready"], g + 1)
                    for b in range(3):
                        dve.wait_ge(F["probs_T"], 3 * g + b + 1)
                        dve.tensor_copy(pt[:, b * 512:(b + 1) * 512], ps[:, 4 + b, :]
                                        ).then_inc(F["pt_ready"], 1)

                def group_cols(ap, n):
                    c = GROUP_ORDER[n] * GW
                    return ap[:, :, c:c + GW]

                def out_heads(n):
                    return group_cols(hn, n).rearrange("p t (h n) -> p t h n", h=H)

                def divided(n, bank, den, pv_n):
                    dve.wait_ge(F["pv_ready"], pv_n)
                    chained(dve.reciprocal(stat(RDEN, 8), stat(den, 8)))
                    tt(out_heads(n), ps[:, bank, :].rearrange("p (t h n) -> p t h n", t=TT, h=H),
                       stat(RDEN, 8).rearrange("p (t h) -> p t h", t=TT).unsqueeze(3)
                       .broadcast_to([P, TT, H, HD]), ALU.mult).then_inc(F["group_out"], 1)

                def group_norm(n):
                    dve.wait_ge(F["group_sq"], TT * (n + 1))
                    chained(half_mean(ST_G + 6 * n, TT, GW))
                    inverse_root(ST_G + 6 * n, TT)
                    c = GROUP_ORDER[n] * GW
                    for t in range(TT):
                        last = stt(hn[:, t, c:c + GW], hn[:, t, c:c + GW],
                                   stat(ST_G + 6 * n + 4 + t),
                                   ng[:, G_GROUP + c:G_GROUP + c + GW], ALU.mult, ALU.mult)
                    last.then_inc(F["group_done"], 1)

                def group_low(n):
                    g = GROUP_ORDER[n]
                    dve.wait_ge(F["mT_high"], n + 1)
                    tt(hT_l[:, 2 * g:2 * g + 2, :], ps[:, 7, :].rearrange("p (k n) -> p k n", k=2),
                       hT_h[:, 2 * g:2 * g + 2, :].bitcast(F32), ALU.subtract
                       ).then_inc(F["mT_low"], 1)

                dve.wait_ge(gain_landed, layer * 16 + 16)
                norm(0)
                x_low(0, 4)
                dve.wait_ge(sg_landed, layer * 16 + 16)
                for i, c in enumerate((S_SWAQ, S_SWAK, S_MOBAQ, S_MOBAK)):
                    def gain(a, n):
                        return sg[:, a:a + n].unsqueeze(1).broadcast_to([P, TT, n])
                    tt(gc[:, i], rope_c[:], gain(c, HD), ALU.mult)
                    tt(gs[:, i, :, 0:32], rope_s[:, :, 0:32], gain(c + 32, 32), ALU.mult)
                    last = tt(gs[:, i, :, 32:64], rope_s[:, :, 32:64], gain(c, 32), ALU.mult)
                chained(last)
                dve.wait_ge(F["conv_T"], 1)
                dve.tensor_copy(conv[:], ps[:, 7, 0:176].rearrange("p (a n) -> p a n", a=4)
                                ).then_inc(F["conv_ready"], 1)

                dve.wait_ge(F["squared"], 2)
                for a, c, w in ((ST_L, 0, QR), (ST_L + 2, QR, KVR), (ST_PE, QR + KVR, PE_DIM)):
                    last = dve.tensor_reduce(stat(a, 2), rot[:, :, c:c + w], AX.X, ALU.add)
                chained(last)
                half_mean(ST_L, 2, QR)
                squares_read(half_mean(ST_L + 2, 2, KVR), 1)
                def rope32(o, src, scratch, shape):
                    full, half = [*shape, PE_DIM], [*shape, 16]

                    def table(a, c, w):
                        a = a[:, :, c:c + w]
                        return a if len(shape) == 2 else a.unsqueeze(2).broadcast_to([*shape, w])
                    one, two = scratch
                    tt(one, src, table(rope_c32, 0, PE_DIM), ALU.mult)
                    at = [slice(None)] * (len(shape))
                    for a in range(2):
                        last = tt(two[(*at, slice(a * 16, a * 16 + 16))],
                                  src[(*at, slice(16 - a * 16, 32 - a * 16))],
                                  table(rope_s32, a * 16, 16), ALU.mult)
                    chained(last)
                    return tt(o, one, two, ALU.add)

                kp = tmp[:, 512:576].rearrange("p (t n) -> p t n", t=TT)
                chained(tt(kp, pr[:, 0, :, QR + KVR:MLA_COLS],
                           sg[:, S_MLAK + NOPE:S_MLAK + QK].unsqueeze(1)
                           .broadcast_to([P, TT, PE_DIM]), ALU.mult))
                chained(rope32(kpe[:], kp, [tmp[:, 576 + 64 * a:640 + 64 * a].rearrange(
                    "p (t n) -> p t n", t=TT) for a in range(2)], [P, TT]))
                inverse_root(ST_L, 4)
                for t in range(TT):
                    for j, (c, w, g) in enumerate(((0, QR, S_QN), (QR, KVR, S_KVN))):
                        v = pr[:, 0, t, c:c + w]
                        last = stt(v, v, stat(ST_L + 8 + 2 * j + t), sg[:, g:g + w], ALU.mult,
                                   ALU.mult)
                    last.then_inc(F["lat_done"], 1)

                dve.wait_ge(F["squared"], 5)
                dve.tensor_reduce(stat(ST_M, 8),
                                  rot[:, :, 0:H * QK].rearrange("p t (h n) -> p t h n", n=QK),
                                  AX.X, ALU.add)
                chained(dve.tensor_reduce(
                    stat(ST_M + 8, 8), tmp[:, 0:512].rearrange("p (h n) -> p h n", n=NOPE),
                    AX.X, ALU.add))
                ssk = stat(ST_M + 8, 8).rearrange("p (t h) -> p t h", t=TT)
                chained(tt(ssk, ssk, stat(ST_PE, 2).unsqueeze(2).broadcast_to([P, TT, H]),
                           ALU.add))
                squares_read(half_mean(ST_M, 16, QK), 2)
                q8 = mq.rearrange("p t h n -> p (t h) n")
                chained(tt(q8, q8, sg[:, S_MLAQ:S_MLAQ + QK].unsqueeze(1)
                           .broadcast_to([P, 8, QK]), ALU.mult))
                qpe = mq[:, :, :, NOPE:QK]
                rope32(qpe, qpe, [tmp[:, 512 + 256 * a:768 + 256 * a].rearrange(
                    "p (t h n) -> p t h n", t=TT, h=H) for a in range(2)], [P, TT, H]
                    ).then_inc(F["mla_qk"], 1)
                inverse_root(ST_M, 16)
                ts(stat(RS_MLA, 8), stat(ST_M + 32, 8), QK ** -0.5, None, ALU.mult)
                rk = stat(ST_M + 40, 8).rearrange("p (t h) -> p t h", t=TT)
                chained(tt(mk[:, :, :, 0:NOPE], mkv[:, :, :, 0:NOPE],
                           rk.unsqueeze(3).broadcast_to([P, TT, H, NOPE]), ALU.mult))
                k8 = mk[:].rearrange("p t h n -> p (t h) n")[:, :, 0:NOPE]
                tt(k8, k8, sg[:, S_MLAK:S_MLAK + NOPE].unsqueeze(1).broadcast_to([P, 8, NOPE]),
                   ALU.mult)
                tt(mk[:, :, :, NOPE:QK], kpe[:].unsqueeze(2).broadcast_to([P, TT, H, PE_DIM]),
                   rk.unsqueeze(3).broadcast_to([P, TT, H, PE_DIM]), ALU.mult
                   ).then_inc(F["mla_qk"], 1)

                for b in range(3):
                    c = slice(b * 512, (b + 1) * 512)
                    dve.wait_ge(F["sb_log"], b + 1)
                    stt(sb_sp[:, c], ps[:, 4 + b, :], 0.0, sb_e[:, c], ALU.max, ALU.add
                        ).then_inc(F["sb_soft"], 1)

                dve.wait_ge(F["squared"], 6)
                heads_norm(ST_B, H, rot, 3, RS_MOBA)
                rotate(2, 3, H, "moba_qk")

                dve.wait_ge(F["pv_ready"], 1)
                dve.tensor_copy(group_cols(hn, 0),
                                ps[:, 7, :].rearrange("p (t n) -> p t n", t=TT)
                                ).then_inc(F["group_out"], 1)
                dve.wait_ge(F["squared"], 7)
                heads_norm(ST_S, 2, tmp2, 4, RS_SWA)
                row_max(0, RS_MLA)
                dve.wait_ge(ng_landed, layer * 16 + 16)
                group_norm(0)
                dve.wait_ge(F["moba_T"], 2)
                rotate(0, 1, 2, "swa_qk")
                probs_out(0)
                group_low(0)
                divided(1, 7, DENS[0], 2)
                row_max(1, RS_MOBA)
                group_norm(1)
                group_low(1)
                probs_out(1)
                divided(2, 7, DENS[1], 3)
                row_max(2, RS_SWA, signal=False)
                sinks = sg[:, S_SINK:S_SINK + H].unsqueeze(1).broadcast_to([P, TT, H])
                chained(tt(stat(MX, 8), stat(MX, 8), stat(RS_SWA, 8), ALU.mult))
                mx = stat(MX, 8).rearrange("p (t h) -> p t h", t=TT)
                chained(tt(mx, mx, sinks, ALU.max))
                tt(stat(SNK, 8).rearrange("p (t h) -> p t h", t=TT), sinks, mx, ALU.subtract
                   ).then_inc(F["sink_arg"], 1)
                ts(stat(NB, 8), stat(MX, 8), -1.0, None, ALU.mult).then_inc(F["softmax_bias"], 1)
                group_norm(2)
                group_low(2)
                probs_out(2)
                dve.wait_ge(F["probs_ready"], 24)
                dve.wait_ge(F["sink_exp"], 1)
                chained(tt(stat(DENS[2], 8), stat(DENS[2], 8), stat(SNK, 8), ALU.add))
                divided(3, 7, DENS[2], 4)
                group_norm(3)
                group_low(3)
                dve.wait_ge(F["pT_high"], 1)
                tt(pT_l[:], ps[:, 4, :].rearrange("p (k n) -> p k n", k=2), pT_h[:].bitcast(F32),
                   ALU.subtract).then_inc(F["pT_low"], 1)

                def add_to_x(name, unit, done):
                    for b in range(4):
                        t, c = quarter(b)
                        if b < 3:
                            dve.wait_ge(F[name], b + 1)
                        else:
                            unit_done(dve, layer, unit)
                        tt(x[:, t, c], x[:, t, c], ps[:, b, :], ALU.add).then_inc(F[done], 1)

                add_to_x("wo_done", U_FFN - 1, "x_mid")
                dve.wait_ge(F["x_squared"], 4)
                norm(1)
                x_low(4, 4)

                def mlp(s, par):
                    bank = 4 + 2 * par
                    for tap, name, before in ((1, "tap1", "tap2"), (0, "conv_done", "tap1")):
                        d = 2 - tap
                        for i in range(4):
                            half, j = divmod(i, 2)
                            f = bass.ds(s * 2 + (half * FT + j), 1)
                            o = cv[par][:, i, d:SEQ]
                            dve.wait_ge(F[before], s * 4 + (2 * half + 2 if tap else i + 1))
                            stt(o, ps[:, bank + half, j * 256:j * 256 + SEQ - d],
                                conv[:, tap, f], o, ALU.mult, ALU.add).then_inc(F[name], 1)
                    dve.wait_ge(F["silu"], s + 1)
                    dve.wait_ge(F["conv_done"], s * 4 + 4)
                    g = cv[par][:, 0:2, :]
                    tt(g, g, cv[par][:, 2:4, :], ALU.mult).then_inc(F["prod"], 1)
                    dve.wait_ge(F["g_high"], s + 1)
                    tt(gT_l[:, par], g, gT_h[:, par].bitcast(F32), ALU.subtract
                       ).then_inc(F["g_low"], 1)

                for s in range(LOOP_FROM):
                    mlp(s, s % 2)
                with dve.Fori(0, LOOPS) as turn:
                    for j in range(2):
                        mlp(turn * 2 + (LOOP_FROM + j), (LOOP_FROM + j) % 2)

                add_to_x("down_done", U_DOWN, "x_low")
                x_low(8, 0)
                for b in range(4):
                    t, c = quarter(b)
                    dve.wait_ge(F["sigmoid"], b + 1)
                    unit_done(dve, layer, U_PROJ)
                    tt(hn[:, t, c], ps[:, 4 + b, :], hn[:, t, c], ALU.mult
                       ).then_inc(F["ple_term"], 1)
                    dve.wait_ge(F["ple_term"], b + 1)
                    tt(x[:, t, c], x[:, t, c], hn[:, t, c], ALU.add).then_inc(x_done, 1)
                dve.drain().then_inc(F["arrived"], 1)
                dve.wait_ge(released, layer + 2)


def kernel(x, p, positions, attn_norm, w_in, mla_q_norm, mla_w_uq, mla_kv_norm, mla_w_ukv,
           mla_q_gain, mla_k_gain, swa_q_gain, swa_k_gain, swa_sinks, moba_q_gain, moba_k_gain,
           group_norm, w_o, ffn_norm, w_up, conv_w, conv_b, w_down, ple_proj, ple_gate):
    import concourse.bacc as bacc
    from concourse.bass_utils import run_bass_kernel_spmd

    a = {k: np.asarray(v) for k, v in locals().items() if k not in ("bacc", "run_bass_kernel_spmd")}
    norm_gains = np.concatenate([np.roll(a["attn_norm"], -1, axis=0), a["ffn_norm"], a["group_norm"]], axis=1)
    small = np.concatenate([a[n] for n in (
        "swa_q_gain", "swa_k_gain", "moba_q_gain", "moba_k_gain", "mla_q_gain", "mla_k_gain",
        "mla_q_norm", "mla_kv_norm", "swa_sinks")], axis=1)
    taps = a["conv_w"].reshape(DEPTH, 3, 2 * FT, P).transpose(0, 2, 1, 3)
    bias = a["conv_b"].reshape(DEPTH, 2 * FT, 1, P)
    conv_rows = np.concatenate([taps, bias], axis=2)
    arrays = {"x_in": a["x"], "p_in": a["p"], "positions": a["positions"], "w_in": a["w_in"],
              "w_uq": a["mla_w_uq"], "w_ukv": a["mla_w_ukv"], "norm_gains": norm_gains,
              "small_gains": small, "w_o": a["w_o"], "w_up": a["w_up"], "conv_rows": conv_rows,
              "w_down": a["w_down"], "ple_proj": a["ple_proj"], "ple_gate": a["ple_gate"]}
    arrays = {k: np.ascontiguousarray(v) for k, v in arrays.items()}
    nc = bacc.Bacc("TRN2", target_bir_lowering=False, num_devices=1)
    args = [nc.dram_tensor(k, v.shape, mybir.dt.from_np(v.dtype), kind="ExternalInput").ap()
            for k, v in arrays.items()]
    out = nc.dram_tensor("out", (1, SEQ, D), F32, kind="ExternalOutput").ap()
    build(nc, *args, out)
    r = run_bass_kernel_spmd(nc, [arrays], core_ids=[0])
    return r.results[0]["out"]
```

```python
from contextlib import ExitStack

import numpy as np

import concourse.bass as bass
from concourse import mybir

F32 = mybir.dt.float32
F32R = mybir.dt.float32r
BF16 = mybir.dt.bfloat16
I32 = mybir.dt.int32
ALU = mybir.AluOpType
ACT = mybir.ActivationFunctionType
AX = mybir.AxisListType

P = 128
D = 1024
SEQ = 256
DEPTH = 2
TT = SEQ // P
KT = D // P
H = 4
HD = 64
GW = H * HD
ROPE_THETA = 10000.0
EPS = 1e-6
NEG = -1e30
QR, KVR = 192, 128
NOPE, PE_DIM = 64, 32
QK = NOPE + PE_DIM
DFF = 2816
FT = DFF // P
PLE = 256

OFF_SB, OFF_MLA = 0, 3 * GW
OFF_SWA = OFF_MLA + QR + KVR + PE_DIM
OFF_MOBA = OFF_SWA + GW + 2 * 2 * HD
MLA_COLS = QR + KVR + PE_DIM

SB, MLA, SWA, MOBA = range(4)

G_ATTN, G_FFN, G_GROUP = 0, D, 2 * D
S_SWAQ, S_SWAK, S_MOBAQ, S_MOBAK = 0, 64, 128, 192
S_MLAQ, S_MLAK = 256, 256 + QK
S_QN = S_MLAK + QK
S_KVN = S_QN + QR
S_SINK = S_KVN + KVR
S_ALL = S_SINK + H

RING = 3
(M_MLA_A, M_MLA_B, M_SB_Q, M_SB_K, M_SB_V, M_MOBA_Q, M_MOBA_K, M_SWA_Q, M_SWA_KV, M_MOBA_V
 ) = range(10)
WIN_PARTS = [(OFF_MLA, MLA_COLS, 0, KT // 2), (OFF_MLA, MLA_COLS, KT // 2, KT // 2),
             (OFF_SB, 256, 0, KT), (OFF_SB + 256, 256, 0, KT), (OFF_SB + 512, 256, 0, KT),
             (OFF_MOBA, 256, 0, KT), (OFF_MOBA + 256, 256, 0, KT),
             (OFF_SWA, 256, 0, KT), (OFF_SWA + 256, 256, 0, KT), (OFF_MOBA + 512, 256, 0, KT)]
WO_ROWS = [(0, 2), (2, 2), (6, 1), (7, 1), (4, 2)]
GATE_ROWS = [(0, 1), (1, 2), (3, 1), (4, 2), (6, 2)]
U_WO = len(WIN_PARTS)
U_FFN = U_WO + len(WO_ROWS)
STEPS = FT // 2
LOOP_FROM = 3
LOOPS = (STEPS - LOOP_FROM) // 2
U_LOOP = U_FFN + 2 + 3 * (LOOP_FROM - 1)
U_AFTER = U_LOOP + 6 * LOOPS
U_PROJ = U_AFTER
U_DOWN = U_PROJ + 1
U_GATE = U_DOWN + 1
UNITS = U_GATE + len(GATE_ROWS)
assert UNITS % RING == 0 and LOOPS * 2 + LOOP_FROM == STEPS
MAGIC = 1.5 * 2.0 ** 23
TWO_PI = [6.28125, 0.0019353071693331003, 1.0253691153482577e-11]
ROOT_GUESS = float(0x5F3759DF - 0x00400000)
SLOT = 2048
COLS = ([n * w for _, w, _, n in WIN_PARTS] + [n * D for _, n in WO_ROWS]
        + [SLOT] * (U_GATE - U_FFN) + [n * D for _, n in GATE_ROWS])
assert len(COLS) == UNITS and max(COLS) == SLOT


def unit_gate(s):
    return U_FFN + 3 * s - (1 if s else 0)


_at = [0]


def _cols(n):
    _at[0] += n
    return _at[0] - n


ST_X = _cols(10)
ST_L = _cols(12)
ST_PE = _cols(2)
ST_M = _cols(48)
ST_B = _cols(48)
ST_S = _cols(42)
RS_MLA, RS_MOBA, RS_SWA = _cols(8), _cols(8), _cols(8)
MX = _cols(8)
NB = _cols(8)
SNK = _cols(8)
DENS = [_cols(8) for _ in range(3)]
RDEN = _cols(8)
ST_G = _cols(24)
ST_T = _cols(16)
ST_ALL = _at[0]

GROUP_ORDER = [SB, MLA, MOBA, SWA]

FLOW = """x_squared hn_ready xT_ready xT_high xT_low
pr_ready squared squares_read lat_done lat_T cT_ready mla_up mla_up_ready
v_ready mla_qk mla_T mT_ready conv_T conv_ready
moba_qk moba_T mobaT_ready swa_qk swa_T swaT_ready
sbT_ready scores_ready half_scores half_z softmax_bias sink_arg sink_exp probs_ready probs_T
pt_ready pv_ready group_out group_sq group_done
sb_z sb_abs sb_exp sb_log sb_soft sb_minus sb_probs groups_T mT_high mT_low
wo_done x_mid tap2 tap1 conv_done silu prod g_high g_low
p_T pT_high pT_low down_done x_mlp gate_ready sigmoid ple_term
dve_step arrived""".split()


PAIRED = (0, 2, 1, 3)
GROUPED = (0, 1, 2, 3)
PART_BANKS = (5, 4, 6)
PART_COLS = (slice(512, 1024), slice(0, 512), slice(1024, 1536))
PARTS = 3


def part_heads(order, part):
    if part == 1:
        return slice(0, H)
    heads = order[part:part + 2]
    return slice(H + heads[0], H + heads[1] + 1, heads[1] - heads[0])


def build(nc, x_in, p_in, positions, w_in, w_uq, w_ukv, norm_gains, small_gains, w_o, w_up,
          conv_rows, w_down, ple_proj, ple_gate, out):
    with ExitStack() as ctx:
        def sb(name, shape, dt=F32):
            return ctx.enter_context(nc.sbuf_tensor(name, shape, dt))

        def sem(name):
            return ctx.enter_context(nc.semaphore(name))

        raw = sb("raw", [P, RING, SLOT])
        wh = sb("wh", [P, RING, SLOT], F32R)
        wl = sb("wl", [P, RING, SLOT], F32R)
        x = sb("x", [P, TT, D])
        hn = sb("hn", [P, TT, D])
        hT_h = sb("hT_h", [P, KT, SEQ], F32R)
        hT_l = sb("hT_l", [P, KT, SEQ], F32R)
        gT_h = sb("gT_h", [P, 2, 2, SEQ], F32R)
        gT_l = sb("gT_l", [P, 2, 2, SEQ], F32R)
        pT_h = sb("pT_h", [P, 2, SEQ], F32R)
        pT_l = sb("pT_l", [P, 2, SEQ], F32R)
        ng = sb("ng", [P, 3 * D])
        sg = sb("sg", [P, S_ALL])
        uq = sb("uq", [P, 2, H * QK])
        ukv = sb("ukv", [P, H * 2 * HD])
        p_sb = sb("p_sb", [P, TT, PLE])
        conv = sb("conv", [P, 4, 2 * FT])
        ident = sb("ident", [P, P])
        ident_b = sb("ident_b", [P, P], BF16)
        causal = sb("causal", [P, P], BF16)
        above = sb("above", [P, P], BF16)
        neg_tri = sb("neg_tri", [P, P])
        neg_ones = sb("neg_ones", [P, P])
        inv_freq = sb("inv_freq", [P, HD // 2])
        pos_i = sb("pos_i", [P, TT], I32)
        pos_f = sb("pos_f", [P, TT])
        rope_c = sb("rope_c", [P, TT, HD])
        rope_s = sb("rope_s", [P, TT, HD])
        rope_c32 = sb("rope_c32", [P, TT, PE_DIM])
        rope_s32 = sb("rope_s32", [P, TT, PE_DIM])
        gc = sb("gc", [P, 4, TT, HD])
        gs = sb("gs", [P, 4, TT, HD])
        pr = sb("pr", [P, 2, TT, 512])
        rot = sb("rot", [P, TT, 512])
        lat = sb("lat", [P, 1536])
        kpe = sb("kpe", [P, TT, PE_DIM])
        tmp = sb("tmp", [P, 1024])
        mT = sb("mT", [P, 2, H, SEQ])
        qkT_moba = sb("qkT_moba", [P, 4, SEQ])
        qkT_swa = sb("qkT_swa", [P, 3, SEQ])
        qkT_sb = sb("qkT_sb", [P, 4, SEQ])
        v_moba = sb("v_moba", [P, TT, GW])
        v_swa = sb("v_swa", [P, TT, 2 * HD])
        v_sb = sb("v_sb", [P, TT, GW])
        pb = sb("pb", [P, 1536])
        pt = sb("pt", [P, 1536])
        st = sb("st", [P, ST_ALL])

        ps = ctx.enter_context(nc.psum_tensor("ps", [P, 8, 512], F32))

        mk = qkT_moba[:].rearrange("p k n -> p (k n)")[:, 0:TT * H * QK].rearrange(
            "p (t h n) -> p t h n", t=TT, h=H)
        mq = lat[:, 0:768].rearrange("p (t h n) -> p t h n", t=TT, h=H)
        cT = lat[:, 768:1536].rearrange("p (k n) -> p k n", k=3)
        mkv = pr[:, 0].rearrange("p t (h n) -> p t h n", h=H)
        sb_e, sb_sp = pb, pt
        cv = [pb[:, 0:1024].rearrange("p (a n) -> p a n", a=4),
              pt[:, 0:1024].rearrange("p (a n) -> p a n", a=4)]
        conv_raw = tmp[0:2 * FT, 0:512].rearrange("p (a n) -> p a n", a=4)
        tmp2 = tmp[:].rearrange("p (t n) -> p t n", t=TT)

        raw_landed = [sem(f"raw_landed{n}") for n in range(RING)]
        h_made = sem("h_made")
        l_made = sem("l_made")
        w_used = sem("w_used")
        x_landed = [sem(f"x_landed{t}") for t in range(TT)]
        pos_landed = sem("pos_landed")
        first_squares = sem("first_squares")
        gain_landed = sem("gain_landed")
        x_done = sem("x_done")
        ng_landed, sg_landed = sem("ng_landed"), sem("sg_landed")
        uq_landed, uq2_landed, ukv_landed = sem("uq_landed"), sem("uq2_landed"), sem("ukv_landed")
        p_landed, conv_landed = sem("p_landed"), sem("conv_landed")
        out_landed = sem("out_landed")
        column_0 = sem("column_0")
        consts_made = sem("consts_made")
        rope_step, rope_arg, rope_sin = sem("rope_step"), sem("rope_arg"), sem("rope_sin")
        released = sem("released")

        F = {name: sem(name) for name in FLOW}
        first = F[FLOW[0]].num
        assert [F[n].num for n in FLOW] == list(range(first, first + len(FLOW)))
        flow_range = range(first, first + len(FLOW))

        block = ctx.enter_context(nc.Block())

        def ge(eng, name, value):
            if not (isinstance(value, int) and value <= 0):
                eng.wait_ge(F[name], value)

        def quarter(i):
            half, t = divmod(i, 2)
            return t, slice(half * 512, (half + 1) * 512)

        def stat(a, n=1):
            return st[:, a:a + n]

        def per_head(ap, width):
            return ap.unsqueeze(2).broadcast_to([P, ap.shape[1], width])

        def unit_done(eng, layer, u, turn=0):
            eng.wait_ge(w_used, layer * UNITS + turn * 6 + (u + 1 + RING))

        @block.sync
        def _(sp):
            for t in range(TT):
                sp.dma_start(x[:, t, :], x_in[0, t * P:(t + 1) * P, :]).then_inc(x_landed[t], 16)
            with sp.Fori(0, DEPTH) as layer:
                def load(src, u, turn=0):
                    slot, k = u % RING, src.shape[1]
                    sp.wait_ge(l_made, layer * UNITS + turn * 6 + (u + 1))
                    if u == M_SB_Q:
                        sp.sem_inc(column_0, 1)
                    sp.dma_start(raw[:, slot, 0:COLS[u]].rearrange("p (k n) -> p k n", k=k),
                                 src).then_inc(raw_landed[slot], 16)

                def rows(w, k, n):
                    return w[layer][k * P:(k + n) * P, :].rearrange("(k p) n -> p k n", p=P)

                def load_up(s, half, u, turn=0):
                    w = w_up[layer].rearrange("(k p) n -> p k n", p=P)
                    load(w[:, :, bass.ds(s * 256 + half * DFF, 256)], u, turn)

                def load_down(s, u, turn=0):
                    load(w_down[layer][bass.ds(s * 256, 256), :].rearrange(
                        "(k p) n -> p k n", p=P), u, turn)

                for u, (c, w, k, n) in enumerate(WIN_PARTS):
                    load(rows(w_in, k, n)[:, :, c:c + w], u)
                for n, (k, m) in enumerate(WO_ROWS):
                    load(rows(w_o, k, m), U_WO + n)
                for s in range(LOOP_FROM):
                    for half in range(2):
                        load_up(s, half, unit_gate(s) + half)
                    if s:
                        load_down(s - 1, unit_gate(s) + 2)
                with sp.Fori(0, LOOPS) as turn:
                    for j in range(2):
                        u = unit_gate(LOOP_FROM + j)
                        for half in range(2):
                            load_up(turn * 2 + (LOOP_FROM + j), half, u + half, turn)
                        load_down(turn * 2 + (LOOP_FROM + j - 1), u + 2, turn)
                load(rows(ple_proj, 0, 2), U_PROJ)
                load_down(STEPS - 1, U_DOWN)
                for n, (k, m) in enumerate(GATE_ROWS):
                    load(rows(ple_gate, k, m), U_GATE + n)
            for i in range(4):
                t, c = quarter(i)
                sp.wait_ge(x_done, (DEPTH - 1) * 4 + i + 1)
                sp.dma_start(out[0, t * P:(t + 1) * P, c], x[:, t, c]).then_inc(out_landed, 16)
            sp.wait_ge(out_landed, 16 * 4)
            sp.wait_ge(gain_landed, 16 * (DEPTH + 1))

        @block.gpsimd
        def _(pool):
            pool.sem_inc(l_made, RING)
            for t, v in ((ident, 0.0), (causal, 0.0), (above, 0.0), (neg_tri, -1.0),
                         (neg_ones, -1.0)):
                pool.memset(t[:], v).then_inc(consts_made, 1)
            for j in range(HD // 2):
                freq = float(np.float32(ROPE_THETA ** (-2.0 * j / HD)))
                last = pool.memset(inv_freq[:, j:j + 1], freq)
            last.then_inc(consts_made, 1)
            pool.wait_ge(consts_made, 6)
            for t, op, fill, sign in ((ident, ALU.not_equal, 1.0, 1), (causal, ALU.is_ge, NEG, 1),
                                      (above, ALU.is_gt, NEG, -1), (neg_tri, ALU.is_ge, 0.0, 1)):
                pool.affine_select(out=t[:], in_=t[:], compare_op=op, fill=fill, base=0,
                                   pattern=[[-sign, P]], channel_multiplier=sign
                                   ).then_inc(consts_made, 1)
            pool.wait_ge(consts_made, 7)
            pool.tensor_copy(ident_b[:], ident[:]).then_inc(consts_made, 1)
            with pool.Fori(0, DEPTH) as layer:
                def low(u, turn=0):
                    slot, n = u % RING, COLS[u]
                    pool.wait_ge(h_made, layer * UNITS + turn * 6 + (u + 1 + RING))
                    pool.wait_ge(w_used, layer * UNITS + turn * 6 + (u + 1))
                    pool.tensor_tensor(wl[:, slot, 0:n], raw[:, slot, 0:n],
                                       wh[:, slot, 0:n].bitcast(F32), ALU.subtract
                                       ).then_inc(l_made, 1)

                for u in range(U_LOOP):
                    low(u)
                with pool.Fori(0, LOOPS) as turn:
                    for u in range(U_LOOP, U_LOOP + 6):
                        low(u, turn)
                for u in range(U_AFTER, UNITS):
                    low(u)

        @block.scalar
        def _(act):
            act.sem_inc(h_made, RING)
            act.dma_start(pos_i[:], positions.rearrange("a (t p) -> p (a t)", p=P),
                          allow_slow_non_contiguous=True).then_inc(pos_landed, 16)
            act.dma_start(ng[:, 0:D], norm_gains[DEPTH - 1, 0:D].partition_broadcast(P)
                          ).then_inc(gain_landed, 16)

            def x_square(i):
                t, c = quarter(i)
                return act.activation(hn[:, t, c], x[:, t, c], ACT.Square,
                                      accum_out=stat(ST_X + i))

            for i in (0, 2, 1, 3):
                act.wait_ge(x_landed[i % 2], 16)
                x_square(i).then_inc(first_squares, 1)
            act.wait_ge(first_squares, 4)
            act.sem_inc(released, 1)
            act.wait_ge(rope_arg, 1)
            for table, a in ((rope_s[:, :, 32:64], 0), (rope_c[:, :, 0:32], 64)):
                act.activation(table, tmp[:, a:a + 64].rearrange("p (t n) -> p t n", t=TT),
                               ACT.Sin).then_inc(rope_sin, 1)

            with act.Fori(0, DEPTH) as layer:
                def high(u, turn=0):
                    slot, n = u % RING, COLS[u]
                    act.wait_ge(raw_landed[slot],
                                (layer * (UNITS // RING) + turn * (6 // RING) + (u // RING + 1)) * 16)
                    act.wait_ge(w_used, layer * UNITS + turn * 6 + (u + 1))
                    act.activation(wh[:, slot, 0:n], raw[:, slot, 0:n], ACT.Copy
                                   ).then_inc(h_made, 1)

                def x_high(n, bank):
                    for k in range(4):
                        half, t = divmod(k, 2)
                        act.wait_ge(F["xT_ready"], n + k + 1)
                        act.activation(hT_h[:, 4 * half:4 * half + 4, t * P:(t + 1) * P],
                                       ps[:, bank + k, :].rearrange("p (k n) -> p k n", k=4),
                                       ACT.Copy).then_inc(F["xT_high"], 1)

                def copied(dst, src, ready, n, done, **kw):
                    if ready == "unit":
                        unit_done(act, layer, n)
                    else:
                        act.wait_ge(F[ready], n)
                    act.activation(dst, src, ACT.Copy, **kw).then_inc(F[done], 1)

                def exps(g, rs, den, order=PAIRED):
                    if g:
                        act.wait_ge(F["probs_T"], PARTS * g)
                    else:
                        act.wait_ge(F["pv_ready"], 1)
                    for part in range(PARTS):
                        act.wait_ge(F["softmax_bias"], PARTS * g + part + 1)
                        cols = range(ST_ALL)[part_heads(order, part)]
                        w = PART_COLS[part]
                        w = (w.stop - w.start) // len(cols)
                        for i, col in enumerate(cols):
                            c = PART_COLS[part].start + i * w
                            act.activation(pb[:, c:c + w],
                                           ps[:, PART_BANKS[part], i * w:(i + 1) * w], ACT.Exp,
                                           bias=stat(NB + col), scale=stat(rs + col),
                                           accum_out=stat(den + col)
                                           ).then_inc(F["probs_ready"], 1)

                def group_squares(n):
                    c = GROUP_ORDER[n] * GW
                    act.wait_ge(F["group_out"], n + 1)
                    for t in range(TT):
                        act.activation(junk(t), hn[:, t, c:c + GW], ACT.Square,
                                       accum_out=stat((ST_G + 6 * n if n else ST_S + 12) + t)
                                       ).then_inc(F["group_sq"], 1)

                def junk(t):
                    return lat[:, 768 + t * GW:768 + (t + 1) * GW]

                def group_high(n):
                    g = GROUP_ORDER[n]
                    copied(hT_h[:, 2 * g:2 * g + 2, :],
                           ps[:, 7, :].rearrange("p (k n) -> p k n", k=2),
                           "groups_T", n + 1, "mT_high")

                high(0)
                act.dma_start(sg[:], small_gains[layer].partition_broadcast(P)
                              ).then_inc(sg_landed, 16)
                act.dma_start(uq[:, 0, :], w_uq[layer][0:P, :]).then_inc(uq_landed, 16)
                act.dma_start(uq[0:QR - P, 1, :], w_uq[layer][P:QR, :]).then_inc(uq2_landed, 16)
                act.dma_start(ukv[:], w_ukv[layer]).then_inc(ukv_landed, 16)
                act.wait_ge(rope_sin, 2)
                act.dma_start(conv_raw, conv_rows[layer]).then_inc(conv_landed, 16)
                high(1)
                x_high(0, 4)
                high(2)

                high(3)
                for t in range(TT):
                    copied(pr[:, 0, t, 0:MLA_COLS], ps[:, t, 0:MLA_COLS], "unit", M_MLA_B,
                           "pr_ready")
                for t in range(TT):
                    act.wait_ge(F["pr_ready"], t + 1)
                    act.activation(rot[:, t, 0:MLA_COLS], pr[:, 0, t, 0:MLA_COLS], ACT.Square
                                   ).then_inc(F["squared"], 1)
                high(4)
                copied(qkT_sb[:, 0:2, :], ps[:, 2, :].rearrange("p (k n) -> p k n", k=2),
                       "unit", M_SB_Q, "sbT_ready", scale=HD ** -0.5)
                high(5)
                for t in range(TT):
                    copied(cT[:, :, t * P:(t + 1) * P],
                           ps[:, 4 + t, 0:384].rearrange("p (k n) -> p k n", k=3),
                           "lat_T", 1 + t, "cT_ready")
                copied(qkT_sb[:, 2:4, :], ps[:, 3, :].rearrange("p (k n) -> p k n", k=2),
                       "unit", M_SB_K, "sbT_ready")
                high(6)
                act.dma_start(p_sb[:], p_in[layer, 0].rearrange("(t p) n -> p t n", p=P)
                              ).then_inc(p_landed, 16)
                act.dma_start(ng[:, D:3 * D], norm_gains[layer, D:3 * D].partition_broadcast(P)
                              ).then_inc(ng_landed, 16)
                act.wait_ge(F["hn_ready"], 4)
                act.dma_start(ng[:, 0:D], norm_gains[layer, 0:D].partition_broadcast(P)
                              ).then_inc(gain_landed, 16)
                for t in range(TT):
                    copied(mq[:, t].rearrange("p h n -> p (h n)"), ps[:, 4 + 2 * t, 0:H * QK],
                           "mla_up", 1 + t, "mla_up_ready")
                    copied(pr[:, 0, t, :], ps[:, 5 + 2 * t, :], "lat_T", 2, "mla_up_ready")
                act.wait_ge(F["mla_up_ready"], 4)
                act.wait_ge(F["squares_read"], 1)
                act.activation(rot[:, :, 0:H * QK], mq.rearrange("p t h n -> p t (h n)"),
                               ACT.Square).then_inc(F["squared"], 1)
                act.wait_ge(F["conv_T"], 1)
                for t in range(TT):
                    act.activation(
                        tmp[:, t * 256:(t + 1) * 256].rearrange("p (h n) -> p h n", h=H),
                        mkv[:, t, :, 0:NOPE], ACT.Square).then_inc(F["squared"], 1)
                for t in range(TT):
                    copied(v_sb[:, t, :], ps[:, t, 0:256], "unit", M_SB_V, "v_ready")
                high(7)
                high(8)
                for b in range(3):
                    c = slice(b * 512, (b + 1) * 512)
                    act.wait_ge(F["sb_z"], b + 1)
                    act.activation(sb_e[:, c], ps[:, 4 + b, :], ACT.Abs).then_inc(F["sb_abs"], 1)
                for b in range(3):
                    c = slice(b * 512, (b + 1) * 512)
                    act.wait_ge(F["sb_abs"], b + 1)
                    act.activation(sb_e[:, c], sb_e[:, c], ACT.Exp, scale=-1.0
                                   ).then_inc(F["sb_exp"], 1)
                for b in range(3):
                    c = slice(b * 512, (b + 1) * 512)
                    act.wait_ge(F["sb_exp"], b + 1)
                    act.activation(sb_e[:, c], sb_e[:, c], ACT.Ln, bias=1.0
                                   ).then_inc(F["sb_log"], 1)
                for t in range(TT):
                    copied(pr[:, 1, t, :], ps[:, 2 + t, :], "unit", M_MOBA_K, "pr_ready")
                act.wait_ge(F["pr_ready"], 4)
                act.wait_ge(F["squares_read"], 2)
                act.activation(rot[:], pr[:, 1], ACT.Square).then_inc(F["squared"], 1)
                high(9)
                for t in range(TT):
                    if t == 1:
                        high(10)
                    for a in range(2):
                        copied(mT[0:QK, a, :, t * P:(t + 1) * P],
                               ps[0:QK, a, :].rearrange("p (k n) -> p k n", k=H),
                               "mla_T", 1 + t, "mT_ready")
                for b in range(3):
                    c = slice(b * 512, (b + 1) * 512)
                    act.wait_ge(F["sb_minus"], b + 1)
                    act.activation(sb_e[:, c], ps[:, 4 + b, :], ACT.Exp
                                   ).then_inc(F["sb_probs"], 1)
                act.wait_ge(F["moba_qk"], 1)
                for t in range(TT):
                    copied(pr[:, 1, t, 0:384], ps[:, 2 + t, 0:384], "unit", M_SWA_KV,
                           "pr_ready")
                    act.activation(v_swa[:, t, :], ps[:, 2 + t, 384:512], ACT.Copy
                                   ).then_inc(F["v_ready"], 1)
                act.wait_ge(F["pr_ready"], 6)
                act.activation(tmp2[:, :, 0:384], pr[:, 1, :, 0:384], ACT.Square
                               ).then_inc(F["squared"], 1)
                group_squares(0)
                high(11)
                for t in range(TT):
                    copied(qkT_moba[:, :, t * P:(t + 1) * P],
                           ps[:, t, :].rearrange("p (k n) -> p k n", k=4),
                           "moba_T", 1 + t, "mobaT_ready")
                exps(0, RS_MLA, DENS[0])
                unit_done(act, layer, M_MOBA_V)
                group_high(0)
                for t in range(TT):
                    copied(v_moba[:, t, :], ps[:, 2 + t, 0:256], "unit", M_MOBA_V, "v_ready")
                high(12)
                group_squares(1)
                for t in range(TT):
                    copied(qkT_swa[:, :, t * P:(t + 1) * P],
                           ps[:, 2 + t, 0:384].rearrange("p (k n) -> p k n", k=3),
                           "swa_T", 1 + t, "swaT_ready")
                exps(1, RS_MOBA, DENS[1])
                group_high(1)
                high(13)
                group_squares(2)
                exps(2, RS_SWA, DENS[2], GROUPED)
                act.wait_ge(F["sink_arg"], PARTS)
                act.activation(stat(SNK, 8), stat(SNK, 8), ACT.Exp).then_inc(F["sink_exp"], 1)
                group_high(2)
                high(14)
                group_squares(3)
                high(15)
                group_high(3)
                act.wait_ge(F["p_T"], 1)
                act.activation(pT_h[:], ps[:, 4, :].rearrange("p (k n) -> p k n", k=2), ACT.Copy
                               ).then_inc(F["pT_high"], 1)
                high(16)

                act.wait_ge(F["groups_T"], 4)
                for i in range(4):
                    act.wait_ge(F["x_mid"], i + 1)
                    x_square(i).then_inc(F["x_squared"], 1)
                x_high(4, 4)

                def mlp(s, par, this, u, turn=0):
                    bank = 4 + 2 * par
                    high(u, turn)
                    high(u + 1, turn)
                    ge(act, "g_low", s - 1)
                    for half in range(2):
                        unit_done(act, layer, this + half, turn)
                        for j in range(2):
                            f = bass.ds(s * 2 + (half * FT + j), 1)
                            act.activation(cv[par][:, 2 * half + j, :],
                                           ps[:, bank + half, j * 256:(j + 1) * 256],
                                           ACT.Identity, bias=conv[:, 3, f],
                                           scale=conv[:, 2, f]).then_inc(F["tap2"], 1)
                    act.wait_ge(F["conv_done"], s * 4 + 2)
                    act.activation(cv[par][:, 0:2, :], cv[par][:, 0:2, :], ACT.Silu
                                   ).then_inc(F["silu"], 1)
                    act.wait_ge(F["prod"], s + 1)
                    if not (isinstance(s, int) and s < 2):
                        unit_done(act, layer, this - 1, turn)
                    act.activation(gT_h[:, par], cv[par][:, 0:2, :], ACT.Copy
                                   ).then_inc(F["g_high"], 1)
                    high(u + 2, turn)

                act.wait_ge(F["conv_ready"], 1)
                for s in range(LOOP_FROM):
                    mlp(s, s % 2, unit_gate(s), unit_gate(s + 1))
                with act.Fori(0, LOOPS) as turn:
                    for j in range(2):
                        s = LOOP_FROM + j
                        mlp(turn * 2 + s, s % 2, unit_gate(s), unit_gate(s + 1), turn)

                high(U_GATE + 1)
                x_high(8, 0)
                for n in range(2, len(GATE_ROWS)):
                    high(U_GATE + n)
                for b in range(4):
                    t, c = quarter(b)
                    if b < 3:
                        act.wait_ge(F["gate_ready"], b + 1)
                    else:
                        unit_done(act, layer, UNITS - 1)
                    act.activation(hn[:, t, c], ps[:, b, :], ACT.Sigmoid
                                   ).then_inc(F["sigmoid"], 1)
                for i in range(4):
                    act.wait_ge(x_done, layer * 4 + (i + 1))
                    x_square(i).then_inc(F["x_squared"], 1)
                act.wait_ge(F["x_squared"], 8)
                act.drain()
                act.wait_ge(F["arrived"], 2)
                act.sem_clear(flow_range)
                act.sem_inc(released, 1)

        @block.tensor
        def _(pe):
            pe.sem_inc(w_used, RING)
            pe.wait_ge(consts_made, 11)
            with pe.Fori(0, DEPTH) as layer:
                def unit(u, turn=0):
                    pe.wait_ge(l_made, layer * UNITS + turn * 6 + (u + 1 + RING))
                    return u % RING

                def split_product(dst, a_h, a_l, b_h, b_l, start, stop):
                    pe.matmul(dst, a_h, b_h, start=start, stop=False, skip_group_check=True)
                    pe.matmul(dst, a_h, b_l, start=False, stop=False, skip_group_check=True)
                    return pe.matmul(dst, a_l, b_h, start=False, stop=stop,
                                     skip_group_check=True)

                def high_part_first(dst, operands, start, stop, low_ready):
                    for i, (a_h, _, b_h, b_l) in enumerate(operands):
                        pe.matmul(dst, a_h, b_h, start=start and i == 0, stop=False,
                                  skip_group_check=True)
                        pe.matmul(dst, a_h, b_l, start=False, stop=False, skip_group_check=True)
                    name, count = low_ready
                    pe.wait_ge(F[name], count)
                    for i, (_, a_l, b_h, _) in enumerate(operands):
                        mm = pe.matmul(dst, a_l, b_h, start=False,
                                       stop=stop and i == len(operands) - 1,
                                       skip_group_check=True)
                    return mm

                def project(u, banks, col, quarters=None):
                    slot, (_, w, k0, n) = unit(u), WIN_PARTS[u]
                    for t in range(TT):
                        tok = slice(t * P, (t + 1) * P)
                        if quarters is not None:
                            pe.wait_ge(F["xT_high"], quarters + t + 1)
                            mm = high_part_first(
                                ps[:, banks[t], col:col + w],
                                [(hT_h[:, k0 + i, tok], hT_l[:, k0 + i, tok],
                                  wh[:, slot, i * w:(i + 1) * w], wl[:, slot, i * w:(i + 1) * w])
                                 for i in range(n)],
                                k0 == 0, k0 + n == KT, ("xT_low", quarters + t + 1))
                            continue
                        for i in range(n):
                            k, c = k0 + i, slice(i * w, (i + 1) * w)
                            mm = split_product(ps[:, banks[t], col:col + w],
                                               hT_h[:, k, tok], hT_l[:, k, tok],
                                               wh[:, slot, c], wl[:, slot, c],
                                               k == 0, k == KT - 1)
                    mm.then_inc(w_used, 1)

                def project_T(u, bank):
                    slot = unit(u)
                    for j in range(2):
                        for k in range(KT):
                            c = slice(k * 256 + j * P, k * 256 + (j + 1) * P)
                            mm = split_product(ps[:, bank, j * 256:(j + 1) * 256],
                                               wh[:, slot, c], wl[:, slot, c],
                                               hT_h[:, k, :], hT_l[:, k, :],
                                               k == 0, k == KT - 1)
                    mm.then_inc(w_used, 1)

                def x_T(src, bank, ready):
                    for k in range(4):
                        half, t = divmod(k, 2)
                        pe.wait_ge(F[ready[0]], ready[1] + k + 1)
                        for j in range(4):
                            c = (4 * half + j) * P
                            mm = pe.transpose(ps[:, bank + k, j * P:(j + 1) * P],
                                              src[:, t, c:c + P], ident[:])
                        mm.then_inc(F["xT_ready"], 1)

                def wide(u, n, k0, act_h, act_l, first, last, banks=0, name=None, turn=0,
                         split=None, between=None, order=range(4), free=None, low_ready=None):
                    slot = unit(u, turn)
                    for i, b in enumerate(order):
                        half, t = divmod(b, 2)
                        if between and i == between[0]:
                            between[1]()
                        if free and i == free[0]:
                            pe.wait_ge(F[free[1]], free[2])
                        tok = slice(t * P, (t + 1) * P)
                        if split is not None:
                            pe.wait_ge(F["xT_low"], split + max(b + 1, 2))
                        cols = [slice(k * D + half * 512, k * D + half * 512 + 512)
                                for k in range(n)]
                        if low_ready and i == 0:
                            mm = high_part_first(
                                ps[:, banks + b, :],
                                [(act_h[:, k0 + k, tok], act_l[:, k0 + k, tok],
                                  wh[:, slot, c], wl[:, slot, c]) for k, c in enumerate(cols)],
                                first, last, low_ready)
                        for k, c in enumerate(cols if not (low_ready and i == 0) else []):
                            mm = split_product(ps[:, banks + b, :],
                                               act_h[:, k0 + k, tok], act_l[:, k0 + k, tok],
                                               wh[:, slot, c], wl[:, slot, c],
                                               first and k == 0, last and k == n - 1)
                        if i < 3 and name:
                            mm.then_inc(F[name], 1)
                    mm.then_inc(w_used, 1)

                def scores(g, q, k, prev_mask, order=PAIRED):
                    def tile_0(heads):
                        for h in heads:
                            o = ps[:, 4, h * P:(h + 1) * P]
                            pe.matmul(o, q(h)[:, 0:P], k(h)[:, 0:P], start=(h == 0), stop=False,
                                      skip_group_check=True)
                            mm = pe.matmul(o, ident_b[:], causal[:], start=False, stop=True,
                                           skip_group_check=True)
                        return mm

                    def tile_1(heads, bank):
                        for i, h in enumerate(heads):
                            o = ps[:, bank, i * 256:(i + 1) * 256]
                            pe.matmul(o, q(h)[:, P:SEQ], k(h)[:, 0:SEQ], start=(i == 0),
                                      stop=False, skip_group_check=True)
                            if prev_mask is not None:
                                pe.matmul(o[:, 0:P], ident_b[:], prev_mask[:], start=False,
                                          stop=True, skip_group_check=True)
                            mm = pe.matmul(o[:, P:256], ident_b[:], causal[:], start=False,
                                           stop=True, skip_group_check=True)
                        return mm

                    tile_0(order[0:2]).then_inc(F["half_scores"], 1)
                    tile_1(order[0:2], 5).then_inc(F["scores_ready"], 1)
                    pe.wait_ge(F["half_scores"], g + 1)
                    tile_0(order[2:4]).then_inc(F["scores_ready"], 1)
                    tile_1(order[2:4], 6).then_inc(F["scores_ready"], 1)

                def probs_T(g):
                    for part, used in enumerate((2, 6, 8)):
                        pe.wait_ge(F["probs_ready"], 8 * g + used)
                        for j in range(4):
                            c = PART_COLS[part].start + j * P
                            mm = pe.transpose(ps[:, PART_BANKS[part], j * P:(j + 1) * P],
                                              pb[:, c:c + P], ident[:])
                        mm.then_inc(F["probs_T"], 1)

                def pv(g, v, bank, order=PAIRED):
                    for part in range(PARTS):
                        pe.wait_ge(F["pt_ready"], PARTS * g + part + 1)
                        if part == 1:
                            for h in range(H):
                                pe.matmul(ps[:, bank, h * HD:(h + 1) * HD],
                                          pt[:, h * P:(h + 1) * P], v(h, 0), start=True,
                                          stop=True, skip_group_check=True)
                            continue
                        for i, h in enumerate(order[part:part + 2]):
                            for k in range(TT):
                                c = PART_COLS[part].start + i * 256 + k * P
                                mm = pe.matmul(ps[:, bank, 256 + h * HD:256 + (h + 1) * HD],
                                               pt[:, c:c + P], v(h, k), start=(k == 0),
                                               stop=(k == TT - 1), skip_group_check=True)
                    mm.then_inc(F["pv_ready"], 1)

                def head(qkT, pair, h):
                    return qkT[(h % 2) * HD:(h % 2) * HD + HD, pair + h // 2, :]

                x_T(hn, 4, ("hn_ready", 0))
                project(M_MLA_A, (0, 1), 0, quarters=0)
                project(M_MLA_B, (0, 1), 0, quarters=2)
                pe.wait_ge(conv_landed, layer * 16 + 16)
                project_T(M_SB_Q, 2)
                for a in range(4):
                    mm = pe.transpose(ps[:, 7, a * 44:a * 44 + 44], conv_raw[:, a, :],
                                      ident[0:2 * FT, 0:2 * FT])
                mm.then_inc(F["conv_T"], 1)
                for t in range(TT):
                    pe.wait_ge(F["lat_done"], t + 1)
                    for n, (c, w) in enumerate(((0, P), (P, QR - P), (QR, KVR))):
                        mm = pe.transpose(ps[0:w, 4 + t, n * P:(n + 1) * P], pr[:, 0, t, c:c + w],
                                          ident[:])
                    mm.then_inc(F["lat_T"], 1)
                project_T(M_SB_K, 3)
                pe.wait_ge(uq_landed, layer * 16 + 16)
                pe.wait_ge(uq2_landed, layer * 16 + 16)
                pe.wait_ge(ukv_landed, layer * 16 + 16)
                pe.wait_ge(F["cT_ready"], 2)
                pe.wait_ge(F["conv_ready"], 1)
                for t in range(TT):
                    tok = slice(t * P, (t + 1) * P)
                    o = ps[:, 4 + 2 * t, 0:H * QK]
                    pe.matmul(o, cT[:, 0, tok], uq[:, 0, :], start=True, stop=False)
                    pe.matmul(o, cT[0:QR - P, 1, tok], uq[0:QR - P, 1, :], start=False, stop=True)
                    pe.matmul(ps[:, 5 + 2 * t, :], cT[:, 2, tok], ukv[:], start=True, stop=True
                              ).then_inc(F["mla_up"], 1)
                pe.wait_ge(F["pr_ready"], 2)
                project(M_SB_V, (0, 1), 0)
                pe.wait_ge(F["sbT_ready"], 2)
                project(M_MOBA_Q, (2, 3), 0)
                pe.wait_ge(F["mla_up_ready"], 4)
                for b in range(2):
                    for j in range(2):
                        h = PAIRED[2 * b + j]
                        o = ps[:, 4 + b, j * 256:(j + 1) * 256]
                        pe.matmul(o, head(qkT_sb, 2, h)[:, 0:P], head(qkT_sb, 0, h),
                                  start=(j == 0), stop=False, skip_group_check=True)
                        mm = pe.matmul(o[:, 0:P], ident_b[:], above[:], start=False, stop=True,
                                       skip_group_check=True)
                    mm.then_inc(F["sb_z"], 1)
                for i, h in enumerate(PAIRED):
                    o = ps[:, 6, h * P:(h + 1) * P]
                    if i == 2:
                        pe.wait_ge(F["half_z"], 1)
                    pe.matmul(o, head(qkT_sb, 2, h)[:, P:SEQ], head(qkT_sb, 0, h)[:, P:SEQ],
                              start=(i == 0), stop=False, skip_group_check=True)
                    mm = pe.matmul(o, ident_b[:], above[:], start=False, stop=True,
                                   skip_group_check=True)
                    if i == 1:
                        mm.then_inc(F["half_z"], 1)
                mm.then_inc(F["sb_z"], 1)
                project(M_MOBA_K, (2, 3), 256)

                def mla_T(t):
                    for a, src in ((0, mq), (1, mk)):
                        for h in range(H):
                            mm = pe.transpose(ps[0:QK, a, h * P:(h + 1) * P], src[:, t, h, :],
                                              ident[:])
                    mm.then_inc(F["mla_T"], 1)

                pe.wait_ge(F["v_ready"], 2)
                pe.wait_ge(F["mla_qk"], 2)
                mla_T(0)
                pe.wait_ge(F["pr_ready"], 4)
                project(M_SWA_Q, (2, 3), 0)
                pe.wait_ge(F["mT_ready"], 2)
                mla_T(1)
                pe.wait_ge(F["sb_soft"], 3)
                for b in range(2):
                    for j in range(2):
                        i = 2 * b + j
                        h = PAIRED[i]
                        o = ps[:, 4 + b, j * 256:(j + 1) * 256]
                        pe.matmul(o, neg_tri[:], sb_sp[:, i * 256:(i + 1) * 256], start=False,
                                  stop=False, skip_group_check=True)
                        mm = pe.matmul(o[:, P:256], neg_ones[:],
                                       sb_sp[:, 1024 + h * P:1024 + (h + 1) * P], start=False,
                                       stop=True, skip_group_check=True)
                    mm.then_inc(F["sb_minus"], 1)
                pe.matmul(ps[:, 6, :], neg_tri[:], sb_sp[:, 1024:1536], start=False, stop=True,
                          skip_group_check=True).then_inc(F["sb_minus"], 1)
                project(M_SWA_KV, (2, 3), 256)
                pe.wait_ge(F["sb_probs"], 3)
                for t in range(TT):
                    for h in range(H):
                        o = ps[:, 7, t * 256 + h * HD:t * 256 + (h + 1) * HD]
                        c = PAIRED.index(h) * 256 + t * P
                        mm = pe.matmul(o, sb_e[:, c:c + P], v_sb[:, 0, h * HD:(h + 1) * HD],
                                       start=True, stop=(t == 0), skip_group_check=True)
                        if t == 1:
                            mm = pe.matmul(o, sb_e[:, 1024 + h * P:1024 + (h + 1) * P],
                                           v_sb[:, 1, h * HD:(h + 1) * HD], start=False,
                                           stop=True, skip_group_check=True)
                mm.then_inc(F["pv_ready"], 1)

                def group_T(n):
                    g = GROUP_ORDER[n]
                    pe.wait_ge(F["group_done"], n + 1)
                    for k in range(2):
                        for t in range(TT):
                            mm = pe.transpose(
                                ps[:, 7, k * 256 + t * P:k * 256 + (t + 1) * P],
                                hn[:, t, g * GW + k * P:g * GW + (k + 1) * P], ident[:])
                    mm.then_inc(F["groups_T"], 1)

                def project_out(n, between=None, free=None, low_ready=None):
                    k, m = WO_ROWS[n]
                    last = n == len(WO_ROWS) - 1
                    wide(U_WO + n, m, k, hT_h, hT_l, n == 0, last,
                         name="wo_done" if last else None, between=between, free=free,
                         low_ready=low_ready)

                pe.wait_ge(F["mT_ready"], 4)
                scores(0, lambda h: mT[0:QK, 0, h, :], lambda h: mT[0:QK, 1, h, :], None)
                pe.wait_ge(F["moba_qk"], 1)
                for t in range(TT):
                    for j in range(4):
                        mm = pe.transpose(ps[:, t, j * P:(j + 1) * P], rot[:, t, j * P:(j + 1) * P],
                                          ident[:])
                    mm.then_inc(F["moba_T"], 1)
                pe.wait_ge(F["pr_ready"], 6)
                pe.wait_ge(F["v_ready"], 4)
                project(M_MOBA_V, (2, 3), 0)
                group_T(0)
                probs_T(0)
                pe.wait_ge(F["mT_low"], 1)
                pv(0, lambda h, k: mkv[:, k, h, NOPE:], 7)
                pe.wait_ge(F["mobaT_ready"], 2)
                scores(1, lambda h: head(qkT_moba, 0, h), lambda h: head(qkT_moba, 2, h), None)
                pe.wait_ge(F["v_ready"], 6)
                pe.wait_ge(F["swa_qk"], 1)
                for t in range(TT):
                    for j in range(3):
                        mm = pe.transpose(ps[:, 2 + t, j * P:(j + 1) * P],
                                          pr[:, 1, t, j * P:(j + 1) * P], ident[:])
                    mm.then_inc(F["swa_T"], 1)
                project_out(0, between=(3, lambda: group_T(1)), free=(2, "swaT_ready", 2))
                probs_T(1)
                pe.wait_ge(F["mT_low"], 2)
                pv(1, lambda h, k: v_moba[:, k, h * HD:(h + 1) * HD], 7)
                scores(2, lambda h: qkT_swa[(h // 2) * HD:(h // 2) * HD + HD, h % 2, :],
                       lambda h: qkT_swa[(h // 2) * HD:(h // 2) * HD + HD, 2, :], above,
                       GROUPED)
                project_out(1)
                group_T(2)
                probs_T(2)
                pe.wait_ge(F["mT_low"], 3)
                pv(2, lambda h, k: v_swa[:, k, (h // 2) * HD:(h // 2 + 1) * HD], 7,
                   GROUPED)
                project_out(2)
                project_out(3)
                group_T(3)
                pe.wait_ge(p_landed, layer * 16 + 16)
                for k in range(2):
                    for t in range(TT):
                        mm = pe.transpose(ps[:, 4, k * 256 + t * P:k * 256 + (t + 1) * P],
                                          p_sb[:, t, k * P:(k + 1) * P], ident[:])
                mm.then_inc(F["p_T"], 1)
                pe.wait_ge(F["mT_high"], 4)
                project_out(4, low_ready=("mT_low", 4))

                pe.wait_ge(F["pT_low"], 1)
                x_T(hn, 4, ("hn_ready", 4))

                def up(s, par, u, turn=0, first=False):
                    for half in range(2):
                        slot = unit(u + half, turn)
                        if half == 0:
                            ge(pe, "conv_done", (s - 1) * 4)
                        for j in range(2):
                            for k in range(KT):
                                c = slice(k * 256 + j * P, k * 256 + (j + 1) * P)
                                if first and half == 0 and j == 0 and k % 4 == 0:
                                    pe.wait_ge(F["xT_low"], 6 + k // 2)
                                mm = split_product(
                                    ps[:, 4 + 2 * par + half, j * 256:(j + 1) * 256],
                                    wh[:, slot, c], wl[:, slot, c], hT_h[:, k, :], hT_l[:, k, :],
                                    k == 0, k == KT - 1)
                        mm.then_inc(w_used, 1)

                def down(s, par, u, first=False, last=False, turn=0):
                    pe.wait_ge(F["g_low"], s + 1)
                    if first:
                        pe.wait_ge(F["x_mid"], 4)
                    wide(u, 2, 0, gT_h[:, par], gT_l[:, par], first, last,
                         name="down_done" if last else None, turn=turn)

                up(0, 0, unit_gate(0), first=True)
                for s in range(1, LOOP_FROM):
                    up(s, s % 2, unit_gate(s))
                    down(s - 1, (s - 1) % 2, unit_gate(s) + 2, first=(s == 1))
                with pe.Fori(0, LOOPS) as turn:
                    for j in range(2):
                        s = LOOP_FROM + j
                        up(turn * 2 + s, s % 2, unit_gate(s), turn)
                        down(turn * 2 + (s - 1), (s - 1) % 2, unit_gate(s) + 2, turn=turn)
                pe.wait_ge(F["conv_done"], 4 * (STEPS - 1))
                wide(U_PROJ, 2, 0, pT_h, pT_l, True, True, banks=4, order=(2, 3, 0, 1),
                     free=(2, "conv_done", 4 * STEPS))
                down(STEPS - 1, 0, U_DOWN, last=True)
                x_T(x, 0, ("x_mlp", 0))
                for n, (k, m) in enumerate(GATE_ROWS):
                    last = n == len(GATE_ROWS) - 1
                    wide(U_GATE + n, m, k, hT_h, hT_l, n == 0, last,
                         name="gate_ready" if last else None, split=8 if n == 0 else None)
                pe.drain().then_inc(F["arrived"], 1)
                pe.wait_ge(released, layer + 2)

        @block.vector
        def _(dve):
            tt, stt, ts = dve.tensor_tensor, dve.scalar_tensor_tensor, dve.tensor_scalar

            rope_steps = [0]

            def rope_chained(ins):
                rope_steps[0] += 1
                ins.then_inc(rope_step, 1)
                dve.wait_ge(rope_step, rope_steps[0])

            dve.wait_ge(pos_landed, 16)
            rope_chained(dve.tensor_copy(pos_f[:], pos_i[:]))
            dve.wait_ge(consts_made, 6)
            angle, turns = tmp[:, 128:192], tmp[:, 192:256]
            for t in range(TT):
                rope_chained(ts(angle[:, t * 32:(t + 1) * 32], inv_freq[:], pos_f[:, t:t + 1],
                                None, ALU.mult))
            rope_chained(ts(turns, angle, float(1.0 / (2.0 * np.pi)), MAGIC, ALU.mult, ALU.add))
            rope_chained(ts(turns, turns, -MAGIC, None, ALU.add))
            for part in TWO_PI:
                rope_chained(stt(angle, turns, -part, angle, ALU.mult, ALU.add))
            pi = 3.1415925
            rope_chained(ts(tmp[:, 0:64], angle, pi, -pi, ALU.min, ALU.max))
            rope_chained(ts(tmp[:, 64:128], tmp[:, 0:64], -1.0, None, ALU.mult))
            rope_chained(tt(tmp[:, 64:128], tmp[:, 64:128], tmp[:, 0:64], ALU.min))
            rope_chained(ts(tmp[:, 64:128], tmp[:, 64:128], float(np.pi / 2), None, ALU.add))
            dve.sem_inc(rope_arg, 1)
            dve.wait_ge(released, 1)
            with dve.Fori(0, DEPTH) as layer:
                steps = [0]

                def chained(ins):
                    steps[0] += 1
                    ins.then_inc(F["dve_step"], 1)
                    dve.wait_ge(F["dve_step"], steps[0])

                def half_mean(a, n, width):
                    return ts(stat(a, n), stat(a, n), 0.5 / width, 0.5 * EPS, ALU.mult, ALU.add)

                def inverse_root(a, n):
                    y, r, half = stat(a + 2 * n, n), stat(a + n, n), stat(a, n)
                    t = stat(ST_T, n)
                    chained(ts(y.bitcast(I32), half.bitcast(I32), 1, None,
                               ALU.logical_shift_right))
                    chained(ts(y.bitcast(I32), y.bitcast(I32), -1.0, ROOT_GUESS, ALU.mult,
                               ALU.add))
                    chained(tt(r, half, y, ALU.mult))
                    chained(tt(r, r, y, ALU.mult))
                    chained(ts(t, r, 1.5, -2.5, ALU.mult, ALU.add))
                    chained(tt(r, r, t, ALU.mult))
                    chained(stt(y, r, 1.875, y, ALU.add, ALU.mult))
                    chained(tt(r, half, y, ALU.mult))
                    chained(stt(r, r, -1.0, y, ALU.mult, ALU.mult))
                    chained(stt(y, r, 1.5, y, ALU.add, ALU.mult))

                def norm(n):
                    chained(tt(stat(ST_X + 4, TT), stat(ST_X, TT), stat(ST_X + 2, TT), ALU.add))
                    chained(half_mean(ST_X + 4, TT, D))
                    inverse_root(ST_X + 4, TT)
                    for i in range(4):
                        t, c = quarter(i)
                        g = ng[:, n * D + c.start:n * D + c.stop]
                        stt(hn[:, t, c], x[:, t, c], stat(ST_X + 8 + t), g, ALU.mult, ALU.mult
                            ).then_inc(F["hn_ready"], 1)

                def x_low(n, bank):
                    for k in range(4):
                        half, t = divmod(k, 2)
                        o = (slice(None), slice(4 * half, 4 * half + 4), slice(t * P, (t + 1) * P))
                        dve.wait_ge(F["xT_high"], n + k + 1)
                        tt(hT_l[o], ps[:, bank + k, :].rearrange("p (k n) -> p k n", k=4),
                           hT_h[o].bitcast(F32), ALU.subtract).then_inc(F["xT_low"], 1)

                def rotate(i_q, i_k, kh):
                    w = HD // 2

                    def view(ap, c, n):
                        return ap[:, :, c:c + n * HD].rearrange("p t (h n) -> p t h n", h=n)

                    for i, c, n in ((i_q, 0, H), (i_k, GW, kh)):
                        src, r, o = view(pr[:, 1], c, n), view(rot, c, n), view(tmp2, c, n)
                        shape = [P, TT, n, HD]
                        last = tt(r, src, gc[:, i].unsqueeze(2).broadcast_to(shape), ALU.mult)
                        half = [P, TT, n, w]
                        for a in range(2):
                            last = tt(o[:, :, :, a * w:(a + 1) * w],
                                      src[:, :, :, (1 - a) * w:(2 - a) * w],
                                      gs[:, i, :, a * w:(a + 1) * w].unsqueeze(2)
                                      .broadcast_to(half), ALU.mult)
                    chained(last)

                def rotated(kh, name):
                    if kh == H:
                        tt(rot[:], rot[:], tmp2, ALU.add).then_inc(F[name], 1)
                        return
                    for t in range(TT):
                        order = [ap[:, t, 0:GW].rearrange("p (a b n) -> p b a n", a=2, b=2)
                                 for ap in (rot, tmp2)]
                        tt(pr[:, 1, t, 0:GW].rearrange("p (b a n) -> p b a n", a=2, b=2),
                           *order, ALU.add)
                    n = slice(GW, GW + kh * HD)
                    tt(pr[:, 1, :, n], rot[:, :, n], tmp2[:, :, n], ALU.add
                       ).then_inc(F[name], 1)

                def squares_read(ins, k):
                    ins.then_inc(F["squares_read"], 1)
                    dve.wait_ge(F["squares_read"], k)

                def heads_norm(a, kh, squares, k, rs, group=0):
                    n = TT * (H + kh)
                    chained(dve.tensor_reduce(
                        stat(a, n),
                        squares[:, :, 0:(H + kh) * HD].rearrange("p t (h n) -> p t h n", n=HD),
                        AX.X, ALU.add))
                    squares_read(half_mean(a, n, HD), k)
                    if group:
                        dve.wait_ge(F["group_sq"], TT)
                        chained(half_mean(a + n, TT, GW))
                    m = n + TT * group
                    inverse_root(a, m)
                    r = stat(a + 2 * m, n).rearrange("p (t h) -> p t h", t=TT)
                    ts(stat(rs, 8).rearrange("p (t h) -> p t h", t=TT), r[:, :, 0:H], HD ** -0.5,
                       None, ALU.mult)
                    k = pr[:, 1, :, GW:GW + kh * HD].rearrange("p t (h n) -> p t h n", h=kh)
                    chained(tt(k, k, r[:, :, H:H + kh].unsqueeze(3).broadcast_to([P, TT, kh, HD]),
                               ALU.mult))

                def row_max(g, rs, order=PAIRED, sinks=None):
                    ge(dve, "probs_ready", 8 * g)
                    for part in range(PARTS):
                        heads = part_heads(order, part)

                        def col(a):
                            return st[:, a + heads.start:a + heads.stop:heads.step or 1]

                        n = len(range(ST_ALL)[heads])
                        dve.wait_ge(F["scores_ready"], PARTS * g + part + 1)
                        chained(dve.tensor_reduce(
                            col(MX), ps[:, PART_BANKS[part], :].rearrange("p (h n) -> p h n", h=n),
                            AX.X, ALU.max))
                        if sinks is None:
                            stt(col(NB), col(MX), -1.0, col(rs), ALU.mult, ALU.mult
                                ).then_inc(F["softmax_bias"], 1)
                            continue
                        h0 = heads.start % H
                        sink = sg[:, sinks + h0:sinks + h0 + n]
                        chained(tt(col(MX), col(MX), col(rs), ALU.mult))
                        chained(tt(col(MX), col(MX), sink, ALU.max))
                        ts(col(NB), col(MX), -1.0, None, ALU.mult
                           ).then_inc(F["softmax_bias"], 1)
                        tt(col(SNK), sink, col(MX), ALU.subtract).then_inc(F["sink_arg"], 1)

                def group_low(n):
                    g = GROUP_ORDER[n]
                    dve.wait_ge(F["mT_high"], n + 1)
                    tt(hT_l[:, 2 * g:2 * g + 2, :], ps[:, 7, :].rearrange("p (k n) -> p k n", k=2),
                       hT_h[:, 2 * g:2 * g + 2, :].bitcast(F32), ALU.subtract
                       ).then_inc(F["mT_low"], 1)

                def probs_out(g, low_first=False):
                    if low_first:
                        group_low(g)
                    dve.wait_ge(F["pv_ready"], g + 1)
                    for part in range(PARTS):
                        dve.wait_ge(F["probs_T"], PARTS * g + part + 1)
                        dve.tensor_copy(pt[:, PART_COLS[part]], ps[:, PART_BANKS[part], :]
                                        ).then_inc(F["pt_ready"], 1)
                        if part == 0 and not low_first:
                            group_low(g)

                def group_cols(ap, n):
                    c = GROUP_ORDER[n] * GW
                    return ap[:, :, c:c + GW]

                def out_heads(n):
                    return group_cols(hn, n).rearrange("p t (h n) -> p t h n", h=H)

                def divided(n, bank, den, pv_n):
                    dve.wait_ge(F["pv_ready"], pv_n)
                    chained(dve.reciprocal(stat(RDEN, 8), stat(den, 8)))
                    tt(out_heads(n), ps[:, bank, :].rearrange("p (t h n) -> p t h n", t=TT, h=H),
                       stat(RDEN, 8).rearrange("p (t h) -> p t h", t=TT).unsqueeze(3)
                       .broadcast_to([P, TT, H, HD]), ALU.mult).then_inc(F["group_out"], 1)

                def group_norm(n):
                    root = ST_S + 2 * (12 + TT) + 12
                    if n:
                        root = ST_G + 6 * n + 4
                        dve.wait_ge(F["group_sq"], TT * (n + 1))
                        chained(half_mean(ST_G + 6 * n, TT, GW))
                        inverse_root(ST_G + 6 * n, TT)
                    c = GROUP_ORDER[n] * GW
                    for t in range(TT):
                        last = stt(hn[:, t, c:c + GW], hn[:, t, c:c + GW],
                                   stat(root + t),
                                   ng[:, G_GROUP + c:G_GROUP + c + GW], ALU.mult, ALU.mult)
                    last.then_inc(F["group_done"], 1)

                dve.wait_ge(gain_landed, layer * 16 + 16)
                norm(0)
                x_low(0, 4)
                dve.wait_ge(rope_sin, 2)
                dve.tensor_copy(rope_c[:, :, 32:64], rope_c[:, :, 0:32])
                chained(ts(rope_s[:, :, 0:32], rope_s[:, :, 32:64], -1.0, None, ALU.mult))
                for a in range(2):
                    dve.tensor_copy(rope_c32[:, :, a * 16:(a + 1) * 16], rope_c[:, :, 0:32:2])
                    last = dve.tensor_copy(rope_s32[:, :, a * 16:(a + 1) * 16],
                                           rope_s[:, :, a * 32:(a + 1) * 32:2])
                chained(last)
                dve.wait_ge(sg_landed, layer * 16 + 16)
                for i, c in enumerate((S_SWAQ, S_SWAK, S_MOBAQ, S_MOBAK)):
                    def gain(a, n):
                        return sg[:, a:a + n].unsqueeze(1).broadcast_to([P, TT, n])
                    tt(gc[:, i], rope_c[:], gain(c, HD), ALU.mult)
                    tt(gs[:, i, :, 0:32], rope_s[:, :, 0:32], gain(c + 32, 32), ALU.mult)
                    last = tt(gs[:, i, :, 32:64], rope_s[:, :, 32:64], gain(c, 32), ALU.mult)
                chained(last)

                dve.wait_ge(F["squared"], 2)
                for a, c, w in ((ST_L, 0, QR), (ST_L + 2, QR, KVR), (ST_PE, QR + KVR, PE_DIM)):
                    last = dve.tensor_reduce(stat(a, 2), rot[:, :, c:c + w], AX.X, ALU.add)
                chained(last)
                half_mean(ST_L, 2, QR)
                squares_read(half_mean(ST_L + 2, 2, KVR), 1)

                def rope32(o, src, scratch, shape):
                    full, half = [*shape, PE_DIM], [*shape, 16]

                    def table(a, c, w):
                        a = a[:, :, c:c + w]
                        return a if len(shape) == 2 else a.unsqueeze(2).broadcast_to([*shape, w])
                    one, two = scratch
                    tt(one, src, table(rope_c32, 0, PE_DIM), ALU.mult)
                    at = [slice(None)] * (len(shape))
                    for a in range(2):
                        last = tt(two[(*at, slice(a * 16, a * 16 + 16))],
                                  src[(*at, slice(16 - a * 16, 32 - a * 16))],
                                  table(rope_s32, a * 16, 16), ALU.mult)
                    chained(last)
                    return tt(o, one, two, ALU.add)

                inverse_root(ST_L, 4)
                for t in range(TT):
                    for j, (c, w, g) in enumerate(((0, QR, S_QN), (QR, KVR, S_KVN))):
                        v = pr[:, 0, t, c:c + w]
                        last = stt(v, v, stat(ST_L + 8 + 2 * j + t), sg[:, g:g + w], ALU.mult,
                                   ALU.mult)
                    last.then_inc(F["lat_done"], 1)
                kp = tmp[:, 512:576].rearrange("p (t n) -> p t n", t=TT)
                chained(tt(kp, pr[:, 0, :, QR + KVR:MLA_COLS],
                           sg[:, S_MLAK + NOPE:S_MLAK + QK].unsqueeze(1)
                           .broadcast_to([P, TT, PE_DIM]), ALU.mult))
                chained(rope32(kpe[:], kp, [tmp[:, 576 + 64 * a:640 + 64 * a].rearrange(
                    "p (t n) -> p t n", t=TT) for a in range(2)], [P, TT]))
                dve.wait_ge(F["conv_T"], 1)
                dve.tensor_copy(conv[:], ps[:, 7, 0:176].rearrange("p (a n) -> p a n", a=4)
                                ).then_inc(F["conv_ready"], 1)

                dve.wait_ge(F["squared"], 5)
                dve.tensor_reduce(stat(ST_M, 8),
                                  rot[:, :, 0:H * QK].rearrange("p t (h n) -> p t h n", n=QK),
                                  AX.X, ALU.add)
                chained(dve.tensor_reduce(
                    stat(ST_M + 8, 8), tmp[:, 0:512].rearrange("p (h n) -> p h n", n=NOPE),
                    AX.X, ALU.add))
                ssk = stat(ST_M + 8, 8).rearrange("p (t h) -> p t h", t=TT)
                chained(tt(ssk, ssk, stat(ST_PE, 2).unsqueeze(2).broadcast_to([P, TT, H]),
                           ALU.add))
                squares_read(half_mean(ST_M, 16, QK), 2)
                q8 = mq.rearrange("p t h n -> p (t h) n")
                chained(tt(q8, q8, sg[:, S_MLAQ:S_MLAQ + QK].unsqueeze(1)
                           .broadcast_to([P, 8, QK]), ALU.mult))
                qpe = mq[:, :, :, NOPE:QK]
                rope32(qpe, qpe, [tmp[:, 512 + 256 * a:768 + 256 * a].rearrange(
                    "p (t h n) -> p t h n", t=TT, h=H) for a in range(2)], [P, TT, H]
                    ).then_inc(F["mla_qk"], 1)
                inverse_root(ST_M, 16)
                ts(stat(RS_MLA, 8), stat(ST_M + 32, 8), QK ** -0.5, None, ALU.mult)
                rk = stat(ST_M + 40, 8).rearrange("p (t h) -> p t h", t=TT)
                chained(tt(mk[:, :, :, 0:NOPE], mkv[:, :, :, 0:NOPE],
                           rk.unsqueeze(3).broadcast_to([P, TT, H, NOPE]), ALU.mult))
                k8 = mk[:].rearrange("p t h n -> p (t h) n")[:, :, 0:NOPE]
                tt(k8, k8, sg[:, S_MLAK:S_MLAK + NOPE].unsqueeze(1).broadcast_to([P, 8, NOPE]),
                   ALU.mult)
                tt(mk[:, :, :, NOPE:QK], kpe[:].unsqueeze(2).broadcast_to([P, TT, H, PE_DIM]),
                   rk.unsqueeze(3).broadcast_to([P, TT, H, PE_DIM]), ALU.mult
                   ).then_inc(F["mla_qk"], 1)

                for b in range(3):
                    c = slice(b * 512, (b + 1) * 512)
                    dve.wait_ge(F["sb_log"], b + 1)
                    stt(sb_sp[:, c], ps[:, 4 + b, :], 0.0, sb_e[:, c], ALU.max, ALU.add
                        ).then_inc(F["sb_soft"], 1)

                dve.wait_ge(F["squared"], 6)
                heads_norm(ST_B, H, rot, 3, RS_MOBA)
                rotate(2, 3, H)
                rotated(H, "moba_qk")

                dve.wait_ge(F["pv_ready"], 1)
                dve.tensor_copy(group_cols(hn, 0),
                                ps[:, 7, :].rearrange("p (t n) -> p t n", t=TT)
                                ).then_inc(F["group_out"], 1)
                dve.wait_ge(F["squared"], 7)
                heads_norm(ST_S, 2, tmp2, 4, RS_SWA, group=1)
                dve.wait_ge(ng_landed, layer * 16 + 16)
                group_norm(0)
                row_max(0, RS_MLA)
                dve.wait_ge(F["moba_T"], 2)
                rotate(0, 1, 2)
                probs_out(0)
                rotated(2, "swa_qk")
                divided(1, 7, DENS[0], 2)
                row_max(1, RS_MOBA)
                group_norm(1)
                probs_out(1, low_first=True)
                divided(2, 7, DENS[1], 3)
                row_max(2, RS_SWA, GROUPED, S_SINK)
                group_norm(2)
                probs_out(2)
                dve.wait_ge(F["probs_ready"], 24)
                dve.wait_ge(F["sink_exp"], 1)
                chained(tt(stat(DENS[2], 8), stat(DENS[2], 8), stat(SNK, 8), ALU.add))
                divided(3, 7, DENS[2], 4)
                group_norm(3)
                group_low(3)
                dve.wait_ge(F["pT_high"], 1)
                tt(pT_l[:], ps[:, 4, :].rearrange("p (k n) -> p k n", k=2), pT_h[:].bitcast(F32),
                   ALU.subtract).then_inc(F["pT_low"], 1)

                def add_to_x(name, unit, done):
                    for b in range(4):
                        t, c = quarter(b)
                        if b < 3:
                            dve.wait_ge(F[name], b + 1)
                        else:
                            unit_done(dve, layer, unit)
                        tt(x[:, t, c], x[:, t, c], ps[:, b, :], ALU.add).then_inc(F[done], 1)

                add_to_x("wo_done", U_FFN - 1, "x_mid")
                dve.wait_ge(F["x_squared"], 4)
                norm(1)
                x_low(4, 4)

                def mlp(s, par):
                    bank = 4 + 2 * par
                    for tap, name, before in ((1, "tap1", "tap2"), (0, "conv_done", "tap1")):
                        d = 2 - tap
                        for i in range(4):
                            half, j = divmod(i, 2)
                            f = bass.ds(s * 2 + (half * FT + j), 1)
                            o = cv[par][:, i, d:SEQ]
                            dve.wait_ge(F[before], s * 4 + (2 * half + 2 if tap else i + 1))
                            stt(o, ps[:, bank + half, j * 256:j * 256 + SEQ - d],
                                conv[:, tap, f], o, ALU.mult, ALU.add).then_inc(F[name], 1)
                    dve.wait_ge(F["silu"], s + 1)
                    dve.wait_ge(F["conv_done"], s * 4 + 4)
                    g = cv[par][:, 0:2, :]
                    tt(g, g, cv[par][:, 2:4, :], ALU.mult).then_inc(F["prod"], 1)
                    dve.wait_ge(F["g_high"], s + 1)
                    tt(gT_l[:, par], g, gT_h[:, par].bitcast(F32), ALU.subtract
                       ).then_inc(F["g_low"], 1)

                for s in range(LOOP_FROM):
                    mlp(s, s % 2)
                with dve.Fori(0, LOOPS) as turn:
                    for j in range(2):
                        mlp(turn * 2 + (LOOP_FROM + j), (LOOP_FROM + j) % 2)

                add_to_x("down_done", U_DOWN, "x_mlp")
                x_low(8, 0)
                for b in range(4):
                    t, c = quarter(b)
                    dve.wait_ge(F["sigmoid"], b + 1)
                    unit_done(dve, layer, U_PROJ)
                    tt(hn[:, t, c], ps[:, 4 + b, :], hn[:, t, c], ALU.mult
                       ).then_inc(F["ple_term"], 1)
                    dve.wait_ge(F["ple_term"], b + 1)
                    tt(x[:, t, c], x[:, t, c], hn[:, t, c], ALU.add).then_inc(x_done, 1)
                dve.drain().then_inc(F["arrived"], 1)
                dve.wait_ge(released, layer + 2)


def kernel(x, p, positions, attn_norm, w_in, mla_q_norm, mla_w_uq, mla_kv_norm, mla_w_ukv,
           mla_q_gain, mla_k_gain, swa_q_gain, swa_k_gain, swa_sinks, moba_q_gain, moba_k_gain,
           group_norm, w_o, ffn_norm, w_up, conv_w, conv_b, w_down, ple_proj, ple_gate):
    import concourse.bacc as bacc
    from concourse.bass_utils import run_bass_kernel_spmd

    a = {k: np.asarray(v) for k, v in locals().items() if k not in ("bacc", "run_bass_kernel_spmd")}
    norm_gains = np.concatenate([np.roll(a["attn_norm"], -1, axis=0), a["ffn_norm"],
                                 a["group_norm"]], axis=1)
    small = np.concatenate([a[n] for n in (
        "swa_q_gain", "swa_k_gain", "moba_q_gain", "moba_k_gain", "mla_q_gain", "mla_k_gain",
        "mla_q_norm", "mla_kv_norm", "swa_sinks")], axis=1)
    taps = a["conv_w"].reshape(DEPTH, 3, 2 * FT, P).transpose(0, 2, 1, 3)
    bias = a["conv_b"].reshape(DEPTH, 2 * FT, 1, P)
    conv_rows = np.concatenate([taps, bias], axis=2)
    arrays = {"x_in": a["x"], "p_in": a["p"], "positions": a["positions"], "w_in": a["w_in"],
              "w_uq": a["mla_w_uq"], "w_ukv": a["mla_w_ukv"], "norm_gains": norm_gains,
              "small_gains": small, "w_o": a["w_o"], "w_up": a["w_up"], "conv_rows": conv_rows,
              "w_down": a["w_down"], "ple_proj": a["ple_proj"], "ple_gate": a["ple_gate"]}
    arrays = {k: np.ascontiguousarray(v) for k, v in arrays.items()}
    nc = bacc.Bacc("TRN2", target_bir_lowering=False, num_devices=1)
    args = [nc.dram_tensor(k, v.shape, mybir.dt.from_np(v.dtype), kind="ExternalInput").ap()
            for k, v in arrays.items()]
    out = nc.dram_tensor("out", (1, SEQ, D), F32, kind="ExternalOutput").ap()
    build(nc, *args, out)
    r = run_bass_kernel_spmd(nc, [arrays], core_ids=[0])
    return r.results[0]["out"]
```
